# Optimizing a Trainium2 kernel written in Bass

```python
import math
import jax, jax.numpy as jnp
from jax import lax
import numpy as np

D_MODEL = 1024
BATCH = 1
SEQ = 1024
DEPTH = 1
DEC_BATCH = 1
DEC_SEQ = 512
PAST_LEN = 128

MIX_WIDTH = D_MODEL
HY_WIDTH = MIX_WIDTH // 2
ML_WIDTH = MIX_WIDTH - HY_WIDTH
ML_HEADS = 4
ML_HEAD_DIM = ML_WIDTH // ML_HEADS
ML_CHUNK = 64
HY_ORDER = 2
HY_EMB = 33
HY_BANDS = (HY_EMB - 1) // 2
HY_FILTER_HIDDEN = 64
HY_DECAY_TARGET = 1e-2
HY_FAST_DECAY_PCT = 0.3
HY_SLOW_DECAY_PCT = 1.5
HY_MAX_DECAY = math.log(HY_DECAY_TARGET) / HY_FAST_DECAY_PCT
HY_MIN_DECAY = math.log(HY_DECAY_TARGET) / HY_SLOW_DECAY_PCT
D_FF = 2816
EPS = 1e-6

OFF_Q = 3 * HY_WIDTH
OFF_K = OFF_Q + ML_WIDTH
OFF_V = OFF_K + ML_WIDTH
OFF_O = OFF_V + ML_WIDTH
OFF_G = OFF_O + ML_WIDTH
N_GATE = 4 * ML_HEADS
P_IN = OFF_G + N_GATE
CONV_CH = OFF_V

kernel_name = "hyena_mlstm_parallel_encoder"

F32 = jnp.float32

def rmsnorm(x, g):
    xf = x.astype(F32)
    y = xf * lax.rsqrt(jnp.mean(jnp.square(xf), axis=-1, keepdims=True) + EPS)
    return (y * g.astype(F32)).astype(x.dtype)

def dwconv3(x, w, b):
    xp = jnp.pad(x, ((0, 0), (1, 1), (0, 0)))
    return xp[:, :-2] * w[0] + xp[:, 1:-1] * w[1] + xp[:, 2:] * w[2] + b

def hyena_filter_spectrum(L, w1, b1, fr1, w2, b2, fr2, w3):
    t = jnp.linspace(0.0, 1.0, L, dtype=F32)[:, None]
    freqs = jnp.linspace(1e-4, HY_BANDS - 1, HY_BANDS, dtype=F32)
    ang = (2.0 * math.pi / L) * jnp.arange(L, dtype=F32)[:, None] * freqs[None, :]
    z = jnp.concatenate([t, jnp.cos(ang), -jnp.sin(ang)], axis=-1)
    h = jnp.sin(fr1.astype(F32) * (z @ w1.astype(F32) + b1.astype(F32)))
    h = jnp.sin(fr2.astype(F32) * (h @ w2.astype(F32) + b2.astype(F32)))
    h = (h @ w3.astype(F32)).reshape(L, 2, HY_ORDER, HY_WIDTH)
    deltas = jnp.abs(jnp.linspace(HY_MIN_DECAY, HY_MAX_DECAY, HY_WIDTH, dtype=F32))
    h = h * jnp.exp(-t * deltas)[:, None, None, :]
    kern = jnp.concatenate([h[:, 0], jnp.zeros((1, HY_ORDER, HY_WIDTH), F32), h[:0:-1, 1]], axis=0)
    kern = kern * lax.rsqrt(jnp.sum(jnp.square(kern), axis=0, keepdims=True))
    return jnp.fft.rfft(kern, axis=0)

def hyena_mix(x1, x2, v, kspec, bias):
    L = v.shape[1]
    bias = bias.astype(F32)

    def long_conv(z, ks, d):
        zf = jnp.fft.rfft(z, n=2 * L, axis=1)
        return jnp.fft.irfft(zf * ks[None], n=2 * L, axis=1)[:, :L] + d * z

    z = x1.astype(F32) * long_conv(v.astype(F32), kspec[:, 0], bias[0])
    return x2.astype(F32) * long_conv(z, kspec[:, 1], bias[1])

def mlstm_chunkwise(q, k, v, ig, fg):
    B, H, S, DH = q.shape
    NC = S // ML_CHUNK
    q = q.reshape(B, H, NC, ML_CHUNK, DH)
    k = k.reshape(B, H, NC, ML_CHUNK, DH)
    v = v.reshape(B, H, NC, ML_CHUNK, DH)
    ig = ig.reshape(B, H, NC, ML_CHUNK)
    b = jnp.cumsum(jax.nn.log_sigmoid(fg).reshape(B, H, NC, ML_CHUNK), axis=-1)
    b_last = b[..., -1]
    a = b_last[..., None] - b + ig
    m_loc = jnp.max(a, axis=-1)
    w_loc = jnp.exp(a - m_loc[..., None])
    kw = k * w_loc[..., None]
    C_loc = jnp.einsum('bhcsk,bhcsv->bhckv', kw, v)
    n_loc = jnp.sum(kw, axis=3)

    def step(carry, xs):
        C, n, m = carry
        C_l, n_l, m_l, bl = xs
        m_new = jnp.maximum(bl + m, m_l)
        s_old = jnp.exp(bl + m - m_new)
        s_loc = jnp.exp(m_l - m_new)
        C_new = s_old[..., None, None] * C + s_loc[..., None, None] * C_l
        n_new = s_old[..., None] * n + s_loc[..., None] * n_l
        return (C_new, n_new, m_new), (C, n, m)

    init = (jnp.zeros((B, H, DH, DH), F32), jnp.zeros((B, H, DH), F32), jnp.zeros((B, H), F32))
    xs = (jnp.moveaxis(C_loc, 2, 0), jnp.moveaxis(n_loc, 2, 0),
          jnp.moveaxis(m_loc, 2, 0), jnp.moveaxis(b_last, 2, 0))
    _, (C_prev, n_prev, m_prev) = lax.scan(step, init, xs)
    m_prev = jnp.transpose(m_prev, (1, 2, 0))

    g = b + m_prev[..., None]
    D = b[..., :, None] - b[..., None, :] + ig[..., None, :]
    mask = jnp.tril(jnp.ones((ML_CHUNK, ML_CHUNK), dtype=bool))
    D = jnp.where(mask, D, -jnp.inf)
    m_t = jnp.maximum(g, jnp.max(D, axis=-1))
    Sm = jnp.einsum('bhctd,bhcsd->bhcts', q, k) * jnp.exp(D - m_t[..., None])
    inter = jnp.exp(g - m_t)
    num = inter[..., None] * jnp.einsum('bhctk,cbhkv->bhctv', q, C_prev) \
        + jnp.einsum('bhcts,bhcsv->bhctv', Sm, v)
    den = inter * jnp.einsum('bhctk,cbhk->bhct', q, n_prev) + jnp.sum(Sm, axis=-1)
    h = num / jnp.maximum(jnp.abs(den), jnp.exp(-m_t))[..., None]
    return h.reshape(B, H, S, DH)

def mlstm_bidir(q, k, v, gates):
    B, S = q.shape[0], q.shape[1]
    g = gates.reshape(B, S, 4, ML_HEADS).transpose(2, 0, 3, 1)
    q, k, v = (a.transpose(0, 2, 1, 3) for a in (q, k, v))
    flip = lambda a: jnp.flip(a, axis=2)
    h_f = mlstm_chunkwise(q, k, v, g[0], g[1])
    h_b = flip(mlstm_chunkwise(flip(q), flip(k), flip(v), flip(g[2]), flip(g[3])))
    return (h_f + h_b).transpose(0, 2, 1, 3)

def encoder_layer(x, norm1_g, w_in, conv_w, conv_b, gate_b, filt_w1, filt_b1, filt_freq1,
                  filt_w2, filt_b2, filt_freq2, filt_w3, hy_bias, ml_norm_g, w_out,
                  norm2_g, w_up, ffn_conv_w, ffn_conv_b, w_down):
    B, S, _ = x.shape
    h = rmsnorm(x, norm1_g)
    proj = h @ w_in
    cp = dwconv3(proj[..., :CONV_CH], conv_w, conv_b)
    x1 = cp[..., :HY_WIDTH]
    x2 = cp[..., HY_WIDTH:2 * HY_WIDTH]
    hv = cp[..., 2 * HY_WIDTH:OFF_Q]
    kspec = hyena_filter_spectrum(S, filt_w1, filt_b1, filt_freq1, filt_w2, filt_b2, filt_freq2, filt_w3)
    y_hy = hyena_mix(x1, x2, hv, kspec, hy_bias).astype(x.dtype)
    q = jax.nn.silu(cp[..., OFF_Q:OFF_K].astype(F32)).reshape(B, S, ML_HEADS, ML_HEAD_DIM)
    k = (jax.nn.silu(cp[..., OFF_K:OFF_V].astype(F32)) * (ML_HEAD_DIM ** -0.5)).reshape(B, S, ML_HEADS, ML_HEAD_DIM)
    v = proj[..., OFF_V:OFF_O].astype(F32).reshape(B, S, ML_HEADS, ML_HEAD_DIM)
    o = jax.nn.sigmoid(proj[..., OFF_O:OFF_G].astype(F32))
    gates = proj[..., OFF_G:].astype(F32) + gate_b.astype(F32)
    hm = mlstm_bidir(q, k, v, gates)
    hm = hm * lax.rsqrt(jnp.mean(jnp.square(hm), axis=-1, keepdims=True) + EPS)
    hm = hm.reshape(B, S, ML_WIDTH) * ml_norm_g.astype(F32)
    y_ml = (o * hm).astype(x.dtype)
    x = x + jnp.concatenate([y_hy, y_ml], axis=-1) @ w_out
    h = rmsnorm(x, norm2_g)
    u = dwconv3(h @ w_up, ffn_conv_w, ffn_conv_b)
    val, gate = u[..., :D_FF], u[..., D_FF:]
    return x + (jax.nn.silu(gate) * val) @ w_down

def trunk(x, layer_params, final_g):
    for l in range(DEPTH):
        x = encoder_layer(x, *[p[l] for p in layer_params])
    return rmsnorm(x, final_g)

def setup_inputs(seed: int = 0) -> dict:
    key = jax.random.key(seed)
    ks = jax.random.split(key, 28)
    nrm = lambda k, shape, scale: jax.random.normal(k, shape, F32) * scale
    is_f = jnp.array([0.0, 1.0, 0.0, 1.0], F32)[None, :, None]
    gate_b = jnp.where(is_f > 0,
                       3.0 + 3.0 * jax.random.uniform(ks[5], (DEPTH, 4, ML_HEADS), F32),
                       0.1 * jax.random.normal(ks[6], (DEPTH, 4, ML_HEADS), F32)).reshape(DEPTH, N_GATE)
    return {
        "x_prompt": nrm(ks[0], (BATCH, SEQ, D_MODEL), 1.0),
        "x_sample": nrm(ks[1], (DEC_BATCH, DEC_SEQ, D_MODEL), 1.0),
        "norm1_g": 1.0 + nrm(ks[2], (DEPTH, D_MODEL), 0.02),
        "w_in": nrm(ks[3], (DEPTH, D_MODEL, P_IN), D_MODEL ** -0.5),
        "conv_w": nrm(ks[4], (DEPTH, 3, CONV_CH), 3 ** -0.5),
        "conv_b": nrm(ks[7], (DEPTH, CONV_CH), 0.02),
        "gate_b": gate_b,
        "filt_w1": nrm(ks[8], (DEPTH, HY_EMB, HY_FILTER_HIDDEN), HY_EMB ** -0.5),
        "filt_b1": nrm(ks[9], (DEPTH, HY_FILTER_HIDDEN), 0.1),
        "filt_freq1": 1.0 + nrm(ks[10], (DEPTH, HY_FILTER_HIDDEN), 0.1),
        "filt_w2": nrm(ks[11], (DEPTH, HY_FILTER_HIDDEN, HY_FILTER_HIDDEN), HY_FILTER_HIDDEN ** -0.5),
        "filt_b2": nrm(ks[12], (DEPTH, HY_FILTER_HIDDEN), 0.1),
        "filt_freq2": 1.0 + nrm(ks[13], (DEPTH, HY_FILTER_HIDDEN), 0.1),
        "filt_w3": nrm(ks[14], (DEPTH, HY_FILTER_HIDDEN, 2 * HY_ORDER * HY_WIDTH), HY_FILTER_HIDDEN ** -0.5),
        "hy_bias": nrm(ks[15], (DEPTH, HY_ORDER, HY_WIDTH), 0.1),
        "ml_norm_g": 1.0 + nrm(ks[16], (DEPTH, ML_WIDTH), 0.02),
        "w_out": nrm(ks[17], (DEPTH, MIX_WIDTH, D_MODEL), MIX_WIDTH ** -0.5),
        "norm2_g": 1.0 + nrm(ks[18], (DEPTH, D_MODEL), 0.02),
        "w_up": nrm(ks[19], (DEPTH, D_MODEL, 2 * D_FF), D_MODEL ** -0.5),
        "ffn_conv_w": nrm(ks[20], (DEPTH, 3, 2 * D_FF), 3 ** -0.5),
        "ffn_conv_b": nrm(ks[21], (DEPTH, 2 * D_FF), 0.02),
        "w_down": nrm(ks[22], (DEPTH, D_FF, D_MODEL), D_FF ** -0.5),
        "final_g": 1.0 + nrm(ks[23], (D_MODEL,), 0.02),
    }

def reference(x_prompt, x_sample, norm1_g, w_in, conv_w, conv_b, gate_b, filt_w1, filt_b1,
              filt_freq1, filt_w2, filt_b2, filt_freq2, filt_w3, hy_bias, ml_norm_g, w_out,
              norm2_g, w_up, ffn_conv_w, ffn_conv_b, w_down, final_g):
    layer_params = (norm1_g, w_in, conv_w, conv_b, gate_b, filt_w1, filt_b1, filt_freq1,
                    filt_w2, filt_b2, filt_freq2, filt_w3, hy_bias, ml_norm_g, w_out,
                    norm2_g, w_up, ffn_conv_w, ffn_conv_b, w_down)
    y_prompt = trunk(x_prompt, layer_params, final_g)
    y_sample = trunk(x_sample, layer_params, final_g)
    return (y_prompt, y_sample)


_drawn_inputs = setup_inputs


def setup_inputs(seed=0):
    import zlib

    import numpy as np

    out = dict(_drawn_inputs(seed))
    spreads = {}
    factors = {'ml_norm_g': 8.0, 'norm2_g': 4.641, 'ffn_conv_b': 4.463, 'final_g': 2.894}
    for name, (base, spread) in spreads.items():
        noise = np.random.default_rng([zlib.crc32(name.encode()), seed]).standard_normal(out[name].shape)
        drawn = base * np.exp(spread * noise) if base else spread * noise
        out[name] = __import__('jax').numpy.asarray(drawn.astype(out[name].dtype))
    for name, factor in factors.items():
        out[name] = (out[name] * factor).astype(out[name].dtype)
    return out
```

```python
import math
from contextlib import ExitStack

import numpy as np

import concourse.bass as bass
from concourse import mybir
from concourse.alu_op_type import AluOpType as ALU

F32, F32R = mybir.dt.float32, mybir.dt.float32r
ACT = mybir.ActivationFunctionType

P = 128
D = 1024
KD = D // P
SEQS = [(0, 1024), (1024, 512)]
T = sum(n for _, n in SEQS)
TT = T // P
CH = 512
NCH = T // CH
HY = 512
HEADS, HD = 4, 128
ORDER = 2
EMB, HID = 33, 64
FF = 2816
KF = FF // P
EPS = 1e-6
CLASSES = 4

N_QK, N_MIX, N_V, N_O = 2 * HEADS, 3 * HY // P, HEADS, HEADS
IN_KINDS = ["qk"] * N_QK + ["mix"] * N_MIX + ["v"] * N_V + ["o"] * N_O + ["gate"]
FIRST_MIX = N_QK
FIRST_V = FIRST_MIX + N_MIX
FIRST_O = FIRST_V + N_V
N_CONV = N_QK + N_MIX
GATE_ROWS = [0, 64, 32, 96]


def pipelined(eng, kinds, stages):
    count, deepest = len(kinds), max(lag for lag, _ in stages)

    def kind_of(k):
        return kinds[k] if 0 <= k < count else None

    def signature(n):
        return [(kind_of(n - lag), kind_of(n - lag - 2)) for lag, _ in stages]

    def step(n0, n, i):
        for lag, body in stages:
            kind = kind_of(n - lag)
            if kind is not None:
                k0 = n - lag
                body(i * 2 + k0 if i is not None else k0, k0 % 2,
                     i + k0 // 2 if i is not None else k0 // 2, kind, kind_of(k0 - 2))

    n = 0
    while n < count + deepest:
        run = 1
        while n + run < count + deepest and signature(n + run) == signature(n):
            run += 1
        if run >= 4:
            with eng.Fori(0, run // 2) as i:
                step(n, n, i)
                step(n, n + 1, i)
            n += run // 2 * 2
        else:
            step(n, n, None)
            n += 1


class Phase:

    lasting = None

    def __init__(self, nc, ctx, name):
        self.nc, self.ctx, self.name, self.sems = nc, ctx, name, []
        ctx.callback(self.clear)

    def sb(self, name, shape, dt=F32):
        return self.ctx.enter_context(self.nc.sbuf_tensor(f"{self.name}_{name}", shape, dt))

    def ps(self, name, shape, dt=F32):
        return self.ctx.enter_context(self.nc.psum_tensor(f"{self.name}_{name}", shape, dt))

    def sem(self, name):
        self.sems.append(self.ctx.enter_context(self.nc.semaphore(f"{self.name}_{name}")))
        return self.sems[-1]

    def pool_dma_sem(self, name):
        return Phase.lasting.enter_context(self.nc.semaphore(f"{self.name}_{name}"))

    def clear(self):
        if self.sems:
            nums = sorted(s.num for s in self.sems)
            starts = [n for n in nums if n - 1 not in nums]
            ends = [n + 1 for n in nums if n + 1 not in nums]
            with self.nc.Block() as block:
                @block.sync
                def _(sp):
                    for start, end in zip(starts, ends):
                        sp.sem_clear(range(start, end))


def three_pass(pe, out, w_hi, w_lo, x_hi, x_lo, first, last):
    pe.matmul(out, w_hi, x_hi, start=first, stop=False)
    pe.matmul(out, w_hi, x_lo, start=False, stop=False)
    return pe.matmul(out, w_lo, x_hi, start=False, stop=last)


def norm_transpose(nc, name, g, ident, ht_hi, ht_lo, x_dram=None, x_sb=None):
    with ExitStack() as ctx:
        p = Phase(nc, ctx, name)
        x_in = [p.sb(f"x_in{b}", [P, D]) for b in range(2)] if x_sb is None else None
        gain = p.sb("gain", [P, D])
        junk = p.sb("junk", [P, D])
        sumsq, root, rstd = (p.sb(n, [P, TT]) for n in ("sumsq", "root", "rstd"))
        eps, eps_set = p.sb("eps", [P, 1]), p.sem("eps_set")
        xn = [p.sb(f"xn{b}", [P, D]) for b in range(2)]
        bank = [p.ps(f"bank{n}", [P, 4, P]) for n in range(4)]
        x_loaded = [p.sem(f"x_loaded{b}") for b in range(2)]
        gain_loaded = p.sem("gain_loaded")
        squared, root_ready, rstd_ready = p.sem("squared"), p.sem("root_ready"), p.sem("rstd_ready")
        xn_ready, transposed = p.sem("xn_ready"), p.sem("transposed")
        hi_ready, lo_ready = p.sem("hi_ready"), p.sem("lo_ready")
        kinds = ["tile"] * TT

        def x_of(k, b):
            return x_in[b][:, :] if x_sb is None else x_sb[:, bass.ds(k, 1), :].rearrange("p a d -> p (a d)")

        with nc.Block() as block:
            @block.sync
            def _(sp):
                sp.dma_start(gain[:, :], g.rearrange("(a d) -> a d", a=1).broadcast_to([P, D])).then_inc(gain_loaded, 16)

                def load(k, b, turn, kind, before):
                    if before:
                        sp.wait_ge(xn_ready, k - 1)
                    sp.dma_start(x_in[b][:, :], x_dram[bass.ds(k, 1), :, :].rearrange("a p d -> (a p) d")
                                 ).then_inc(x_loaded[b], 16)
                if x_sb is None:
                    pipelined(sp, kinds, [(0, load)])

            @block.scalar
            def _(act):
                act.wait_ge(eps_set, 1)

                def square(k, b, turn, kind, before):
                    if x_sb is None:
                        act.wait_ge(x_loaded[b], (turn + 1) * 16)
                    act.activation(junk[:, :], x_of(k, b), ACT.Square,
                                   accum_out=sumsq[:, bass.ds(k, 1)]).then_inc(squared, 1)
                    act.wait_ge(squared, k + 1)
                    act.activation(root[:, bass.ds(k, 1)], sumsq[:, bass.ds(k, 1)], ACT.Sqrt, bias=eps[:, :],
                                   scale=1.0 / D).then_inc(root_ready, 1)

                def high(k, b, turn, kind, before):
                    for h in range(2):
                        act.wait_ge(transposed, k * 2 + h + 1)
                        act.activation(ht_hi[:, 4 * h:4 * h + 4, bass.ds(k * P, P)], bank[2 * b + h][:, :, :],
                                       ACT.Copy).then_inc(hi_ready, 1)
                pipelined(act, kinds, [(0, square), (1, high)])

            @block.vector
            def _(dve):
                dve.memset(eps[:, :], EPS).then_inc(eps_set, 1)
                dve.wait_ge(gain_loaded, 16)

                def scale(k, b, turn, kind, before):
                    dve.wait_ge(root_ready, k + 1)
                    dve.reciprocal(rstd[:, bass.ds(k, 1)], root[:, bass.ds(k, 1)]).then_inc(rstd_ready, 1)
                    if before:
                        dve.wait_ge(transposed, k * 2 - 2)
                    dve.wait_ge(rstd_ready, k + 1)
                    dve.scalar_tensor_tensor(xn[b][:, :], x_of(k, b), rstd[:, bass.ds(k, 1)], gain[:, :],
                                             ALU.mult, ALU.mult).then_inc(xn_ready, 1)

                def low(k, b, turn, kind, before):
                    for h in range(2):
                        dve.wait_ge(hi_ready, k * 2 + h + 1)
                        dve.tensor_tensor(ht_lo[:, 4 * h:4 * h + 4, bass.ds(k * P, P)], bank[2 * b + h][:, :, :],
                                          ht_hi[:, 4 * h:4 * h + 4, bass.ds(k * P, P)].bitcast(F32),
                                          ALU.subtract).then_inc(lo_ready, 1)
                pipelined(dve, kinds, [(0, scale), (1, low)])

            @block.tensor
            def _(pe):
                def turn_tiles(k, b, turn, kind, before):
                    pe.wait_ge(xn_ready, k + 1)
                    for h in range(2):
                        if before:
                            pe.wait_ge(lo_ready, k * 2 + h - 3)
                        for q in range(4):
                            c = 4 * h + q
                            last = pe.transpose(bank[2 * b + h][:, q, :], xn[b][:, c * P:(c + 1) * P], ident[:, :])
                        last.then_inc(transposed, 1)
                pipelined(pe, kinds, [(0, turn_tiles)])



def split_weights(p, w_tiles, kinds, width=D):
    raw = [p.sb(f"w_raw{b}", [P, KD, P]) for b in range(2)]
    hi = [p.sb(f"w_hi{b}", [P, KD, P], F32R) for b in range(2)]
    lo = [p.sb(f"w_lo{b}", [P, KD, P], F32R) for b in range(2)]
    return raw, hi, lo


def channel_major_product(pe, out, w_hi, w_lo, ht_hi, ht_lo):
    for kt in range(KD):
        for c in range(NCH):
            last = three_pass(pe, out[:, c * CH:(c + 1) * CH], w_hi[:, kt, :], w_lo[:, kt, :],
                              ht_hi[:, kt, c * CH:(c + 1) * CH], ht_lo[:, kt, c * CH:(c + 1) * CH],
                              kt == 0, kt == KD - 1)
    return last


def add_neighbours(dve, u, acc, w_prev, w_next, half_step, done, k):
    for t0, n in SEQS:
        dve.scalar_tensor_tensor(u[:, t0 + 1:t0 + n], acc[:, t0:t0 + n - 1], w_prev, u[:, t0 + 1:t0 + n],
                                 ALU.mult, ALU.add).then_inc(half_step, 1)
    for s, (t0, n) in enumerate(SEQS):
        dve.wait_ge(half_step, k * 2 + s + 1)
        last = dve.scalar_tensor_tensor(u[:, t0:t0 + n - 1], acc[:, t0 + 1:t0 + n], w_next, u[:, t0:t0 + n - 1],
                                        ALU.mult, ALU.add)
    last.then_inc(done, 1)


def input_projection(nc, w_tiles, conv_par, gate_bias, ident, ht_hi, ht_lo, qk_d, tok_d, o_d, gates_d):
    with ExitStack() as ctx:
        p = Phase(nc, ctx, "in")
        raw, w_hi, w_lo = split_weights(p, w_tiles, IN_KINDS)
        cp = p.sb("conv_par", [P, N_CONV, 4])
        gb = p.sb("gate_bias", [P, 1])
        u = [p.sb(f"u{b}", [P, T]) for b in range(2)]
        out = [p.sb(f"out{b}", [P, TT, P]) for b in range(2)]
        acc = [p.ps(f"acc{b}", [P, T]) for b in range(2)]
        tbank = [p.ps(f"tbank{b}", [P, 4, P]) for b in range(2)]
        par_loaded = p.sem("par_loaded")
        raw_loaded = [p.sem(f"raw_loaded{b}") for b in range(2)]
        stored = [p.pool_dma_sem(f"stored{b}") for b in range(2)]
        hi_ready, lo_ready, multiplied = p.sem("hi_ready"), p.sem("lo_ready"), p.sem("multiplied")
        centred, half_step, u_ready = p.sem("centred"), p.sem("half_step"), p.sem("u_ready")
        transposed, t_copied, activated = p.sem("transposed"), p.sem("t_copied"), p.sem("activated")

        def u_free(eng, k, before):
            if before in ("mix", "v"):
                eng.wait_ge(transposed, (k - 2 - FIRST_MIX) * 3 + 3)
            elif before == "qk":
                eng.wait_ge(activated, k - 1)
            elif before:
                eng.wait_ge(activated, k - 1 - (FIRST_O - N_QK))

        with nc.Block() as block:
            @block.sync
            def _(sp):
                sp.dma_start(cp[:, :, :], conv_par).then_inc(par_loaded, 16)
                sp.dma_start(gb[:, :], gate_bias).then_inc(par_loaded, 16)

                def load(k, b, turn, kind, before):
                    if before:
                        sp.wait_ge(lo_ready, k - 1)
                    sp.dma_start(raw[b][:, :, :], w_tiles[bass.ds(k, 1), :, :, :].rearrange("a p k c -> (a p) k c")
                                 ).then_inc(raw_loaded[b], 16)
                pipelined(sp, ["w"] * len(IN_KINDS), [(0, load)])

            @block.scalar
            def _(act):
                act.wait_ge(par_loaded, 32)

                def high(k, b, turn, kind, before):
                    act.wait_ge(raw_loaded[b], (turn + 1) * 16)
                    if before:
                        act.wait_ge(multiplied, k - 1)
                    act.activation(w_hi[b][:, :, :], raw[b][:, :, :], ACT.Copy).then_inc(hi_ready, 1)

                def finish(k, b, turn, kind, before):
                    if before:
                        act.wait_ge(stored[b], turn * 16)
                    if kind in ("mix", "v"):
                        for g in range(3):
                            act.wait_ge(transposed, (k - FIRST_MIX) * 3 + g + 1)
                            act.activation(out[b][:, 4 * g:4 * g + 4, :], tbank[(b + g) % 2][:, :, :],
                                           ACT.Copy).then_inc(t_copied, 1)
                    else:
                        act.wait_ge(u_ready, k + 1)
                        func = {"qk": ACT.Silu, "o": ACT.Sigmoid, "gate": ACT.Copy}[kind]
                        act.activation(out[b][:, :, :].rearrange("p a b -> p (a b)"), u[b][:, :],
                                       func).then_inc(activated, 1)

                def centre(k, b, turn, kind, before):
                    if kind in ("qk", "mix"):
                        act.wait_ge(multiplied, k + 1)
                        u_free(act, k, before)
                        act.activation(u[b][:, :], acc[b][:, :], ACT.Identity,
                                       bias=cp[:, bass.ds(k, 1), 3:4].rearrange("p a b -> p (a b)"),
                                       scale=cp[:, bass.ds(k, 1), 1:2].rearrange("p a b -> p (a b)")
                                       ).then_inc(centred, 1)
                pipelined(act, IN_KINDS, [(0, high), (2, finish), (1, centre)])

            @block.vector
            def _(dve):
                dve.wait_ge(par_loaded, 32)

                def low(k, b, turn, kind, before):
                    dve.wait_ge(hi_ready, k + 1)
                    dve.tensor_tensor(w_lo[b][:, :, :], raw[b][:, :, :], w_hi[b][:, :, :].bitcast(F32),
                                      ALU.subtract).then_inc(lo_ready, 1)

                def gather(k, b, turn, kind, before):
                    if kind in ("qk", "mix"):
                        dve.wait_ge(centred, k + 1)
                        add_neighbours(dve, u[b], acc[b],
                                       cp[:, bass.ds(k, 1), 0:1].rearrange("p a b -> p (a b)"),
                                       cp[:, bass.ds(k, 1), 2:3].rearrange("p a b -> p (a b)"),
                                       half_step, u_ready, k)
                    else:
                        dve.wait_ge(multiplied, k + 1)
                        u_free(dve, k, before)
                        if kind == "gate":
                            dve.tensor_scalar(u[b][:, :], acc[b][:, :], gb[:, :], None, ALU.add).then_inc(u_ready, 1)
                        else:
                            dve.tensor_copy(u[b][:, :], acc[b][:, :]).then_inc(u_ready, 1)
                pipelined(dve, IN_KINDS, [(0, low), (1, gather)])

            @block.tensor
            def _(pe):
                def product(k, b, turn, kind, before):
                    pe.wait_ge(lo_ready, k + 1)
                    if before:
                        pe.wait_ge(u_ready, k - 1)
                    channel_major_product(pe, acc[b], w_hi[b], w_lo[b], ht_hi, ht_lo).then_inc(multiplied, 1)

                def turn_tiles(k, b, turn, kind, before):
                    if kind not in ("mix", "v"):
                        return
                    pe.wait_ge(u_ready, k + 1)
                    for g in range(3):
                        n = (k - FIRST_MIX) * 3 + g
                        if not isinstance(n, int) or n >= 2:
                            pe.wait_ge(t_copied, n - 1)
                        for q in range(4):
                            t = 4 * g + q
                            last = pe.transpose(tbank[(b + g) % 2][:, q, :], u[b][:, t * P:(t + 1) * P], ident[:, :])
                        last.then_inc(transposed, 1)
                pipelined(pe, IN_KINDS, [(0, product), (1, turn_tiles)])

            @block.gpsimd
            def _(pool):
                def store(k, b, turn, kind, before):
                    if kind in ("mix", "v"):
                        pool.wait_ge(t_copied, (k - FIRST_MIX) * 3 + 3)
                        pool.dma_start(tok_d[:, :, bass.ds((k - FIRST_MIX) * P, P)].rearrange("t p c -> p t c"),
                                       out[b][:, :, :]).then_inc(stored[b], 16)
                        return
                    first, dst = {"qk": (0, qk_d), "o": (FIRST_O, o_d), "gate": (FIRST_O + N_O, gates_d)}[kind]
                    pool.wait_ge(activated, k + 1 - (0 if kind == "qk" else FIRST_O - N_QK))
                    pool.dma_start(dst[bass.ds(k - first, 1), :, :].rearrange("a p t -> (a p) t"),
                                   out[b][:, :, :].rearrange("p a b -> p (a b)")).then_inc(stored[b], 16)
                pipelined(pool, IN_KINDS, [(0, store)])
                n = len(IN_KINDS)
                pool.wait_ge(stored[0], 16 * ((n + 1) // 2))
                pool.wait_ge(stored[1], 16 * (n // 2))


def gated_up_projection(nc, w_tiles, conv_par, ht_hi, ht_lo, g_d):
    kinds = ["ff"] * (2 * KF)
    with ExitStack() as ctx:
        p = Phase(nc, ctx, "up")
        raw, w_hi, w_lo = split_weights(p, w_tiles, kinds)
        cp = p.sb("conv_par", [P, 2 * KF, 4])
        u = [p.sb(f"u{b}", [P, T]) for b in range(2)]
        sg = p.sb("silu_gate", [P, T])
        prod = p.sb("prod", [P, T])
        acc = [p.ps(f"acc{b}", [P, T]) for b in range(2)]
        par_loaded, stored = p.sem("par_loaded"), p.pool_dma_sem("stored")
        raw_loaded = [p.sem(f"raw_loaded{b}") for b in range(2)]
        hi_ready, lo_ready, multiplied = p.sem("hi_ready"), p.sem("lo_ready"), p.sem("multiplied")
        centred, half_step, u_ready = p.sem("centred"), p.sem("half_step"), p.sem("u_ready")
        gate_ready, gated = p.sem("gate_ready"), p.sem("gated")

        with nc.Block() as block:
            @block.sync
            def _(sp):
                sp.dma_start(cp[:, :, :], conv_par).then_inc(par_loaded, 16)

                def load(k, b, turn, kind, before):
                    if before:
                        sp.wait_ge(lo_ready, k - 1)
                    sp.dma_start(raw[b][:, :, :], w_tiles[bass.ds(k, 1), :, :, :].rearrange("a p k c -> (a p) k c")
                                 ).then_inc(raw_loaded[b], 16)
                pipelined(sp, kinds, [(0, load)])

            @block.scalar
            def _(act):
                act.wait_ge(par_loaded, 16)

                def high(k, b, turn, kind, before):
                    act.wait_ge(raw_loaded[b], (turn + 1) * 16)
                    if before:
                        act.wait_ge(multiplied, k - 1)
                    act.activation(w_hi[b][:, :, :], raw[b][:, :, :], ACT.Copy).then_inc(hi_ready, 1)

                def silu(k, b, turn, kind, before):
                    if b == 1:
                        act.wait_ge(u_ready, k + 1)
                        if before:
                            act.wait_ge(gated, turn)
                        act.activation(sg[:, :], u[1][:, :], ACT.Silu).then_inc(gate_ready, 1)

                def centre(k, b, turn, kind, before):
                    act.wait_ge(multiplied, k + 1)
                    if before:
                        act.wait_ge(gated, turn)
                    act.activation(u[b][:, :], acc[b][:, :], ACT.Identity,
                                   bias=cp[:, bass.ds(k, 1), 3:4].rearrange("p a b -> p (a b)"),
                                   scale=cp[:, bass.ds(k, 1), 1:2].rearrange("p a b -> p (a b)")
                                   ).then_inc(centred, 1)
                pipelined(act, kinds, [(0, high), (2, silu), (1, centre)])

            @block.vector
            def _(dve):
                dve.wait_ge(par_loaded, 16)

                def low(k, b, turn, kind, before):
                    dve.wait_ge(hi_ready, k + 1)
                    dve.tensor_tensor(w_lo[b][:, :, :], raw[b][:, :, :], w_hi[b][:, :, :].bitcast(F32),
                                      ALU.subtract).then_inc(lo_ready, 1)

                def gate(k, b, turn, kind, before):
                    if b == 1:
                        dve.wait_ge(gate_ready, turn + 1)
                        if before:
                            dve.wait_ge(stored, turn * 16)
                        dve.tensor_tensor(prod[:, :], sg[:, :], u[0][:, :], ALU.mult).then_inc(gated, 1)

                def gather(k, b, turn, kind, before):
                    dve.wait_ge(centred, k + 1)
                    add_neighbours(dve, u[b], acc[b],
                                   cp[:, bass.ds(k, 1), 0:1].rearrange("p a b -> p (a b)"),
                                   cp[:, bass.ds(k, 1), 2:3].rearrange("p a b -> p (a b)"),
                                   half_step, u_ready, k)
                pipelined(dve, kinds, [(0, low), (2, gate), (1, gather)])

            @block.tensor
            def _(pe):
                def product(k, b, turn, kind, before):
                    pe.wait_ge(lo_ready, k + 1)
                    if before:
                        pe.wait_ge(u_ready, k - 1)
                    channel_major_product(pe, acc[b], w_hi[b], w_lo[b], ht_hi, ht_lo).then_inc(multiplied, 1)
                pipelined(pe, kinds, [(0, product)])

            @block.gpsimd
            def _(pool):
                with pool.Fori(0, KF) as i:
                    pool.wait_ge(gated, i + 1)
                    pool.dma_start(g_d[bass.ds(i, 1), :, :].rearrange("a p t -> (a p) t"), prod[:, :]).then_inc(stored, 16)
                pool.wait_ge(stored, 16 * KF)


def token_major_projection(nc, name, kt_count, w_halves, src_d, x_sb, x_dram=None):
    half = D // 2
    with ExitStack() as ctx:
        p = Phase(nc, ctx, name)
        w_raw = [p.sb(f"w_raw{b}", [P, half]) for b in range(2)]
        w_hi, w_lo = (p.sb(n, [P, kt_count, half], F32R) for n in ("w_hi", "w_lo"))
        s_raw = p.sb("s_raw", [P, kt_count, P])
        s_hi, s_lo = ([p.sb(f"{n}{b}", [P, kt_count, P], F32R) for b in range(2)] for n in ("s_hi", "s_lo"))
        acc = [p.ps(f"acc{b}", [P, half]) for b in range(2)]
        x_loaded, s_loaded = p.sem("x_loaded"), p.sem("s_loaded")
        w_loaded = [p.sem(f"w_loaded{b}") for b in range(2)]
        w_hi_ready, w_lo_ready = p.sem("w_hi_ready"), p.sem("w_lo_ready")
        s_hi_ready, s_lo_ready = p.sem("s_hi_ready"), p.sem("s_lo_ready")
        multiplied, added = p.sem("multiplied"), p.sem("added")
        w_kinds, t_kinds = ["w"] * kt_count, ["t"] * TT

        with nc.Block() as block:
            @block.sync
            def _(sp):
                if x_dram is not None:
                    sp.dma_start(x_sb[:, :, :], x_dram.rearrange("t p d -> p t d")).then_inc(x_loaded, 16)
                for h in range(2):
                    def load_w(k, b, turn, kind, before):
                        if h or before:
                            sp.wait_ge(w_lo_ready, k - 1 + h * kt_count)
                        sp.dma_start(w_raw[b][:, :], w_halves[h, bass.ds(k, 1), :, :].rearrange("a p c -> (a p) c")
                                     ).then_inc(w_loaded[b], 16)

                    def load_s(k, b, turn, kind, before):
                        if not isinstance(k, int) or h * TT + k > 0:
                            sp.wait_ge(s_lo_ready, k + h * TT)
                        sp.dma_start(s_raw[:, :, :], src_d[:, :, bass.ds(k * P, P)].rearrange("k p t -> p k t")
                                     ).then_inc(s_loaded, 16)
                    pipelined(sp, w_kinds, [(0, load_w)])
                    pipelined(sp, t_kinds, [(0, load_s)])

            @block.scalar
            def _(act):
                for h in range(2):
                    def high_w(k, b, turn, kind, before):
                        act.wait_ge(w_loaded[b], (turn + 1) * 16 + h * (kt_count // 2) * 16)
                        act.activation(w_hi[:, bass.ds(k, 1), :].rearrange("p a c -> p (a c)"), w_raw[b][:, :],
                                       ACT.Copy).then_inc(w_hi_ready, 1)

                    def high_s(k, b, turn, kind, before):
                        act.wait_ge(s_loaded, (k + 1 + h * TT) * 16)
                        if h or before:
                            act.wait_ge(multiplied, k - 1 + h * TT)
                        act.activation(s_hi[b][:, :, :], s_raw[:, :, :], ACT.Copy).then_inc(s_hi_ready, 1)
                    if h:
                        act.wait_ge(multiplied, TT)
                    pipelined(act, w_kinds, [(0, high_w)])
                    pipelined(act, t_kinds, [(0, high_s)])

            @block.vector
            def _(dve):
                if x_dram is not None:
                    dve.wait_ge(x_loaded, 16)
                for h in range(2):
                    def low_w(k, b, turn, kind, before):
                        dve.wait_ge(w_hi_ready, k + 1 + h * kt_count)
                        hi = w_hi[:, bass.ds(k, 1), :].rearrange("p a c -> p (a c)").bitcast(F32)
                        dve.tensor_tensor(w_lo[:, bass.ds(k, 1), :].rearrange("p a c -> p (a c)"), w_raw[b][:, :], hi,
                                          ALU.subtract).then_inc(w_lo_ready, 1)

                    def low_s(k, b, turn, kind, before):
                        dve.wait_ge(s_hi_ready, k + 1 + h * TT)
                        dve.tensor_tensor(s_lo[b][:, :, :], s_raw[:, :, :], s_hi[b][:, :, :].bitcast(F32),
                                          ALU.subtract).then_inc(s_lo_ready, 1)

                    def accumulate(k, b, turn, kind, before):
                        dve.wait_ge(multiplied, k + 1 + h * TT)
                        x = x_sb[:, bass.ds(k, 1), h * half:(h + 1) * half].rearrange("p a c -> p (a c)")
                        dve.tensor_tensor(x, acc[b][:, :], x, ALU.add).then_inc(added, 1)
                    pipelined(dve, w_kinds, [(0, low_w)])
                    pipelined(dve, t_kinds, [(0, low_s), (1, accumulate)])

            @block.tensor
            def _(pe):
                for h in range(2):
                    def product(k, b, turn, kind, before):
                        pe.wait_ge(s_lo_ready, k + 1 + h * TT)
                        if h or before:
                            pe.wait_ge(added, k - 1 + h * TT)
                        for kt in range(kt_count):
                            last = three_pass(pe, acc[b][:, :], s_hi[b][:, kt, :], s_lo[b][:, kt, :],
                                              w_hi[:, kt, :], w_lo[:, kt, :], kt == 0, kt == kt_count - 1)
                        last.then_inc(multiplied, 1)
                    pe.wait_ge(w_lo_ready, (h + 1) * kt_count)
                    pipelined(pe, t_kinds, [(0, product)])


def final_norm(nc, x_sb, g, out_prompt, out_sample):
    with ExitStack() as ctx:
        p = Phase(nc, ctx, "fin")
        gain, junk = p.sb("gain", [P, D]), p.sb("junk", [P, D])
        sumsq, root, rstd = (p.sb(n, [P, TT]) for n in ("sumsq", "root", "rstd"))
        eps, eps_set = p.sb("eps", [P, 1]), p.sem("eps_set")
        y = [p.sb(f"y{b}", [P, D]) for b in range(2)]
        gain_loaded, squared, root_ready = p.sem("gain_loaded"), p.sem("squared"), p.sem("root_ready")
        rstd_ready, y_ready = p.sem("rstd_ready"), p.sem("y_ready")
        stored = [p.sem(f"stored{b}") for b in range(2)]
        kinds = ["prompt"] * (SEQS[0][1] // P) + ["sample"] * (SEQS[1][1] // P)

        def x_of(k):
            return x_sb[:, bass.ds(k, 1), :].rearrange("p a d -> p (a d)")

        with nc.Block() as block:
            @block.sync
            def _(sp):
                sp.dma_start(gain[:, :], g.rearrange("(a d) -> a d", a=1).broadcast_to([P, D])).then_inc(gain_loaded, 16)

                def store(k, b, turn, kind, before):
                    sp.wait_ge(y_ready, k + 1)
                    dst, first = (out_prompt, 0) if kind == "prompt" else (out_sample, SEQS[1][0])
                    sp.dma_start(dst[0, bass.ds(k * P - first, P), :], y[b][:, :]).then_inc(stored[b], 16)
                pipelined(sp, kinds, [(0, store)])
                for b in range(2):
                    sp.wait_ge(stored[b], 16 * TT // 2)

            @block.scalar
            def _(act):
                act.wait_ge(eps_set, 1)

                def square(k, b, turn, kind, before):
                    act.activation(junk[:, :], x_of(k), ACT.Square,
                                   accum_out=sumsq[:, bass.ds(k, 1)]).then_inc(squared, 1)
                    act.wait_ge(squared, k + 1)
                    act.activation(root[:, bass.ds(k, 1)], sumsq[:, bass.ds(k, 1)], ACT.Sqrt, bias=eps[:, :],
                                   scale=1.0 / D).then_inc(root_ready, 1)
                pipelined(act, kinds, [(0, square)])

            @block.vector
            def _(dve):
                dve.memset(eps[:, :], EPS).then_inc(eps_set, 1)
                dve.wait_ge(gain_loaded, 16)

                def scale(k, b, turn, kind, before):
                    dve.wait_ge(root_ready, k + 1)
                    dve.reciprocal(rstd[:, bass.ds(k, 1)], root[:, bass.ds(k, 1)]).then_inc(rstd_ready, 1)
                    if before:
                        dve.wait_ge(stored[b], turn * 16)
                    dve.wait_ge(rstd_ready, k + 1)
                    dve.scalar_tensor_tensor(y[b][:, :], x_of(k), rstd[:, bass.ds(k, 1)], gain[:, :],
                                             ALU.mult, ALU.mult).then_inc(y_ready, 1)
                pipelined(dve, kinds, [(0, scale)])


C1, S1, RH = math.cos(math.pi / 8), math.sin(math.pi / 8), math.sqrt(0.5)


def transform_tables(n):
    b = n // 4
    m = np.arange(b)[:, None]
    fwd = np.zeros((CLASSES, P, 3, b // P, b // P, P), np.float32)
    inv = np.zeros((CLASSES, P, 3, b // P, b // P, P), np.float32)
    for c in range(CLASSES):
        k = c + 8 * np.arange(b)[None, :]
        phase = 2 * np.pi * ((m * (2 * k + 1)) % (4 * n)) / (4 * n)
        for j, a in enumerate((np.cos(phase), np.sin(phase), -np.sin(phase))):
            fwd[c, :, j] = a.reshape(b // P, P, b // P, P).transpose(1, 0, 2, 3)
            inv[c, :, j] = a.T.reshape(b // P, P, b // P, P).transpose(1, 0, 2, 3)
    return fwd, inv


def filter_tables():
    zs, ts = [], []
    for _, n in SEQS:
        t = np.linspace(0.0, 1.0, n, dtype=np.float32)[:, None]
        bands = (EMB - 1) // 2
        freqs = np.linspace(1e-4, bands - 1, bands, dtype=np.float32)
        ang = np.float32(2.0 * math.pi / n) * np.arange(n, dtype=np.float32)[:, None] * freqs[None, :]
        zs.append(np.concatenate([t, np.cos(ang), -np.sin(ang)], axis=-1).astype(np.float32))
        ts.append(-t[:, 0])
    lo, hi = math.log(1e-2) / 1.5, math.log(1e-2) / 0.3
    rates = np.abs(np.linspace(lo, hi, HY, dtype=np.float32))
    return (np.ascontiguousarray(np.concatenate(zs).T), np.ascontiguousarray(np.concatenate(ts).reshape(TT, P).T),
            np.ascontiguousarray(np.broadcast_to(rates, (P, HY))))


class Chain:

    def __init__(self, eng, sem):
        self.eng, self.sem, self.count = eng, sem, 0

    def __call__(self, ins):
        ins.then_inc(self.sem, 1)
        self.count += 1
        return self.count

    def need(self, count):
        self.eng.wait_ge(self.sem, count)


def radix_stage(dve, ch, x, cr, sn, tmp, width):
    r, t1, t2, u, v, pp, qq, ps_, qs = (tmp(j) for j in range(9))
    n_r = ch(dve.tensor_scalar(r, x(2), RH, None, ALU.mult))
    n_1 = ch(dve.tensor_scalar(t1, x(1), C1, None, ALU.mult))
    n_2 = ch(dve.tensor_scalar(t2, x(1), S1, None, ALU.mult))
    ch.need(n_r)
    ch(dve.tensor_tensor(u, x(0), r, ALU.add))
    ch(dve.tensor_tensor(v, x(0), r, ALU.subtract))
    ch.need(n_1)
    ch(dve.scalar_tensor_tensor(pp, x(3), S1, t1, ALU.mult, ALU.add))
    ch(dve.scalar_tensor_tensor(qs, x(3), -S1, t1, ALU.mult, ALU.add))
    ch.need(n_2)
    ch(dve.scalar_tensor_tensor(qq, x(3), -C1, t2, ALU.mult, ALU.add))
    n_p = ch(dve.scalar_tensor_tensor(ps_, x(3), C1, t2, ALU.mult, ALU.add))
    ch.need(n_p)
    for c, a, b, sign in ((0, u, pp, ALU.add), (3, u, pp, ALU.subtract), (1, v, qq, ALU.add), (2, v, qq, ALU.subtract)):
        ch(dve.tensor_tensor(cr(c), a, b, sign))
    for c, a, sign in ((0, ps_, ALU.add), (3, ps_, ALU.subtract), (1, qs, ALU.add), (2, qs, ALU.subtract)):
        last = ch(dve.tensor_tensor(sn(c), a, r, sign))
    return last


def hyena_hidden(nc, par, w1, z_t, h2_d):
    magic, two_pi_hi, two_pi_lo = 1.5 * 2.0 ** 23, 6.28125, 2 * math.pi - 6.28125
    limit = 3.1415925
    with ExitStack() as ctx:
        p = Phase(nc, ctx, "hid")
        z = p.sb("z", [EMB, T])
        w1_sb = p.sb("w1", [EMB, HID])
        w2_sb = p.sb("w2", [HID, HID])
        bf = p.sb("bf", [HID, 4])
        x, n, h = p.sb("x", [HID, T]), p.sb("n", [HID, T]), p.sb("h", [HID, T])
        acc = p.ps("acc", [HID, T])
        loaded, multiplied, step, sined, stored = (p.sem(s) for s in ("loaded", "multiplied", "step", "sined", "stored"))
        with nc.Block() as block:
            @block.sync
            def _(sp):
                sp.dma_start(z[:, :], z_t).then_inc(loaded, 16)
                sp.dma_start(w1_sb[:, :], w1).then_inc(loaded, 16)
                sp.dma_start(w2_sb[:, :], par["filt_w2"]).then_inc(loaded, 16)
                sp.dma_start(bf[:, :], par["filt_bf"]).then_inc(loaded, 16)
                sp.wait_ge(sined, 2)
                sp.dma_start(h2_d, h[:, :]).then_inc(stored, 16)
                sp.wait_ge(stored, 16)

            @block.tensor
            def _(pe):
                pe.wait_ge(loaded, 64)
                for layer, (w, src) in enumerate(((w1_sb, z), (w2_sb, h))):
                    if layer:
                        pe.wait_ge(sined, 1)
                    for c in range(NCH):
                        last = pe.matmul(acc[:, c * CH:(c + 1) * CH], w[:, :], src[:, c * CH:(c + 1) * CH],
                                         start=True, stop=True)
                    last.then_inc(multiplied, 1)

            @block.vector
            def _(dve):
                ch = Chain(dve, step)
                dve.wait_ge(loaded, 64)
                for layer in range(2):
                    dve.wait_ge(multiplied, layer + 1)
                    if layer:
                        dve.wait_ge(sined, 1)
                    ch.need(ch(dve.tensor_scalar(x[:, :], acc[:, :], bf[:, 2 * layer:2 * layer + 1],
                                                 bf[:, 2 * layer + 1:2 * layer + 2], ALU.add, ALU.mult)))
                    ch.need(ch(dve.tensor_scalar(n[:, :], x[:, :], 1 / (2 * math.pi), magic, ALU.mult, ALU.add)))
                    ch.need(ch(dve.tensor_scalar(n[:, :], n[:, :], -magic, None, ALU.add)))
                    ch.need(ch(dve.scalar_tensor_tensor(x[:, :], n[:, :], -two_pi_hi, x[:, :], ALU.mult, ALU.add)))
                    ch.need(ch(dve.scalar_tensor_tensor(x[:, :], n[:, :], -two_pi_lo, x[:, :], ALU.mult, ALU.add)))
                    ch.need(ch(dve.tensor_scalar(x[:, :], x[:, :], limit, -limit, ALU.min, ALU.max)))

            @block.scalar
            def _(act):
                for layer in range(2):
                    act.wait_ge(step, 6 * (layer + 1))
                    if layer:
                        act.wait_ge(multiplied, 2)
                    act.activation(h[:, :], x[:, :], ACT.Sin).then_inc(sined, 1)


def hyena_filters(nc, name, t0, n, tables, neg_t, rates, par, h2_d, k_d):
    nt, s_n = n // P, n // 512
    width = s_n * HY
    first = t0 // P
    with ExitStack() as ctx:
        p = Phase(nc, ctx, name)
        h2, w3 = p.sb("h2", [HID, n]), p.sb("w3", [HID, 2, ORDER, HY])
        nt_sb, rate = p.sb("neg_t", [P, TT]), p.sb("rates", [P, HY])
        keep, ones = p.sb("keep", [P, 1]), p.sb("ones", [P, P])
        decay = p.sb("decay", [P, HY])
        taps = [p.sb(f"taps{b}", [P, 2, HY]) for b in range(2)]
        squares = [p.sb(f"squares{b}", [P, 2, HY]) for b in range(2)]
        both = [p.sb(f"both{b}", [P, nt, HY]) for b in range(2)]
        cr, sn = p.sb("cr", [P, CLASSES, width]), p.sb("sn", [P, CLASSES, width])
        tmp = p.sb("tmp", [P, 9, width])
        tab = p.sb("tab", [P, 3, s_n, s_n, P])
        norm = p.sb("norm", [P, HY])
        root = p.sb("root", [P, HY])
        kout = [p.sb(f"kout{b}", [P, HY]) for b in range(2)]
        tap_acc = [p.ps(f"tap_acc{b}", [P, 2, HY]) for b in range(2)]
        sum_acc = p.ps("sum_acc", [P, HY])
        kacc = [p.ps(f"kacc{b}", [P, HY]) for b in range(2)]
        loaded, const_set, tab_loaded = p.sem("loaded"), p.sem("const_set"), p.sem("tab_loaded")
        taps_ready, decay_ready, squared = p.sem("taps_ready"), p.sem("decay_ready"), p.sem("squared")
        summed, step, combined = p.sem("summed"), p.sem("step"), p.sem("combined")
        norm_ready, rooted, staged = p.sem("norm_ready"), p.sem("rooted"), p.sem("staged")
        decayed = p.sem("decayed")
        k_ready, k_scaled = p.sem("k_ready"), p.sem("k_scaled")
        k_stored = [p.pool_dma_sem(f"k_stored{b}") for b in range(2)]

        units = [(o, ri, c, kb) for o in range(ORDER) for ri in range(2) for c in range(CLASSES) for kb in range(s_n)]

        with nc.Block() as block:
            @block.sync
            def _(sp):
                sp.dma_start(h2[:, :], h2_d[:, t0:t0 + n]).then_inc(loaded, 16)
                sp.dma_start(w3[:, :, :, :], par["filt_w3"].rearrange("h (d o c) -> h d o c", d=2, o=ORDER)).then_inc(loaded, 16)
                sp.dma_start(nt_sb[:, :], neg_t).then_inc(loaded, 16)
                sp.dma_start(rate[:, :], rates).then_inc(loaded, 16)
                sp.dma_start(keep[:, :], par["keep"]).then_inc(loaded, 16)
                for q in range(2 * ORDER * CLASSES):
                    if q:
                        sp.wait_ge(k_ready, q * s_n)
                    sp.dma_start(tab[:, :, :, :, :], tables[q % CLASSES]).then_inc(tab_loaded, 16)

            @block.tensor
            def _(pe):
                pe.wait_ge(loaded, 80)
                pe.wait_ge(const_set, 1)
                for o in range(ORDER):
                    for tt in range(nt + 1):
                        m = o * nt + tt
                        if tt < nt:
                            if m >= 2:
                                pe.wait_ge(decayed, m - 1)
                            for d in range(2):
                                last = pe.matmul(tap_acc[m % 2][:, d, :], h2[:, tt * P:(tt + 1) * P], w3[:, d, o, :],
                                                 start=True, stop=True)
                            last.then_inc(taps_ready, 1)
                        if tt > 0:
                            pe.wait_ge(squared, m)
                            if o and tt == 1:
                                pe.wait_ge(rooted, 1)
                            for d in range(2):
                                last = pe.matmul(sum_acc[:, :], ones[:, :], squares[(m - 1) % 2][:, d, :],
                                                 start=tt == 1 and d == 0, stop=tt == nt and d == 1)
                            last.then_inc(summed, 1)
                    for ri in range(2):
                        pe.wait_ge(staged, o * 2 + ri + 1)
                        for c in range(CLASSES):
                            q = (o * 2 + ri) * CLASSES + c
                            pe.wait_ge(tab_loaded, 16 * (q + 1))
                            for kb in range(s_n):
                                v = q * s_n + kb
                                if v >= 2:
                                    pe.wait_ge(k_scaled, v - 1)
                                terms = [(0, cr), (2, sn)] if ri == 0 else [(1, cr), (0, sn)]
                                for j, (which, src) in enumerate(terms):
                                    for s in range(s_n):
                                        last = pe.matmul(kacc[v % 2][:, :], tab[:, which, s, kb, :],
                                                         src[:, c, s * HY:(s + 1) * HY],
                                                         start=j == 0 and s == 0, stop=j == 1 and s == s_n - 1)
                                last.then_inc(k_ready, 1)

            @block.scalar
            def _(act):
                act.wait_ge(loaded, 80)
                for o in range(ORDER):
                    for tt in range(nt):
                        m = o * nt + tt
                        if m:
                            act.wait_ge(decayed, m)
                        act.activation(decay[:, :], rate[:, :], ACT.Exp,
                                       scale=nt_sb[:, first + tt:first + tt + 1]).then_inc(decay_ready, 1)
                        act.wait_ge(decayed, m + 1)
                        if m >= 2:
                            act.wait_ge(summed, m - 1)
                        act.activation(squares[m % 2][:, :, :], taps[m % 2][:, :, :], ACT.Square).then_inc(squared, 1)
                    act.wait_ge(summed, (o + 1) * nt)
                    act.activation(root[:, :], sum_acc[:, :], ACT.Sqrt, scale=float(n) * n).then_inc(rooted, 1)

            @block.gpsimd
            def _(pool):
                pool.memset(ones[:, :], 1.0).then_inc(const_set, 1)
                for o in range(ORDER):
                    for tt in range(nt):
                        m = o * nt + tt
                        pool.wait_ge(decayed, m + 1)
                        if o and tt == 0:
                            pool.wait_ge(staged, 2 * o)
                        pool.tensor_tensor(both[0][:, tt, :], taps[m % 2][:, 0, :], taps[m % 2][:, 1, :], ALU.add)
                        pool.tensor_tensor(both[1][:, tt, :], taps[m % 2][:, 0, :], taps[m % 2][:, 1, :],
                                           ALU.subtract).then_inc(combined, 1)
                    for v, (_, ri, c, kb) in enumerate(units[:len(units) // ORDER]):
                        v += o * len(units) // ORDER
                        pool.wait_ge(k_scaled, v + 1)
                        pool.dma_start(k_d[o, c, :, ri, kb, :], kout[v % 2][:, :]).then_inc(k_stored[v % 2], 16)
                for b in range(2):
                    pool.wait_ge(k_stored[b], 16 * (len(units) // 2))

            @block.vector
            def _(dve):
                ch = Chain(dve, step)
                dve.wait_ge(loaded, 80)
                for o in range(ORDER):
                    for tt in range(nt):
                        m = o * nt + tt
                        dve.wait_ge(taps_ready, m + 1)
                        dve.wait_ge(decay_ready, m + 1)
                        if m >= 2:
                            dve.wait_ge(squared, m - 1)
                            dve.wait_ge(combined, m - 1)
                        dve.tensor_tensor(taps[m % 2][:, 0, :], tap_acc[m % 2][:, 0, :], decay[:, :], ALU.mult)
                        dve.scalar_tensor_tensor(taps[m % 2][:, 1, :], tap_acc[m % 2][:, 1, :],
                                                 keep[:, :] if tt == 0 else 1.0, decay[:, :],
                                                 ALU.mult, ALU.mult).then_inc(decayed, 1)
                    dve.wait_ge(rooted, o + 1)
                    if o:
                        dve.wait_ge(k_scaled, o * 2 * CLASSES * s_n)
                    ch.need(ch(dve.reciprocal(norm[:, :], root[:, :])))
                    dve.wait_ge(combined, (o + 1) * nt)
                    for ri in range(2):
                        q = o * 2 + ri
                        if q:
                            dve.wait_ge(k_ready, q * CLASSES * s_n)
                        radix_stage(dve, ch, lambda a: both[ri][:, a * s_n:(a + 1) * s_n, :].rearrange("p s c -> p (s c)"),
                                    lambda c: cr[:, c, :], lambda c: sn[:, c, :], lambda j: tmp[:, j, :], width)
                        ch.need(ch.count)
                        dve.sem_inc(staged, 1)
                        for c in range(CLASSES):
                            for kb in range(s_n):
                                v = (q * CLASSES + c) * s_n + kb
                                dve.wait_ge(k_ready, v + 1)
                                if v >= 2:
                                    dve.wait_ge(k_stored[v % 2], 16 * (v // 2))
                                dve.tensor_tensor(kout[v % 2][:, :], kacc[v % 2][:, :], norm[:, :],
                                                  ALU.mult).then_inc(k_scaled, 1)


def long_convolution(nc, name, t0, n, o, fwd_tab, inv_tab, k_d, bias, z, mix_d, tok_col, ident, y_d):
    s_n = n // 512
    nt = n // P
    width = s_n * HY
    first = t0 // P
    with ExitStack() as ctx:
        p = Phase(nc, ctx, name)
        gate = p.sb("gate", [P, nt, HY])
        bias_sb = p.sb("bias", [P, HY])
        cr, sn = p.sb("cr", [P, CLASSES, width]), p.sb("sn", [P, CLASSES, width])
        tmp = p.sb("tmp", [P, 9, width])
        tab = [p.sb(f"tab{b}", [P, 2, 3, s_n, s_n, P]) for b in range(2)]
        kf = [p.sb(f"kf{b}", [P, 2, s_n, HY]) for b in range(2)]
        prod = p.sb("prod", [P, 4, HY])
        spec = [p.sb(f"spec{b}", [P, 2, s_n, HY]) for b in range(2)]
        facc = [p.ps(f"facc{b}", [P, 2, HY]) for b in range(2)]
        iacc = [p.ps(f"iacc{b}", [P, 2, HY]) for b in range(2)]
        z_loaded, loaded, step = p.sem("z_loaded"), p.sem("loaded"), p.sem("step")
        tab_loaded = [p.sem(f"tab_loaded{b}") for b in range(2)]
        k_loaded = [p.sem(f"k_loaded{b}") for b in range(2)]
        staged, f_ready, products, spec_ready = (p.sem(s) for s in ("staged", "f_ready", "products", "spec_ready"))
        i_ready, i_copied, mixed = p.sem("i_ready"), p.sem("i_copied"), p.sem("mixed")
        transposed, copied, stored, biased = p.sem("transposed"), p.sem("copied"), p.sem("stored"), p.sem("biased")

        y_t = cr[:, :, :].rearrange("p a b -> p (a b)").rearrange("p (c t q) -> p c t q", c=HY // P, q=P)

        with nc.Block() as block:
            @block.sync
            def _(sp):
                def rows(col):
                    return mix_d[first:first + nt, :, col:col + HY].rearrange("t p c -> p t c")
                if o == 0:
                    sp.dma_start(z[:, 0:nt, :], rows(2 * HY)).then_inc(z_loaded, 16)
                sp.dma_start(gate[:, :, :], rows(tok_col)).then_inc(loaded, 16)
                sp.dma_start(bias_sb[:, :], bias.broadcast_to([P, HY])).then_inc(loaded, 16)
                for c in range(CLASSES):
                    if c >= 2:
                        sp.wait_ge(i_ready, (c - 1) * s_n)
                    sp.dma_start(tab[c % 2][:, 0, :, :, :, :], fwd_tab[c]).then_inc(tab_loaded[c % 2], 16)
                    sp.dma_start(tab[c % 2][:, 1, :, :, :, :], inv_tab[c]).then_inc(tab_loaded[c % 2], 16)
                    sp.dma_start(kf[c % 2][:, :, :, :], k_d[o, c]).then_inc(k_loaded[c % 2], 16)
                if o == ORDER - 1:
                    sp.wait_ge(copied, nt)
                    for ct in range(HY // P):
                        sp.dma_start(y_d[ct, :, t0:t0 + n].rearrange("p (t q) -> p t q", q=P),
                                     y_t[:, ct, :, :]).then_inc(stored, 16)
                    sp.wait_ge(stored, 16 * (HY // P))

            @block.tensor
            def _(pe):
                def forward(c):
                    pe.wait_ge(tab_loaded[c % 2], 32 * (c // 2 + 1))
                    for kb in range(s_n):
                        v = c * s_n + kb
                        if v >= 2:
                            pe.wait_ge(products, v - 1)
                        for ri, terms in enumerate((((0, cr), (2, sn)), ((1, cr), (0, sn)))):
                            for j, (which, src) in enumerate(terms):
                                for s in range(s_n):
                                    last = pe.matmul(facc[v % 2][:, ri, :], tab[c % 2][:, 0, which, s, kb, :],
                                                     src[:, c, s * HY:(s + 1) * HY],
                                                     start=j == 0 and s == 0, stop=j == 1 and s == s_n - 1)
                        last.then_inc(f_ready, 1)

                def inverse(c):
                    pe.wait_ge(spec_ready, (c + 1) * s_n)
                    for sb in range(s_n):
                        v = c * s_n + sb
                        if v >= 2:
                            pe.wait_ge(i_copied, v - 1)
                        for ri, terms in enumerate((((0, 0), (1, 1)), ((0, 1), (2, 0)))):
                            for j, (which, part) in enumerate(terms):
                                for kb in range(s_n):
                                    last = pe.matmul(iacc[v % 2][:, ri, :], tab[c % 2][:, 1, which, kb, sb, :],
                                                     spec[c % 2][:, part, kb, :],
                                                     start=j == 0 and kb == 0, stop=j == 1 and kb == s_n - 1)
                        last.then_inc(i_ready, 1)

                pe.wait_ge(staged, 1)
                forward(0)
                for c in range(1, CLASSES):
                    forward(c)
                    inverse(c - 1)
                inverse(CLASSES - 1)
                if o == ORDER - 1:
                    pe.wait_ge(mixed, 1)
                    for tt in range(nt):
                        if tt >= 2:
                            pe.wait_ge(copied, tt - 1)
                        for ct in range(HY // P):
                            last = pe.transpose(facc[tt % 2][:, 0, ct * P:(ct + 1) * P],
                                                z[:, tt, ct * P:(ct + 1) * P], ident[:, :])
                        last.then_inc(transposed, 1)

            @block.scalar
            def _(act):
                for v in range(CLASSES * s_n):
                    c, sb = v // s_n, v % s_n
                    act.wait_ge(i_ready, v + 1)
                    act.activation(cr[:, c, sb * HY:(sb + 1) * HY], iacc[v % 2][:, 0, :], ACT.Copy)
                    act.activation(sn[:, c, sb * HY:(sb + 1) * HY], iacc[v % 2][:, 1, :], ACT.Copy).then_inc(i_copied, 1)
                if o == ORDER - 1:
                    for tt in range(nt):
                        act.wait_ge(transposed, tt + 1)
                        act.activation(y_t[:, :, tt, :], facc[tt % 2][:, 0, :].rearrange("p (c q) -> p c q", q=P),
                                       ACT.Copy).then_inc(copied, 1)

            @block.gpsimd
            def _(pool):
                pool.wait_ge(loaded, 32)
                pool.wait_ge(staged, 1)
                for v in range(CLASSES * s_n):
                    c, kb = v // s_n, v % s_n
                    pool.wait_ge(products, v + 1)
                    if c >= 2:
                        pool.wait_ge(i_ready, (c - 1) * s_n)
                    pool.tensor_tensor(spec[c % 2][:, 0, kb, :], prod[:, 0, :], prod[:, 1, :], ALU.subtract)
                    pool.tensor_tensor(spec[c % 2][:, 1, kb, :], prod[:, 2, :], prod[:, 3, :],
                                       ALU.add).then_inc(spec_ready, 1)

            @block.vector
            def _(dve):
                ch = Chain(dve, step)
                if o == 0:
                    dve.wait_ge(z_loaded, 16)

                def slab(buf, a):
                    return buf[:, a * s_n:(a + 1) * s_n, :].rearrange("p s c -> p (s c)")
                radix_stage(dve, ch, lambda a: slab(z, a), lambda c: cr[:, c, :], lambda c: sn[:, c, :],
                            lambda j: tmp[:, j, :], width)
                ch.need(ch.count)
                dve.sem_inc(staged, 1)
                for v in range(CLASSES * s_n):
                    c, kb = v // s_n, v % s_n
                    dve.wait_ge(f_ready, v + 1)
                    dve.wait_ge(k_loaded[c % 2], 16 * (c // 2 + 1))
                    if v:
                        dve.wait_ge(spec_ready, v)
                    xr, xn, k = facc[v % 2][:, 0, :], facc[v % 2][:, 1, :], kf[c % 2]
                    dve.tensor_tensor(prod[:, 0, :], xr, k[:, 0, kb, :], ALU.mult)
                    dve.tensor_tensor(prod[:, 1, :], xn, k[:, 1, kb, :], ALU.mult)
                    dve.tensor_tensor(prod[:, 2, :], xr, k[:, 1, kb, :], ALU.mult)
                    dve.tensor_tensor(prod[:, 3, :], xn, k[:, 0, kb, :], ALU.mult).then_inc(products, 1)
                dve.wait_ge(i_copied, CLASSES * s_n)
                dve.wait_ge(loaded, 32)
                dr, dn, t = (lambda c: cr[:, c, :]), (lambda c: sn[:, c, :]), (lambda j: tmp[:, j, :])
                for j, (src, c, e, op) in enumerate(((dr, 0, 3, ALU.add), (dr, 0, 3, ALU.subtract), (dr, 1, 2, ALU.add),
                                                     (dr, 1, 2, ALU.subtract), (dn, 0, 3, ALU.add), (dn, 0, 3, ALU.subtract),
                                                     (dn, 1, 2, ALU.add), (dn, 1, 2, ALU.subtract))):
                    ch(dve.tensor_tensor(t(j), src(c), src(e), op))
                ch.need(ch.count)
                y = dr
                ch(dve.tensor_tensor(y(0), t(0), t(2), ALU.add))
                ch(dve.tensor_tensor(y(2), t(0), t(2), ALU.subtract))
                ch(dve.tensor_tensor(t(8), t(5), t(7), ALU.add))
                ch(dve.tensor_scalar(y(1), t(1), C1, None, ALU.mult))
                ch(dve.tensor_scalar(y(3), t(1), S1, None, ALU.mult))
                ch.need(ch.count)
                ch(dve.tensor_tensor(y(2), y(2), t(8), ALU.add))
                for j, w1_, w3_ in ((3, S1, -C1), (4, S1, C1), (6, C1, -S1)):
                    ch(dve.scalar_tensor_tensor(y(1), t(j), w1_, y(1), ALU.mult, ALU.add))
                    ch(dve.scalar_tensor_tensor(y(3), t(j), w3_, y(3), ALU.mult, ALU.add))
                    ch.need(ch.count)
                ch(dve.tensor_scalar(y(2), y(2), RH, None, ALU.mult))
                for tt in range(nt):
                    a, s = tt // s_n, tt % s_n
                    ys = cr[:, a, s * HY:(s + 1) * HY]
                    zs = z[:, tt, :]
                    ch.need(ch(dve.tensor_tensor(zs, zs, bias_sb[:, :], ALU.mult)))
                    ch.need(ch(dve.tensor_tensor(zs, zs, ys, ALU.add)))
                    ch(dve.tensor_tensor(zs, zs, gate[:, tt, :], ALU.mult))
                ch.need(ch.count)
                dve.sem_inc(mixed, 1)


DIRS = 2
GATE_P = 64


def mlstm_gates(nc, gates_d, neg_max_d, a_cols, floor_cols, ident):
    with ExitStack() as ctx:
        p = Phase(nc, ctx, "gates")
        gi, gf, ab, ls, one, f_sum, a, top, m, fl = (p.sb(s, [GATE_P, T]) for s in (
            "gi", "gf", "ab", "ls", "one", "f_sum", "a", "top", "m", "floor"))
        tbank = [p.ps(f"tbank{b}", [P, TT, GATE_P]) for b in range(2)]
        loaded, step, soft, floored = p.sem("loaded"), p.sem("step"), p.sem("soft"), p.sem("floored")
        act_step, transposed, copied, stored = p.sem("act_step"), p.sem("transposed"), p.sem("copied"), p.sem("stored")
        m_ready, a_ready, top_ready = p.sem("m_ready"), p.sem("a_ready"), p.sem("top_ready")

        def scans():
            for d in range(DIRS):
                for t0, n in SEQS:
                    yield slice(32 * d, 32 * d + 32), slice(t0, t0 + n), d == 1

        with nc.Block() as block:
            @block.sync
            def _(sp):
                sp.dma_start(gi[:, :], gates_d[0, 0:GATE_P, :]).then_inc(loaded, 16)
                sp.dma_start(gf[:, :], gates_d[0, GATE_P:P, :]).then_inc(loaded, 16)
                sp.wait_ge(top_ready, 1)
                sp.dma_start(neg_max_d, top[:, :]).then_inc(stored, 16)
                sp.wait_ge(stored, 16)

            @block.scalar
            def _(act):
                act.wait_ge(loaded, 32)
                act.activation(ab[:, :], gf[:, :], ACT.Abs).then_inc(act_step, 1)
                act.wait_ge(act_step, 1)
                act.activation(ab[:, :], ab[:, :], ACT.Exp, scale=-1.0).then_inc(act_step, 1)
                act.wait_ge(act_step, 2)
                act.activation(ab[:, :], ab[:, :], ACT.Ln, bias=1.0).then_inc(soft, 1)
                act.wait_ge(m_ready, 1)
                act.activation(fl[:, :], m[:, :], ACT.Exp, scale=-1.0).then_inc(floored, 1)

            @block.vector
            def _(dve):
                ch = Chain(dve, step)
                ch(dve.memset(one[:, :], 1.0))
                dve.wait_ge(soft, 1)
                ch.need(ch(dve.scalar_tensor_tensor(ls[:, :], gf[:, :], 0.0, ab[:, :], ALU.min, ALU.subtract)))
                for rows, cols, back in scans():
                    o, x = f_sum[rows, cols], ls[rows, cols]
                    ch(dve.tensor_tensor_scan(out=o[:, ::-1] if back else o, data0=one[rows, cols],
                                              data1=x[:, ::-1] if back else x, initial=0.0, op0=ALU.mult, op1=ALU.add))
                ch.need(ch.count)
                ch.need(ch(dve.tensor_tensor(a[:, :], gi[:, :], f_sum[:, :], ALU.subtract)))
                for rows, cols, back in scans():
                    o, x = top[rows, cols], a[rows, cols]
                    ch(dve.tensor_tensor_scan(out=o[:, ::-1] if back else o, data0=x[:, ::-1] if back else x,
                                              data1=x[:, ::-1] if back else x, initial=0.0, op0=ALU.max, op1=ALU.max))
                ch.need(ch.count)
                dve.tensor_tensor(m[:, :], f_sum[:, :], top[:, :], ALU.add).then_inc(m_ready, 1)
                dve.wait_ge(m_ready, 1)
                dve.tensor_scalar(a[:, :], a[:, :], math.log(HD ** -0.5), None, ALU.add).then_inc(a_ready, 1)
                dve.tensor_scalar(top[:, :], top[:, :], -1.0, None, ALU.mult).then_inc(top_ready, 1)
                for j, cols in enumerate((a_cols, floor_cols)):
                    dve.wait_ge(transposed, j + 1)
                    dve.tensor_copy(cols[:, :, :], tbank[j][:, :, :]).then_inc(copied, 1)

            @block.tensor
            def _(pe):
                for j, src in enumerate((a, fl)):
                    pe.wait_ge((a_ready, floored)[j], 1)
                    for tt in range(TT):
                        last = pe.transpose(tbank[j][:, tt, :], src[:, tt * P:(tt + 1) * P], ident[0:GATE_P, 0:GATE_P])
                    last.then_inc(transposed, 1)


def mlstm_heads(nc, qk_d, tok_d, o_d, neg_max_d, masks, ml_gain, a_cols, floor_cols, ident, y_d):
    jobs = [(h, s) for h in range(HEADS) for s in range(len(SEQS))]
    kinds = [f"job {j}" for j in range(len(jobs))]
    nts = [n // P for _, n in SEQS]
    most = max(nts)
    W = HD + 1
    with ExitStack() as ctx:
        p = Phase(nc, ctx, "heads")
        q, k = ([p.sb(f"{s}{b}", [P, T]) for b in range(2)] for s in ("q", "k"))
        v = [p.sb(f"v{b}", [P, TT, W]) for b in range(2)]
        neg_m = [p.sb(f"neg_m{d}", [P, T]) for d in range(DIRS)]
        diag = [p.sb(f"diag{d}", [P, TT, P]) for d in range(DIRS)]
        mask = p.sb("mask", [P, DIRS, P])
        e = [[p.sb(f"e{d}_{b}", [P, most * P]) for b in range(2)] for d in range(DIRS)]
        pt = [[p.sb(f"pt{d}_{b}", [P, most * (most + 1) // 2, P]) for b in range(2)] for d in range(DIRS)]
        hs = p.sb("hs", [P, most, DIRS, W])
        den, rden = p.sb("den", [P, most, DIRS]), p.sb("rden", [P, most, DIRS])
        x1, x2 = p.sb("x1", [P, most, HD]), p.sb("x2", [P, most, HD])
        hn = p.sb("hn", [P, most, HD])
        ss, rs = p.sb("ss", [P, most]), p.sb("rs", [P, most])
        eps = p.sb("eps", [P, 1])
        gm = p.sb("gain", [P, HEADS])
        og, y = p.sb("og", [P, T]), p.sb("y", [P, T])
        sacc = [p.ps(f"sacc{b}", [P, most * P]) for b in range(2)]
        hacc = [p.ps(f"hacc{b}", [P, CH]) for b in range(2)]
        tbank = [p.ps(f"tbank{b}", [P, CH]) for b in range(2)]
        names = ("const_loaded const_set v_set ones_set m_loaded diag_ready scored exp_ready weighted attended "
                 "h_copied abs_ready squared step normed transposed scaled y_stored og_loaded rooted").split()
        sem = {s: p.sem(s) for s in names}
        qk_loaded = [p.sem(f"qk_loaded{b}") for b in range(2)]
        v_loaded = [p.sem(f"v_loaded{b}") for b in range(2)]

        tiles_before = [sum(nts[s] for _, s in jobs[:j]) for j in range(len(jobs) + 1)]

        def place(d, nt, s_tile, t_tile):
            if d == 0:
                return s_tile * nt - s_tile * (s_tile - 1) // 2 + t_tile - s_tile
            return s_tile * (s_tile + 1) // 2 + t_tile

        with nc.Block() as block:
            @block.sync
            def _(sp):
                sp.dma_start(mask[:, :, :], masks).then_inc(sem["const_loaded"], 16)
                sp.dma_start(gm[:, :], ml_gain).then_inc(sem["const_loaded"], 16)
                for h in range(HEADS):
                    b = h % 2
                    if h >= 2:
                        sp.wait_ge(sem["attended"], tiles_before[2 * (h - 1)])
                    sp.dma_start(q[b][:, :], qk_d[h]).then_inc(qk_loaded[b], 16)
                    sp.dma_start(k[b][:, :], qk_d[HEADS + h]).then_inc(qk_loaded[b], 16)
                    if h == 0:
                        sp.wait_ge(sem["ones_set"], 2)
                    sp.dma_start(v[b][:, :, 0:HD], tok_d[:, :, 3 * HY + h * HD:3 * HY + (h + 1) * HD].rearrange(
                        "t p c -> p t c")).then_inc(v_loaded[b], 16)
                    if h:
                        sp.wait_ge(sem["exp_ready"], tiles_before[2 * h])
                    for d in range(DIRS):
                        row = neg_max_d[32 * d + h:32 * d + h + 1, :]
                        sp.dma_start(neg_m[d][:, :], row.broadcast_to([P, T])).then_inc(sem["m_loaded"], 16)
                    if h:
                        sp.wait_ge(sem["scaled"], tiles_before[2 * h])
                        sp.dma_start(y_d[HY // P + h - 1], y[:, :]).then_inc(sem["y_stored"], 16)
                    sp.dma_start(og[:, :], o_d[h]).then_inc(sem["og_loaded"], 16)
                sp.wait_ge(sem["scaled"], tiles_before[-1])
                sp.dma_start(y_d[HY // P + HEADS - 1], y[:, :]).then_inc(sem["y_stored"], 16)
                sp.wait_ge(sem["y_stored"], 16 * HEADS)

            @block.gpsimd
            def _(pool):
                for b in range(2):
                    pool.memset(v[b][:, :, HD:W], 1.0).then_inc(sem["ones_set"], 1)
                pool.memset(eps[:, :], EPS).then_inc(sem["const_set"], 1)
                pool.wait_ge(sem["const_loaded"], 32)
                for h in range(HEADS):
                    pool.wait_ge(sem["m_loaded"], 32 * (h + 1))
                    if h:
                        pool.wait_ge(sem["exp_ready"], tiles_before[2 * h])
                    for d in range(DIRS):
                        pool.tensor_tensor(diag[d][:, :, :], neg_m[d][:, :].rearrange("p (t q) -> p t q", q=P),
                                           mask[:, d:d + 1, :].broadcast_to([P, TT, P]),
                                           ALU.add).then_inc(sem["diag_ready"], 1)

            @block.tensor
            def _(pe):
                pe.wait_ge(sem["ones_set"], 2)

                def score(j, jb, turn, kind, before):
                    h, s = jobs[j]
                    t0, n = SEQS[s]
                    if s == 0:
                        pe.wait_ge(qk_loaded[h % 2], 32 * (h // 2 + 1))
                    for st in range(nts[s]):
                        i = tiles_before[j] + st
                        if i >= 2:
                            pe.wait_ge(sem["weighted"], i - 1)
                        for c in range(0, n, CH):
                            last = pe.matmul(sacc[i % 2][:, c:c + CH], k[h % 2][:, t0 + st * P:t0 + (st + 1) * P],
                                             q[h % 2][:, t0 + c:t0 + c + CH], start=True, stop=True)
                        last.then_inc(sem["scored"], 1)

                def attend(j, jb, turn, kind, before):
                    h, s = jobs[j]
                    nt, first = nts[s], SEQS[s][0] // P
                    if s == 0:
                        pe.wait_ge(v_loaded[h % 2], 16 * (h // 2 + 1))
                    pe.wait_ge(sem["weighted"], tiles_before[j + 1])
                    for tt in range(nt):
                        i = tiles_before[j] + tt
                        if i >= 2:
                            pe.wait_ge(sem["h_copied"], i - 1)
                        for d in range(DIRS):
                            keys = range(0, tt + 1) if d == 0 else range(tt, nt)
                            for st in keys:
                                last = pe.matmul(hacc[i % 2][:, d * W:(d + 1) * W], pt[d][jb][:, place(d, nt, st, tt), :],
                                                 v[h % 2][:, first + st, :], start=st == keys[0], stop=st == keys[-1])
                        last.then_inc(sem["attended"], 1)

                def turn_tiles(j, jb, turn, kind, before):
                    nt = nts[jobs[j][1]]
                    pe.wait_ge(sem["normed"], j + 1)
                    for tt in range(nt):
                        i = tiles_before[j] + tt
                        if i >= 2:
                            pe.wait_ge(sem["scaled"], i - 1)
                        pe.transpose(tbank[i % 2][:, 0:P], hn[:, tt, :], ident[:, :]).then_inc(sem["transposed"], 1)
                pipelined(pe, kinds, [(0, score), (1, attend), (2, turn_tiles)])

            @block.scalar
            def _(act):
                act.wait_ge(sem["const_set"], 1)

                def weights(j, jb, turn, kind, before):
                    h, s = jobs[j]
                    nt, first = nts[s], SEQS[s][0] // P
                    act.wait_ge(sem["diag_ready"], 2 * (h + 1))
                    for st in range(nt):
                        i = tiles_before[j] + st
                        if i >= 2:
                            act.wait_ge(sem["weighted"], i - 1)
                        for d in range(DIRS):
                            bias = a_cols[:, first + st, 32 * d + h:32 * d + h + 1]
                            dst, tile = e[d][i % 2], first + st
                            lo, hi = ((st + 1, nt) if d == 0 else (0, st))
                            last = act.activation(dst[:, st * P:(st + 1) * P], diag[d][:, tile, :], ACT.Exp, bias=bias)
                            if hi > lo:
                                last = act.activation(dst[:, lo * P:hi * P], neg_m[d][:, (first + lo) * P:(first + hi) * P],
                                                      ACT.Exp, bias=bias)
                        last.then_inc(sem["exp_ready"], 1)

                def copy_heads(j, jb, turn, kind, before):
                    nt = nts[jobs[j][1]]
                    if j:
                        act.wait_ge(sem["squared"], j)
                    for tt in range(nt):
                        i = tiles_before[j] + tt
                        act.wait_ge(sem["attended"], i + 1)
                        act.activation(hs[:, tt, :, :].rearrange("p d w -> p (d w)"), hacc[i % 2][:, 0:DIRS * W],
                                       ACT.Copy).then_inc(sem["h_copied"], 1)
                    act.wait_ge(sem["h_copied"], tiles_before[j + 1])
                    act.activation(den[:, 0:nt, :], hs[:, 0:nt, :, HD], ACT.Abs).then_inc(sem["abs_ready"], 1)

                def root(j, jb, turn, kind, before):
                    nt = nts[jobs[j][1]]
                    act.wait_ge(sem["squared"], j + 1)
                    act.activation(rs[:, 0:nt], ss[:, 0:nt], ACT.Sqrt, bias=eps[:, :], scale=1.0 / HD
                                   ).then_inc(sem["rooted"], 1)
                pipelined(act, kinds, [(0, weights), (1, copy_heads), (1, root)])

            @block.vector
            def _(dve):
                ch = Chain(dve, sem["step"])
                dve.wait_ge(sem["const_loaded"], 32)

                def weigh(j, jb, turn, kind, before):
                    s = jobs[j][1]
                    nt = nts[s]
                    if before:
                        dve.wait_ge(sem["attended"], tiles_before[j - 1])
                    for st in range(nt):
                        i = tiles_before[j] + st
                        dve.wait_ge(sem["scored"], i + 1)
                        dve.wait_ge(sem["exp_ready"], i + 1)
                        for d in range(DIRS):
                            lo, hi = (st, nt) if d == 0 else (0, st + 1)
                            at = place(d, nt, st, lo)
                            last = dve.tensor_tensor(pt[d][jb][:, at:at + hi - lo, :].rearrange("p t q -> p (t q)"),
                                                     sacc[i % 2][:, lo * P:hi * P], e[d][i % 2][:, lo * P:hi * P], ALU.mult)
                        last.then_inc(sem["weighted"], 1)

                def normalise(j, jb, turn, kind, before):
                    h, s = jobs[j]
                    nt, first = nts[s], SEQS[s][0] // P
                    dve.wait_ge(sem["abs_ready"], j + 1)
                    floor = floor_cols[:, first:first + nt, :].rearrange("p t (d r) -> p t d r", d=DIRS)[:, :, :, h]
                    ch.need(ch(dve.tensor_tensor(den[:, 0:nt, :], den[:, 0:nt, :], floor, ALU.max)))
                    ch.need(ch(dve.reciprocal(rden[:, 0:nt, :], den[:, 0:nt, :])))
                    for d, x in ((0, x1), (1, x2)):
                        ch(dve.tensor_tensor(x[:, 0:nt, :], hs[:, 0:nt, d, 0:HD],
                                             rden[:, 0:nt, d:d + 1].broadcast_to([P, nt, HD]), ALU.mult))
                    ch.need(ch.count)
                    ch.need(ch(dve.tensor_tensor(x1[:, 0:nt, :], x1[:, 0:nt, :], x2[:, 0:nt, :], ALU.add)))
                    ch.need(ch(dve.tensor_tensor(x2[:, 0:nt, :], x1[:, 0:nt, :], x1[:, 0:nt, :], ALU.mult)))
                    dve.reduce_sum(ss[:, 0:nt], x2[:, 0:nt, :], axis=mybir.AxisListType.X).then_inc(sem["squared"], 1)
                    dve.wait_ge(sem["rooted"], j + 1)
                    ch.need(ch(dve.reciprocal(rs[:, 0:nt], rs[:, 0:nt])))
                    if j:
                        dve.wait_ge(sem["transposed"], tiles_before[j])
                    dve.tensor_tensor(hn[:, 0:nt, :], x1[:, 0:nt, :],
                                      rs[:, 0:nt].unsqueeze(2).broadcast_to([P, nt, HD]), ALU.mult).then_inc(sem["normed"], 1)

                def scale(j, jb, turn, kind, before):
                    h, s = jobs[j]
                    t0, nt = SEQS[s][0], nts[s]
                    dve.wait_ge(sem["og_loaded"], 16 * (h + 1))
                    if h:
                        dve.wait_ge(sem["y_stored"], 16 * h)
                    for tt in range(nt):
                        i = tiles_before[j] + tt
                        dve.wait_ge(sem["transposed"], i + 1)
                        cols = slice(t0 + tt * P, t0 + (tt + 1) * P)
                        dve.scalar_tensor_tensor(y[:, cols], tbank[i % 2][:, 0:P], gm[:, h:h + 1], og[:, cols],
                                                 ALU.mult, ALU.mult).then_inc(sem["scaled"], 1)
                pipelined(dve, kinds, [(0, weigh), (2, scale), (1, normalise)])


WEIGHTS = ["w_in_t", "w_out_t", "w_up_t", "w_down_t"]


def encoder(nc, a, out_prompt, out_sample):
    def scratch(name, shape):
        return nc.dram_tensor(name, shape, F32).ap()
    h2_d = scratch("h2_scratch", (HID, T))
    k_d = [scratch(f"k_scratch{s}", (ORDER, CLASSES, P, 2, n // 512, HY)) for s, (_, n) in enumerate(SEQS)]
    qk_d = scratch("qk_scratch", (N_QK, P, T))
    tok_d = scratch("tok_scratch", (TT, P, 4 * HY))
    o_d = scratch("o_scratch", (N_O, P, T))
    gates_d = scratch("gates_scratch", (1, P, T))
    neg_max_d = scratch("neg_max_scratch", (GATE_P, T))
    y_d = scratch("y_scratch", (KD, P, T))
    g_d = scratch("g_scratch", (KF, P, T))

    with ExitStack() as whole:
        Phase.lasting = whole
        w = Phase(nc, whole, "all")
        ident = w.sb("ident", [P, P])
        ident_loaded = w.sem("ident_loaded")
        with nc.Block() as block:
            @block.sync
            def _(sp):
                sp.dma_start(ident[:, :], a["identity"]).then_inc(ident_loaded, 16)
                sp.wait_ge(ident_loaded, 16)

        hyena_hidden(nc, a, a["filt_w1"], a["positions"], h2_d)
        for s, (t0, n) in enumerate(SEQS):
            hyena_filters(nc, f"filt{s}", t0, n, a[f"fwd{s}"], a["neg_t"], a["rates"], a, h2_d, k_d[s])
        with ExitStack() as ctx:
            p = Phase(nc, ctx, "h1")
            ht_hi, ht_lo = p.sb("hi", [P, KD, T], F32R), p.sb("lo", [P, KD, T], F32R)
            norm_transpose(nc, "n1", a["norm1_g"], ident, ht_hi, ht_lo, x_dram=a["x"])
            input_projection(nc, a["w_in_t"], a["conv_par"], a["gate_bias"], ident, ht_hi, ht_lo, qk_d, tok_d, o_d, gates_d)
        for s, (t0, n) in enumerate(SEQS):
            with ExitStack() as ctx:
                z = Phase(nc, ctx, f"z{s}").sb("z", [P, n // P, HY])
                for o in range(ORDER):
                    long_convolution(nc, f"conv{s}{o}", t0, n, o, a[f"fwd{s}"], a[f"inv{s}"], k_d[s],
                                     a["hy_bias"][o:o + 1, :], z, tok_d, o * HY, ident, y_d)
        with ExitStack() as ctx:
            p = Phase(nc, ctx, "cols")
            a_cols, floor_cols = p.sb("a", [P, TT, GATE_P]), p.sb("floor", [P, TT, GATE_P])
            mlstm_gates(nc, gates_d, neg_max_d, a_cols, floor_cols, ident)
            mlstm_heads(nc, qk_d, tok_d, o_d, neg_max_d, a["masks"], a["ml_gain"], a_cols, floor_cols, ident, y_d)
        x_sb = w.sb("x", [P, TT, D])
        token_major_projection(nc, "out", KD, a["w_out_t"], y_d, x_sb, x_dram=a["x"])
        with ExitStack() as ctx:
            p = Phase(nc, ctx, "h2")
            ht_hi, ht_lo = p.sb("hi", [P, KD, T], F32R), p.sb("lo", [P, KD, T], F32R)
            norm_transpose(nc, "n2", a["norm2_g"], ident, ht_hi, ht_lo, x_sb=x_sb)
            gated_up_projection(nc, a["w_up_t"], a["ffn_par"], ht_hi, ht_lo, g_d)
        token_major_projection(nc, "down", KF, a["w_down_t"], g_d, x_sb)
        final_norm(nc, x_sb, a["final_g"], out_prompt, out_sample)


def laid_out(inputs):
    get = {n: np.asarray(v) for n, v in inputs.items()}
    a = {}
    a["x"] = np.concatenate([get["x_prompt"].reshape(-1, D), get["x_sample"].reshape(-1, D)]).reshape(TT, P, D)
    w_in = get["w_in"][0]
    hy, ml = 3 * HY, HEADS * HD
    gate_cols = np.zeros((D, P), np.float32)
    for g, row in enumerate(GATE_ROWS):
        gate_cols[:, row:row + HEADS] = w_in[:, hy + 4 * ml + g * HEADS:hy + 4 * ml + (g + 1) * HEADS]
    w = np.concatenate([w_in[:, hy:hy + 2 * ml], w_in[:, :hy], w_in[:, hy + 2 * ml:hy + 4 * ml], gate_cols], axis=1)

    def column_tiles(m):
        return m.reshape(KD, P, -1, P).transpose(2, 1, 0, 3)

    a["w_in_t"] = column_tiles(w)
    par = np.concatenate([get["conv_w"][0], get["conv_b"]], axis=0)
    par = np.concatenate([par[:, hy:], par[:, :hy]], axis=1)
    a["conv_par"] = par.reshape(4, N_CONV, P).transpose(2, 1, 0)
    bias = np.zeros((P, 1), np.float32)
    for g, row in enumerate(GATE_ROWS):
        bias[row:row + HEADS, 0] = get["gate_b"][0, g * HEADS:(g + 1) * HEADS]
    a["gate_bias"] = bias

    def halves(m):
        return m.reshape(-1, P, 2, D // 2).transpose(2, 0, 1, 3)

    def pairs(m):
        return m.reshape(m.shape[0], 2, KF, P).transpose(0, 2, 1, 3).reshape(m.shape[0], -1)

    a["w_out_t"] = halves(get["w_out"][0])
    a["w_up_t"] = column_tiles(pairs(get["w_up"][0]))
    a["w_down_t"] = halves(get["w_down"][0])
    a["ffn_par"] = pairs(np.concatenate([get["ffn_conv_w"][0], get["ffn_conv_b"]], axis=0)).reshape(4, 2 * KF, P).transpose(2, 1, 0)
    a["ml_gain"] = get["ml_norm_g"].reshape(HEADS, HD).T
    a["filt_w1"], a["filt_w2"], a["filt_w3"] = get["filt_w1"][0], get["filt_w2"][0], get["filt_w3"][0]
    a["filt_bf"] = np.stack([get["filt_b1"][0], get["filt_freq1"][0], get["filt_b2"][0], get["filt_freq2"][0]], axis=1)
    a["hy_bias"] = get["hy_bias"][0]
    a["norm1_g"], a["norm2_g"], a["final_g"] = get["norm1_g"][0], get["norm2_g"][0], get["final_g"]
    a["positions"], a["neg_t"], a["rates"] = filter_tables()
    for s, (_, n) in enumerate(SEQS):
        a[f"fwd{s}"], a[f"inv{s}"] = transform_tables(n)
    a["identity"] = np.eye(P, dtype=np.float32)
    a["keep"] = np.ones((P, 1), np.float32)
    a["keep"][0, 0] = 0.0
    key, query = np.arange(P)[:, None], np.arange(P)[None, :]
    a["masks"] = np.stack([np.where(key > query, -1e30, 0.0), np.where(key < query, -1e30, 0.0)], axis=1).astype(np.float32)
    return {n: np.ascontiguousarray(v) for n, v in a.items()}


def kernel(**inputs):
    import concourse.bacc as bacc
    from concourse.bass_utils import run_bass_kernel_spmd

    nc = bacc.Bacc("TRN2", target_bir_lowering=False, num_devices=1)
    arrays = {f"arg_{n}": v for n, v in laid_out(inputs).items()}
    a = {n[4:]: nc.dram_tensor(n, v.shape, mybir.dt.from_np(v.dtype), kind="ExternalInput").ap()
         for n, v in arrays.items()}
    outs = [nc.dram_tensor(f"out_{s}", (1, n, D), F32, kind="ExternalOutput").ap() for s, (_, n) in enumerate(SEQS)]
    encoder(nc, a, *outs)
    r = run_bass_kernel_spmd(nc, [arrays], core_ids=[0])
    return tuple(r.results[0][f"out_{s}"] for s in range(len(SEQS)))
```

```python
import math
from contextlib import ExitStack

import numpy as np

import concourse.bass as bass
from concourse import mybir
from concourse.alu_op_type import AluOpType as ALU

F32, F32R = mybir.dt.float32, mybir.dt.float32r
ACT = mybir.ActivationFunctionType

P = 128
D = 1024
KD = D // P
SEQS = [(0, 1024), (1024, 512)]
T = sum(n for _, n in SEQS)
TT = T // P
CH = 512
NCH = T // CH
HY = 512
HEADS, HD = 4, 128
ORDER = 2
EMB, HID = 33, 64
FF = 2816
KF = FF // P
EPS = 1e-6
CLASSES = 4

N_QK, N_MIX, N_V, N_O = 2 * HEADS, 3 * HY // P, HEADS, HEADS
IN_KINDS = ["qk"] * N_QK + ["mix"] * N_MIX + ["v"] * N_V + ["o"] * N_O + ["gate"]
FIRST_MIX = N_QK
FIRST_V = FIRST_MIX + N_MIX
FIRST_O = FIRST_V + N_V
N_CONV = N_QK + N_MIX
GATE_ROWS = [0, 64, 32, 96]


def pipelined(eng, kinds, stages, first=0, tail=True):
    count, deepest = len(kinds), max(lag for lag, _ in stages) if tail else 0

    def kind_of(k):
        return kinds[k] if 0 <= k < count else None

    def signature(n):
        return [(kind_of(n - lag), kind_of(n - lag - 2)) for lag, _ in stages]

    def step(n0, n, i):
        for lag, body in stages:
            kind = kind_of(n - lag)
            if kind is not None:
                k0 = n - lag
                body(i * 2 + k0 if i is not None else k0, k0 % 2,
                     i + k0 // 2 if i is not None else k0 // 2, kind, kind_of(k0 - 2))

    n = first
    while n < count + deepest:
        run = 1
        while n + run < count + deepest and signature(n + run) == signature(n):
            run += 1
        if run >= 4:
            with eng.Fori(0, run // 2) as i:
                step(n, n, i)
                step(n, n + 1, i)
            n += run // 2 * 2
        else:
            step(n, n, None)
            n += 1


class Phase:

    lasting = None

    def __init__(self, nc, ctx, name):
        self.nc, self.ctx, self.name, self.sems = nc, ctx, name, []
        ctx.callback(self.clear)

    def sb(self, name, shape, dt=F32):
        return self.ctx.enter_context(self.nc.sbuf_tensor(f"{self.name}_{name}", shape, dt))

    def ps(self, name, shape, dt=F32):
        return self.ctx.enter_context(self.nc.psum_tensor(f"{self.name}_{name}", shape, dt))

    def sem(self, name):
        self.sems.append(self.ctx.enter_context(self.nc.semaphore(f"{self.name}_{name}")))
        return self.sems[-1]

    def pool_dma_sem(self, name):
        return Phase.lasting.enter_context(self.nc.semaphore(f"{self.name}_{name}"))

    def clear(self):
        if self.sems:
            nums = sorted(s.num for s in self.sems)
            starts = [n for n in nums if n - 1 not in nums]
            ends = [n + 1 for n in nums if n + 1 not in nums]
            with self.nc.Block() as block:
                @block.sync
                def _(sp):
                    for start, end in zip(starts, ends):
                        sp.sem_clear(range(start, end))


def three_pass(pe, out, w_hi, w_lo, x_hi, x_lo, first, last):
    pe.matmul(out, w_hi, x_hi, start=first, stop=False)
    pe.matmul(out, w_hi, x_lo, start=False, stop=False)
    return pe.matmul(out, w_lo, x_hi, start=False, stop=last)


def norm_transpose(nc, name, g, ident, ht_hi, ht_lo, x_dram=None, x_sb=None):
    with ExitStack() as ctx:
        p = Phase(nc, ctx, name)
        x_in = [p.sb(f"x_in{b}", [P, D]) for b in range(2)] if x_sb is None else None
        gain = p.sb("gain", [P, D])
        junk = p.sb("junk", [P, D])
        sumsq, root, rstd = (p.sb(n, [P, TT]) for n in ("sumsq", "root", "rstd"))
        eps, eps_set = p.sb("eps", [P, 1]), p.sem("eps_set")
        xn = [p.sb(f"xn{b}", [P, D]) for b in range(2)]
        bank = [p.ps(f"bank{n}", [P, 4, P]) for n in range(4)]
        x_loaded = [p.sem(f"x_loaded{b}") for b in range(2)]
        gain_loaded = p.sem("gain_loaded")
        squared, root_ready, rstd_ready = p.sem("squared"), p.sem("root_ready"), p.sem("rstd_ready")
        xn_ready, transposed = p.sem("xn_ready"), p.sem("transposed")
        hi_ready, lo_ready = p.sem("hi_ready"), p.sem("lo_ready")
        kinds = ["tile"] * TT

        def x_of(k, b):
            return x_in[b][:, :] if x_sb is None else x_sb[:, bass.ds(k, 1), :].rearrange("p a d -> p (a d)")

        with nc.Block() as block:
            @block.sync
            def _(sp):
                sp.dma_start(gain[:, :], g.rearrange("(a d) -> a d", a=1).broadcast_to([P, D])).then_inc(gain_loaded, 16)

                def load(k, b, turn, kind, before):
                    if before:
                        sp.wait_ge(xn_ready, k - 1)
                    sp.dma_start(x_in[b][:, :], x_dram[bass.ds(k, 1), :, :].rearrange("a p d -> (a p) d")
                                 ).then_inc(x_loaded[b], 16)
                if x_sb is None:
                    pipelined(sp, kinds, [(0, load)])

            @block.scalar
            def _(act):
                act.wait_ge(eps_set, 1)

                def square(k, b, turn, kind, before):
                    if x_sb is None:
                        act.wait_ge(x_loaded[b], (turn + 1) * 16)
                    act.activation(junk[:, :], x_of(k, b), ACT.Square,
                                   accum_out=sumsq[:, bass.ds(k, 1)]).then_inc(squared, 1)
                    act.wait_ge(squared, k + 1)
                    act.activation(root[:, bass.ds(k, 1)], sumsq[:, bass.ds(k, 1)], ACT.Sqrt, bias=eps[:, :],
                                   scale=1.0 / D).then_inc(root_ready, 1)

                def high(k, b, turn, kind, before):
                    for h in range(2):
                        act.wait_ge(transposed, k * 2 + h + 1)
                        act.activation(ht_hi[:, 4 * h:4 * h + 4, bass.ds(k * P, P)], bank[2 * b + h][:, :, :],
                                       ACT.Copy).then_inc(hi_ready, 1)
                pipelined(act, kinds, [(0, square), (1, high)])

            @block.vector
            def _(dve):
                dve.memset(eps[:, :], EPS).then_inc(eps_set, 1)
                dve.wait_ge(gain_loaded, 16)

                def scale(k, b, turn, kind, before):
                    dve.wait_ge(root_ready, k + 1)
                    dve.reciprocal(rstd[:, bass.ds(k, 1)], root[:, bass.ds(k, 1)]).then_inc(rstd_ready, 1)
                    if before:
                        dve.wait_ge(transposed, k * 2 - 2)
                    dve.wait_ge(rstd_ready, k + 1)
                    dve.scalar_tensor_tensor(xn[b][:, :], x_of(k, b), rstd[:, bass.ds(k, 1)], gain[:, :],
                                             ALU.mult, ALU.mult).then_inc(xn_ready, 1)

                def low(k, b, turn, kind, before):
                    for h in range(2):
                        dve.wait_ge(hi_ready, k * 2 + h + 1)
                        dve.tensor_tensor(ht_lo[:, 4 * h:4 * h + 4, bass.ds(k * P, P)], bank[2 * b + h][:, :, :],
                                          ht_hi[:, 4 * h:4 * h + 4, bass.ds(k * P, P)].bitcast(F32),
                                          ALU.subtract).then_inc(lo_ready, 1)
                pipelined(dve, kinds, [(0, scale), (1, low)])

            @block.tensor
            def _(pe):
                def turn_tiles(k, b, turn, kind, before):
                    pe.wait_ge(xn_ready, k + 1)
                    for h in range(2):
                        if before:
                            pe.wait_ge(lo_ready, k * 2 + h - 3)
                        for q in range(4):
                            c = 4 * h + q
                            last = pe.transpose(bank[2 * b + h][:, q, :], xn[b][:, c * P:(c + 1) * P], ident[:, :])
                        last.then_inc(transposed, 1)
                pipelined(pe, kinds, [(0, turn_tiles)])



def split_weights(p, w_tiles, kinds, width=D):
    raw = [p.sb(f"w_raw{b}", [P, KD, P]) for b in range(2)]
    hi = [p.sb(f"w_hi{b}", [P, KD, P], F32R) for b in range(2)]
    lo = [p.sb(f"w_lo{b}", [P, KD, P], F32R) for b in range(2)]
    return raw, hi, lo


def channel_major_product(pe, out, w_hi, w_lo, ht_hi, ht_lo):
    for kt in range(KD):
        for c in range(NCH):
            last = three_pass(pe, out[:, c * CH:(c + 1) * CH], w_hi[:, kt, :], w_lo[:, kt, :],
                              ht_hi[:, kt, c * CH:(c + 1) * CH], ht_lo[:, kt, c * CH:(c + 1) * CH],
                              kt == 0, kt == KD - 1)
    return last


def add_neighbours(dve, u, acc, w_prev, w_next, half_step, done, k):
    for t0, n in SEQS:
        dve.scalar_tensor_tensor(u[:, t0 + 1:t0 + n], acc[:, t0:t0 + n - 1], w_prev, u[:, t0 + 1:t0 + n],
                                 ALU.mult, ALU.add).then_inc(half_step, 1)
    for s, (t0, n) in enumerate(SEQS):
        dve.wait_ge(half_step, k * 2 + s + 1)
        last = dve.scalar_tensor_tensor(u[:, t0:t0 + n - 1], acc[:, t0 + 1:t0 + n], w_next, u[:, t0:t0 + n - 1],
                                        ALU.mult, ALU.add)
    last.then_inc(done, 1)


def input_projection(nc, w_tiles, conv_par, gate_bias, ident, ht_hi, ht_lo, qk_d, tok_d, o_d, gates_d):
    with ExitStack() as ctx:
        p = Phase(nc, ctx, "in")
        raw, w_hi, w_lo = split_weights(p, w_tiles, IN_KINDS)
        cp = p.sb("conv_par", [P, N_CONV, 4])
        gb = p.sb("gate_bias", [P, 1])
        u = [p.sb(f"u{b}", [P, T]) for b in range(2)]
        out = [p.sb(f"out{b}", [P, TT, P]) for b in range(2)]
        acc = [p.ps(f"acc{b}", [P, T]) for b in range(2)]
        tbank = [p.ps(f"tbank{b}", [P, 4, P]) for b in range(2)]
        par_loaded = p.sem("par_loaded")
        raw_loaded = [p.sem(f"raw_loaded{b}") for b in range(2)]
        stored = [p.pool_dma_sem(f"stored{b}") for b in range(2)]
        hi_ready, lo_ready, multiplied = p.sem("hi_ready"), p.sem("lo_ready"), p.sem("multiplied")
        centred, half_step, u_ready = p.sem("centred"), p.sem("half_step"), p.sem("u_ready")
        transposed, t_copied, activated = p.sem("transposed"), p.sem("t_copied"), p.sem("activated")

        def u_free(eng, k, before):
            if before in ("mix", "v"):
                eng.wait_ge(transposed, (k - 2 - FIRST_MIX) * 3 + 3)
            elif before == "qk":
                eng.wait_ge(activated, k - 1)
            elif before:
                eng.wait_ge(activated, k - 1 - (FIRST_O - N_QK))

        with nc.Block() as block:
            @block.sync
            def _(sp):
                sp.dma_start(cp[:, :, :], conv_par).then_inc(par_loaded, 16)
                sp.dma_start(gb[:, :], gate_bias).then_inc(par_loaded, 16)

                def load(k, b, turn, kind, before):
                    if before:
                        sp.wait_ge(lo_ready, k - 1)
                    sp.dma_start(raw[b][:, :, :], w_tiles[bass.ds(k, 1), :, :, :].rearrange("a p k c -> (a p) k c")
                                 ).then_inc(raw_loaded[b], 16)
                pipelined(sp, ["w"] * len(IN_KINDS), [(0, load)])

            @block.scalar
            def _(act):
                act.wait_ge(par_loaded, 32)

                def high(k, b, turn, kind, before):
                    act.wait_ge(raw_loaded[b], (turn + 1) * 16)
                    if before:
                        act.wait_ge(multiplied, k - 1)
                    act.activation(w_hi[b][:, :, :], raw[b][:, :, :], ACT.Copy).then_inc(hi_ready, 1)

                def finish(k, b, turn, kind, before):
                    if before:
                        act.wait_ge(stored[b], turn * 16)
                    if kind in ("mix", "v"):
                        for g in range(3):
                            act.wait_ge(transposed, (k - FIRST_MIX) * 3 + g + 1)
                            act.activation(out[b][:, 4 * g:4 * g + 4, :], tbank[(b + g) % 2][:, :, :],
                                           ACT.Copy).then_inc(t_copied, 1)
                    else:
                        act.wait_ge(u_ready, k + 1)
                        func = {"qk": ACT.Silu, "o": ACT.Sigmoid, "gate": ACT.Copy}[kind]
                        act.activation(out[b][:, :, :].rearrange("p a b -> p (a b)"), u[b][:, :],
                                       func).then_inc(activated, 1)

                def centre(k, b, turn, kind, before):
                    if kind in ("qk", "mix"):
                        act.wait_ge(multiplied, k + 1)
                        u_free(act, k, before)
                        act.activation(u[b][:, :], acc[b][:, :], ACT.Identity,
                                       bias=cp[:, bass.ds(k, 1), 3:4].rearrange("p a b -> p (a b)"),
                                       scale=cp[:, bass.ds(k, 1), 1:2].rearrange("p a b -> p (a b)")
                                       ).then_inc(centred, 1)
                pipelined(act, IN_KINDS, [(0, high), (2, finish), (1, centre)])

            @block.vector
            def _(dve):
                dve.wait_ge(par_loaded, 32)

                def low(k, b, turn, kind, before):
                    dve.wait_ge(hi_ready, k + 1)
                    dve.tensor_tensor(w_lo[b][:, :, :], raw[b][:, :, :], w_hi[b][:, :, :].bitcast(F32),
                                      ALU.subtract).then_inc(lo_ready, 1)

                def gather(k, b, turn, kind, before):
                    if kind in ("qk", "mix"):
                        dve.wait_ge(centred, k + 1)
                        add_neighbours(dve, u[b], acc[b],
                                       cp[:, bass.ds(k, 1), 0:1].rearrange("p a b -> p (a b)"),
                                       cp[:, bass.ds(k, 1), 2:3].rearrange("p a b -> p (a b)"),
                                       half_step, u_ready, k)
                    else:
                        dve.wait_ge(multiplied, k + 1)
                        u_free(dve, k, before)
                        if kind == "gate":
                            dve.tensor_scalar(u[b][:, :], acc[b][:, :], gb[:, :], None, ALU.add).then_inc(u_ready, 1)
                        else:
                            dve.tensor_copy(u[b][:, :], acc[b][:, :]).then_inc(u_ready, 1)
                pipelined(dve, IN_KINDS, [(0, low), (1, gather)])

            @block.tensor
            def _(pe):
                def product(k, b, turn, kind, before):
                    pe.wait_ge(lo_ready, k + 1)
                    if before:
                        pe.wait_ge(u_ready, k - 1)
                    channel_major_product(pe, acc[b], w_hi[b], w_lo[b], ht_hi, ht_lo).then_inc(multiplied, 1)

                def turn_tiles(k, b, turn, kind, before):
                    if kind not in ("mix", "v"):
                        return
                    pe.wait_ge(u_ready, k + 1)
                    for g in range(3):
                        n = (k - FIRST_MIX) * 3 + g
                        if not isinstance(n, int) or n >= 2:
                            pe.wait_ge(t_copied, n - 1)
                        for q in range(4):
                            t = 4 * g + q
                            last = pe.transpose(tbank[(b + g) % 2][:, q, :], u[b][:, t * P:(t + 1) * P], ident[:, :])
                        last.then_inc(transposed, 1)
                pipelined(pe, IN_KINDS, [(0, product), (1, turn_tiles)])

            @block.gpsimd
            def _(pool):
                def store(k, b, turn, kind, before):
                    if kind in ("mix", "v"):
                        pool.wait_ge(t_copied, (k - FIRST_MIX) * 3 + 3)
                        pool.dma_start(tok_d[:, :, bass.ds((k - FIRST_MIX) * P, P)].rearrange("t p c -> p t c"),
                                       out[b][:, :, :]).then_inc(stored[b], 16)
                        return
                    first, dst = {"qk": (0, qk_d), "o": (FIRST_O, o_d), "gate": (FIRST_O + N_O, gates_d)}[kind]
                    pool.wait_ge(activated, k + 1 - (0 if kind == "qk" else FIRST_O - N_QK))
                    pool.dma_start(dst[bass.ds(k - first, 1), :, :].rearrange("a p t -> (a p) t"),
                                   out[b][:, :, :].rearrange("p a b -> p (a b)")).then_inc(stored[b], 16)
                pipelined(pool, IN_KINDS, [(0, store)])
                n = len(IN_KINDS)
                pool.wait_ge(stored[0], 16 * ((n + 1) // 2))
                pool.wait_ge(stored[1], 16 * (n // 2))


def gated_up_projection(nc, w_tiles, conv_par, ht_hi, ht_lo, g_d):
    kinds = ["ff"] * (2 * KF)
    with ExitStack() as ctx:
        p = Phase(nc, ctx, "up")
        raw, w_hi, w_lo = split_weights(p, w_tiles, kinds)
        cp = p.sb("conv_par", [P, 2 * KF, 4])
        u = [p.sb(f"u{b}", [P, T]) for b in range(2)]
        sg = p.sb("silu_gate", [P, T])
        prod = p.sb("prod", [P, T])
        acc = [p.ps(f"acc{b}", [P, T]) for b in range(2)]
        par_loaded, stored = p.sem("par_loaded"), p.pool_dma_sem("stored")
        raw_loaded = [p.sem(f"raw_loaded{b}") for b in range(2)]
        hi_ready, lo_ready, multiplied = p.sem("hi_ready"), p.sem("lo_ready"), p.sem("multiplied")
        centred, half_step, u_ready = p.sem("centred"), p.sem("half_step"), p.sem("u_ready")
        gate_ready, gated = p.sem("gate_ready"), p.sem("gated")

        with nc.Block() as block:
            @block.sync
            def _(sp):
                sp.dma_start(cp[:, :, :], conv_par).then_inc(par_loaded, 16)

                def load(k, b, turn, kind, before):
                    if before:
                        sp.wait_ge(lo_ready, k - 1)
                    sp.dma_start(raw[b][:, :, :], w_tiles[bass.ds(k, 1), :, :, :].rearrange("a p k c -> (a p) k c")
                                 ).then_inc(raw_loaded[b], 16)
                pipelined(sp, kinds, [(0, load)])

            @block.scalar
            def _(act):
                act.wait_ge(par_loaded, 16)

                def high(k, b, turn, kind, before):
                    act.wait_ge(raw_loaded[b], (turn + 1) * 16)
                    if before:
                        act.wait_ge(multiplied, k - 1)
                    act.activation(w_hi[b][:, :, :], raw[b][:, :, :], ACT.Copy).then_inc(hi_ready, 1)

                def silu(k, b, turn, kind, before):
                    if b == 1:
                        act.wait_ge(u_ready, k + 1)
                        if before:
                            act.wait_ge(gated, turn)
                        act.activation(sg[:, :], u[1][:, :], ACT.Silu).then_inc(gate_ready, 1)

                def centre(k, b, turn, kind, before):
                    act.wait_ge(multiplied, k + 1)
                    if before:
                        act.wait_ge(gated, turn)
                    act.activation(u[b][:, :], acc[b][:, :], ACT.Identity,
                                   bias=cp[:, bass.ds(k, 1), 3:4].rearrange("p a b -> p (a b)"),
                                   scale=cp[:, bass.ds(k, 1), 1:2].rearrange("p a b -> p (a b)")
                                   ).then_inc(centred, 1)
                pipelined(act, kinds, [(0, high), (2, silu), (1, centre)])

            @block.vector
            def _(dve):
                dve.wait_ge(par_loaded, 16)

                def low(k, b, turn, kind, before):
                    dve.wait_ge(hi_ready, k + 1)
                    dve.tensor_tensor(w_lo[b][:, :, :], raw[b][:, :, :], w_hi[b][:, :, :].bitcast(F32),
                                      ALU.subtract).then_inc(lo_ready, 1)

                def gate(k, b, turn, kind, before):
                    if b == 1:
                        dve.wait_ge(gate_ready, turn + 1)
                        if before:
                            dve.wait_ge(stored, turn * 16)
                        dve.tensor_tensor(prod[:, :], sg[:, :], u[0][:, :], ALU.mult).then_inc(gated, 1)

                def gather(k, b, turn, kind, before):
                    dve.wait_ge(centred, k + 1)
                    add_neighbours(dve, u[b], acc[b],
                                   cp[:, bass.ds(k, 1), 0:1].rearrange("p a b -> p (a b)"),
                                   cp[:, bass.ds(k, 1), 2:3].rearrange("p a b -> p (a b)"),
                                   half_step, u_ready, k)
                pipelined(dve, kinds, [(0, low), (2, gate), (1, gather)])

            @block.tensor
            def _(pe):
                def product(k, b, turn, kind, before):
                    pe.wait_ge(lo_ready, k + 1)
                    if before:
                        pe.wait_ge(u_ready, k - 1)
                    channel_major_product(pe, acc[b], w_hi[b], w_lo[b], ht_hi, ht_lo).then_inc(multiplied, 1)
                pipelined(pe, kinds, [(0, product)])

            @block.gpsimd
            def _(pool):
                with pool.Fori(0, KF) as i:
                    pool.wait_ge(gated, i + 1)
                    pool.dma_start(g_d[bass.ds(i, 1), :, :].rearrange("a p t -> (a p) t"), prod[:, :]).then_inc(stored, 16)
                pool.wait_ge(stored, 16 * KF)


def token_major_projection(nc, name, kt_count, w_halves, src_d, x_sb, x_dram=None, final=None):
    half = D // 2
    with ExitStack() as ctx:
        p = Phase(nc, ctx, name)
        w_raw = [p.sb(f"w_raw{b}", [P, 2, half]) for b in range(2)]
        w_hi, w_lo = (p.sb(n, [P, kt_count, half], F32R) for n in ("w_hi", "w_lo"))
        s_raw = p.sb("s_raw", [P, kt_count, P])
        s_hi, s_lo = ([p.sb(f"{n}{b}", [P, kt_count, P], F32R) for b in range(2)] for n in ("s_hi", "s_lo"))
        acc = [p.ps(f"acc{b}", [P, half]) for b in range(2)]
        s_loaded = p.sem("s_loaded")
        x_loaded = [p.sem(f"x_loaded{h}") for h in range(2)]
        w_loaded = [p.sem(f"w_loaded{b}") for b in range(2)]
        w_hi_ready, w_lo_ready, w_used = p.sem("w_hi_ready"), p.sem("w_lo_ready"), p.sem("w_used")
        s_hi_ready, s_lo_ready = p.sem("s_hi_ready"), p.sem("s_lo_ready")
        multiplied, added = p.sem("multiplied"), p.sem("added")
        if final:
            gain, y = p.sb("gain", [P, D]), p.sb("y", [P, D])
            sumsq, root, rstd = (p.sb(n, [P, TT]) for n in ("sumsq", "root", "rstd"))
            eps = p.sb("eps", [P, 1])
            eps_set, gain_loaded, squared, root_ready = (p.sem(n) for n in ("eps_set", "gain_loaded", "squared", "root_ready"))
            rstd_ready, y_ready, stored = p.sem("rstd_ready"), p.sem("y_ready"), p.pool_dma_sem("stored")
        pairs = kt_count // 2
        w_kinds = ["w"] * (pairs - 1) + ["last"]
        uses = [(pairs + 1) // 2, pairs // 2]
        n_prompt = SEQS[0][1] // P
        t_kinds = ["first"] + ["prompt"] * (n_prompt - 1) + ["sample"] * (TT - n_prompt - 1) + ["last"]

        def row(k):
            return x_sb[:, bass.ds(k, 1), :].rearrange("p a d -> p (a d)")

        with nc.Block() as block:
            @block.sync
            def _(sp):
                def load_s(h, k, b, turn, kind, before):
                    if h or kind != "first":
                        sp.wait_ge(s_lo_ready, k + h * TT)
                    sp.dma_start(s_raw[:, :, :], src_d[:, :, bass.ds(k * P, P)].rearrange("k p t -> p k t")
                                 ).then_inc(s_loaded, 16)

                if final:
                    sp.dma_start(gain[:, :], final[0].rearrange("(a d) -> a d", a=1).broadcast_to([P, D])).then_inc(gain_loaded, 16)
                for h in range(2):
                    def load_w(k, b, turn, kind, before):
                        if before:
                            sp.wait_ge(w_lo_ready, k - 1 + h * pairs)
                        elif h:
                            sp.wait_ge(w_lo_ready, pairs)
                        sp.dma_start(w_raw[b][:, :, :], w_halves[h, bass.ds(k, 1), :, :, :].rearrange("a p q c -> (a p) q c")
                                     ).then_inc(w_loaded[b], 16)
                    load_s(h, 0, 0, 0, "first", None)
                    pipelined(sp, w_kinds, [(0, load_w)])
                    if x_dram is not None:
                        sp.dma_start(x_sb[:, :, h * half:(h + 1) * half], x_dram[:, :, h * half:(h + 1) * half].rearrange(
                            "t p d -> p t d")).then_inc(x_loaded[h], 16)
                    pipelined(sp, t_kinds, [(0, lambda *at: load_s(h, *at))], first=1)

            @block.scalar
            def _(act):
                def high_s(h, k, b, turn, kind, before):
                    act.wait_ge(s_loaded, (k + 1 + h * TT) * 16)
                    if h or before:
                        act.wait_ge(multiplied, k - 1 + h * TT)
                    act.activation(s_hi[b][:, :, :], s_raw[:, :, :], ACT.Copy).then_inc(s_hi_ready, 1)

                def square(k, b, turn, kind, before):
                    act.wait_ge(added, TT + k + 1)
                    if kind != "first":
                        act.wait_ge(stored, k * 16)
                    act.activation(y[:, :], row(k), ACT.Square, accum_out=sumsq[:, bass.ds(k, 1)]).then_inc(squared, 1)
                    act.wait_ge(squared, k + 1)
                    act.activation(root[:, bass.ds(k, 1)], sumsq[:, bass.ds(k, 1)], ACT.Sqrt, bias=eps[:, :],
                                   scale=1.0 / D).then_inc(root_ready, 1)

                if final:
                    act.wait_ge(eps_set, 1)
                for h in range(2):
                    def high_w(k, b, turn, kind, before):
                        act.wait_ge(w_loaded[b], (turn + 1) * 16 + h * uses[b] * 16)
                        if h and kind == "last":
                            act.wait_ge(multiplied, TT)
                        elif h:
                            act.wait_ge(w_used, k * 2 + 2)
                        act.activation(w_hi[:, bass.ds(k * 2, 2), :], w_raw[b][:, :, :],
                                       ACT.Copy).then_inc(w_hi_ready, 1)
                    high_s(h, 0, 0, 0, "first", None)
                    pipelined(act, w_kinds, [(0, high_w)])
                    stages = [(0, lambda *at: high_s(h, *at))]
                    if final and h:
                        stages.append((2, square))
                    pipelined(act, t_kinds, stages, first=1)

            @block.vector
            def _(dve):
                def low_s(h, k, b, turn, kind, before):
                    dve.wait_ge(s_hi_ready, k + 1 + h * TT)
                    dve.tensor_tensor(s_lo[b][:, :, :], s_raw[:, :, :], s_hi[b][:, :, :].bitcast(F32),
                                      ALU.subtract).then_inc(s_lo_ready, 1)

                def accumulate(h, k, b, turn, kind, before):
                    dve.wait_ge(multiplied, k + 1 + h * TT)
                    if x_dram is not None and kind == "first":
                        dve.wait_ge(x_loaded[h], 16)
                    x = x_sb[:, bass.ds(k, 1), h * half:(h + 1) * half].rearrange("p a c -> p (a c)")
                    dve.tensor_tensor(x, acc[b][:, :], x, ALU.add).then_inc(added, 1)

                def scale(k, b, turn, kind, before):
                    dve.wait_ge(root_ready, k + 1)
                    dve.reciprocal(rstd[:, bass.ds(k, 1)], root[:, bass.ds(k, 1)]).then_inc(rstd_ready, 1)
                    dve.wait_ge(rstd_ready, k + 1)
                    dve.scalar_tensor_tensor(y[:, :], row(k), rstd[:, bass.ds(k, 1)], gain[:, :],
                                             ALU.mult, ALU.mult).then_inc(y_ready, 1)

                if final:
                    dve.memset(eps[:, :], EPS).then_inc(eps_set, 1)
                    dve.wait_ge(gain_loaded, 16)
                for h in range(2):
                    def low_w(k, b, turn, kind, before):
                        dve.wait_ge(w_hi_ready, k + 1 + h * pairs)
                        dve.tensor_tensor(w_lo[:, bass.ds(k * 2, 2), :], w_raw[b][:, :, :],
                                          w_hi[:, bass.ds(k * 2, 2), :].bitcast(F32), ALU.subtract).then_inc(w_lo_ready, 1)
                    low_s(h, 0, 0, 0, "first", None)
                    pipelined(dve, w_kinds, [(0, low_w)])
                    if h:
                        accumulate(0, TT - 1, (TT - 1) % 2, None, "last", None)
                    stages = [(0, lambda *at: low_s(h, *at)), (1, lambda *at: accumulate(h, *at))]
                    if final and h:
                        stages.append((2, scale))
                    pipelined(dve, t_kinds, stages, first=1, tail=h == 1)

            @block.tensor
            def _(pe):
                for h in range(2):
                    def product(k, b, turn, kind, before):
                        pe.wait_ge(s_lo_ready, k + 1 + h * TT)
                        if h or before:
                            pe.wait_ge(added, k - 1 + h * TT)
                        for kt in range(kt_count):
                            if kind == "first" and kt % 2 == 0:
                                pe.wait_ge(w_lo_ready, h * pairs + kt // 2 + 1)
                            last = three_pass(pe, acc[b][:, :], s_hi[b][:, kt, :], s_lo[b][:, kt, :],
                                              w_hi[:, kt, :], w_lo[:, kt, :], kt == 0, kt == kt_count - 1)
                            if kind == "last" and h == 0 and kt < kt_count - 1:
                                last.then_inc(w_used, 1)
                        last.then_inc(multiplied, 1)
                    pipelined(pe, t_kinds, [(0, product)])

            if final:
                @block.gpsimd
                def _(pool):
                    def store(k, b, turn, kind, before):
                        pool.wait_ge(y_ready, k + 1)
                        prompt = kind in ("first", "prompt")
                        dst = final[1][0 if prompt else 1]
                        pool.dma_start(dst[0, bass.ds(k * P - (0 if prompt else SEQS[1][0]), P), :], y[:, :]
                                       ).then_inc(stored, 16)
                    pipelined(pool, t_kinds, [(0, store)])
                    pool.wait_ge(stored, 16 * TT)


C1, S1, RH = math.cos(math.pi / 8), math.sin(math.pi / 8), math.sqrt(0.5)


def transform_tables(n):
    b = n // 4
    m = np.arange(b)[:, None]
    fwd = np.zeros((CLASSES, P, 3, b // P, b // P, P), np.float32)
    inv = np.zeros((CLASSES, P, 3, b // P, b // P, P), np.float32)
    for c in range(CLASSES):
        k = c + 8 * np.arange(b)[None, :]
        phase = 2 * np.pi * ((m * (2 * k + 1)) % (4 * n)) / (4 * n)
        for j, a in enumerate((np.cos(phase), np.sin(phase), -np.sin(phase))):
            fwd[c, :, j] = a.reshape(b // P, P, b // P, P).transpose(1, 0, 2, 3)
            inv[c, :, j] = a.T.reshape(b // P, P, b // P, P).transpose(1, 0, 2, 3)
    return fwd, inv


def filter_tables():
    zs, ts = [], []
    for _, n in SEQS:
        t = np.linspace(0.0, 1.0, n, dtype=np.float32)[:, None]
        bands = (EMB - 1) // 2
        freqs = np.linspace(1e-4, bands - 1, bands, dtype=np.float32)
        ang = np.float32(2.0 * math.pi / n) * np.arange(n, dtype=np.float32)[:, None] * freqs[None, :]
        zs.append(np.concatenate([t, np.cos(ang), -np.sin(ang)], axis=-1).astype(np.float32))
        ts.append(-t[:, 0])
    lo, hi = math.log(1e-2) / 1.5, math.log(1e-2) / 0.3
    rates = np.abs(np.linspace(lo, hi, HY, dtype=np.float32))
    return (np.ascontiguousarray(np.concatenate(zs).T), np.ascontiguousarray(np.concatenate(ts).reshape(TT, P).T),
            np.ascontiguousarray(np.broadcast_to(rates, (P, HY))))


class Chain:

    def __init__(self, eng, sem):
        self.eng, self.sem, self.count = eng, sem, 0

    def __call__(self, ins):
        ins.then_inc(self.sem, 1)
        self.count += 1
        return self.count

    def need(self, count):
        self.eng.wait_ge(self.sem, count)


def radix_stage(dve, ch, x, cr, sn, tmp):
    r, t1, t2, u, v, pp, qq, ps_, qs = (tmp(j) for j in range(9))
    n_r = ch(dve.tensor_scalar(r, x(2), RH, None, ALU.mult))
    n_1 = ch(dve.tensor_scalar(t1, x(1), C1, None, ALU.mult))
    n_2 = ch(dve.tensor_scalar(t2, x(1), S1, None, ALU.mult))
    ch.need(n_r)
    ch(dve.tensor_tensor(u, x(0), r, ALU.add))
    ch(dve.tensor_tensor(v, x(0), r, ALU.subtract))
    ch.need(n_1)
    ch(dve.scalar_tensor_tensor(pp, x(3), S1, t1, ALU.mult, ALU.add))
    ch(dve.scalar_tensor_tensor(qs, x(3), -S1, t1, ALU.mult, ALU.add))
    ch.need(n_2)
    ch(dve.scalar_tensor_tensor(qq, x(3), -C1, t2, ALU.mult, ALU.add))
    n_p = ch(dve.scalar_tensor_tensor(ps_, x(3), C1, t2, ALU.mult, ALU.add))
    ch.need(n_p)
    for c, a, b, sign in ((0, u, pp, ALU.add), (3, u, pp, ALU.subtract), (1, v, qq, ALU.add), (2, v, qq, ALU.subtract)):
        ch(dve.tensor_tensor(cr(c), a, b, sign))
    for c, a, sign in ((0, ps_, ALU.add), (3, ps_, ALU.subtract), (1, qs, ALU.add), (2, qs, ALU.subtract)):
        last = dve.tensor_tensor(sn(c), a, r, sign)
    return last


def hyena_hidden(nc, par, w1, z_t, h2_d):
    magic, two_pi_hi, two_pi_lo = 1.5 * 2.0 ** 23, 6.28125, 2 * math.pi - 6.28125
    limit = 3.1415925
    with ExitStack() as ctx:
        p = Phase(nc, ctx, "hid")
        z = p.sb("z", [EMB, T])
        w1_sb = p.sb("w1", [EMB, HID])
        w2_sb = p.sb("w2", [HID, HID])
        bf = p.sb("bf", [HID, 4])
        x, n, h = p.sb("x", [HID, T]), p.sb("n", [HID, T]), p.sb("h", [HID, T])
        acc = p.ps("acc", [HID, T])
        loaded, multiplied, step, sined, stored = (p.sem(s) for s in ("loaded", "multiplied", "step", "sined", "stored"))
        with nc.Block() as block:
            @block.sync
            def _(sp):
                sp.dma_start(z[:, :], z_t).then_inc(loaded, 16)
                sp.dma_start(w1_sb[:, :], w1).then_inc(loaded, 16)
                sp.dma_start(w2_sb[:, :], par["filt_w2"]).then_inc(loaded, 16)
                sp.dma_start(bf[:, :], par["filt_bf"]).then_inc(loaded, 16)
                sp.wait_ge(sined, 2)
                sp.dma_start(h2_d, h[:, :]).then_inc(stored, 16)
                sp.wait_ge(stored, 16)

            @block.tensor
            def _(pe):
                pe.wait_ge(loaded, 64)
                for layer, (w, src) in enumerate(((w1_sb, z), (w2_sb, h))):
                    if layer:
                        pe.wait_ge(sined, 1)
                    for c in range(NCH):
                        last = pe.matmul(acc[:, c * CH:(c + 1) * CH], w[:, :], src[:, c * CH:(c + 1) * CH],
                                         start=True, stop=True)
                    last.then_inc(multiplied, 1)

            @block.vector
            def _(dve):
                ch = Chain(dve, step)
                dve.wait_ge(loaded, 64)
                for layer in range(2):
                    dve.wait_ge(multiplied, layer + 1)
                    if layer:
                        dve.wait_ge(sined, 1)
                    ch.need(ch(dve.tensor_scalar(x[:, :], acc[:, :], bf[:, 2 * layer:2 * layer + 1],
                                                 bf[:, 2 * layer + 1:2 * layer + 2], ALU.add, ALU.mult)))
                    ch.need(ch(dve.tensor_scalar(n[:, :], x[:, :], 1 / (2 * math.pi), magic, ALU.mult, ALU.add)))
                    ch.need(ch(dve.tensor_scalar(n[:, :], n[:, :], -magic, None, ALU.add)))
                    ch.need(ch(dve.scalar_tensor_tensor(x[:, :], n[:, :], -two_pi_hi, x[:, :], ALU.mult, ALU.add)))
                    ch.need(ch(dve.scalar_tensor_tensor(x[:, :], n[:, :], -two_pi_lo, x[:, :], ALU.mult, ALU.add)))
                    ch.need(ch(dve.tensor_scalar(x[:, :], x[:, :], limit, -limit, ALU.min, ALU.max)))

            @block.scalar
            def _(act):
                for layer in range(2):
                    act.wait_ge(step, 6 * (layer + 1))
                    if layer:
                        act.wait_ge(multiplied, 2)
                    act.activation(h[:, :], x[:, :], ACT.Sin).then_inc(sined, 1)


HC = HY // 2


def hyena_filters(nc, tables, neg_t, rates, par, h2_d, k_d, power_d):
    groups = [(s, o) for s in range(len(SEQS)) for o in range(ORDER)]
    nts = [n // P for _, n in SEQS]
    sns = [n // 512 for _, n in SEQS]
    tiles_before = [sum(nts[s] for s, _ in groups[:g]) for g in range(len(groups) + 1)]
    jobs = [(g, ri, half) for g in range(len(groups)) for ri in range(2) for half in range(2)]
    per_group = 4
    with ExitStack() as ctx:
        p = Phase(nc, ctx, "filt")
        h2, w3 = p.sb("h2", [HID, T]), p.sb("w3", [HID, 2, ORDER, HY])
        nt_sb, rate = p.sb("neg_t", [P, TT]), p.sb("rates", [P, HY])
        keep, ones = p.sb("keep", [P, 1]), p.sb("ones", [P, P])
        decay = [p.sb(f"decay{b}", [P, HY]) for b in range(2)]
        taps = [p.sb(f"taps{b}", [P, 2, HY]) for b in range(2)]
        squares = p.sb("squares", [P, 2, HY])
        power = [p.sb(f"power{b}", [P, 2, HY]) for b in range(2)]
        both = [[p.sb(f"both{ri}_{b}", [P, max(nts), HY]) for b in range(2)] for ri in range(2)]
        cr, sn = ([p.sb(f"{x}{b}", [P, CLASSES, max(sns), HC]) for b in range(2)] for x in ("cr", "sn"))
        tmp = p.sb("tmp", [P, 9, max(sns) * HC])
        tabs = [p.sb(f"tab{s}", [P, CLASSES, 3, sns[s], sns[s], P]) for s in range(len(SEQS))]
        kout = [p.sb(f"kout{b}", [P, CLASSES, max(sns), HC]) for b in range(2)]
        pout = [p.sb(f"pout{b}", [P, HY]) for b in range(2)]
        tap_acc = p.ps("tap_acc", [P, 2, HY])
        sum_acc = p.ps("sum_acc", [P, HY])
        kacc = [p.ps(f"kacc{b}", [P, max(sns), HC]) for b in range(4)]
        loaded, const_set = p.sem("loaded"), p.sem("const_set")
        tab_loaded = [p.sem(f"tab_loaded{s}") for s in range(len(SEQS))]
        taps_ready, decay_ready, decayed = p.sem("taps_ready"), p.sem("decay_ready"), p.sem("decayed")
        squared, combined, added, summed = p.sem("squared"), p.sem("combined"), p.sem("added"), p.sem("summed")
        step, staged, k_ready, k_copied = p.sem("step"), p.sem("staged"), p.sem("k_ready"), p.sem("k_copied")
        power_ready, power_stored = p.sem("power_ready"), p.sem("power_stored")
        k_stored = [p.sem(f"k_stored{b}") for b in range(2)]

        def taps_during(j):
            g, i = jobs[j][0] + 1, j % per_group
            nt = nts[groups[g][0]] if g < len(groups) else 0
            return range(nt * i // per_group, nt * (i + 1) // per_group)

        with nc.Block() as block:
            @block.sync
            def _(sp):
                sp.dma_start(h2[:, :], h2_d).then_inc(loaded, 16)
                sp.dma_start(w3[:, :, :, :], par["filt_w3"].rearrange("h (d o c) -> h d o c", d=2, o=ORDER)).then_inc(loaded, 16)
                sp.dma_start(nt_sb[:, :], neg_t).then_inc(loaded, 16)
                sp.dma_start(rate[:, :], rates).then_inc(loaded, 16)
                sp.dma_start(keep[:, :], par["keep"]).then_inc(loaded, 16)
                for s in range(len(SEQS)):
                    sp.dma_start(tabs[s][:, :, :, :, :, :], tables[s].rearrange("c p j s k q -> p c j s k q")
                                 ).then_inc(tab_loaded[s], 16)
                for j, (g, ri, half) in enumerate(jobs):
                    s, o = groups[g]
                    sp.wait_ge(k_copied, (j + 1) * CLASSES)
                    sp.dma_start(k_d[s][o, half, :, ri, :, :, :], kout[j % 2][:, :, 0:sns[s], :]).then_inc(k_stored[j % 2], 16)
                    if j % per_group == 0:
                        sp.wait_ge(power_ready, g + 1)
                        sp.dma_start(power_d[s, o], pout[g % 2][:, :]).then_inc(power_stored, 16)
                sp.wait_ge(power_stored, 16 * len(groups))
                for b in range(2):
                    sp.wait_ge(k_stored[b], 16 * (len(jobs) // 2))

            @block.tensor
            def _(pe):
                def tap_products(g, tiles):
                    s, o = groups[g]
                    t0 = SEQS[s][0]
                    for tt in tiles:
                        m = tiles_before[g] + tt
                        if m:
                            pe.wait_ge(decayed, m)
                        for d in range(2):
                            last = pe.matmul(tap_acc[:, d, :], h2[:, t0 + tt * P:t0 + (tt + 1) * P], w3[:, d, o, :],
                                             start=True, stop=True)
                        last.then_inc(taps_ready, 1)

                def transform(j):
                    g, ri, half = jobs[j]
                    s = groups[g][0]
                    s_n = sns[s]
                    pe.wait_ge(staged, j + 1)
                    pe.wait_ge(tab_loaded[s], 16)
                    ahead = taps_during(j)
                    terms = [(0, cr), (2, sn)] if ri == 0 else [(1, cr), (0, sn)]
                    for c in range(CLASSES):
                        v = j * CLASSES + c
                        if v >= 4:
                            pe.wait_ge(k_copied, v - 3)
                        for kb in range(s_n):
                            for i, (which, src) in enumerate(terms):
                                for sb in range(s_n):
                                    last = pe.matmul(kacc[v % 4][:, kb, :], tabs[s][:, c, which, sb, kb, :],
                                                     src[j % 2][:, c, sb, :],
                                                     start=i == 0 and sb == 0, stop=i == 1 and sb == s_n - 1)
                        last.then_inc(k_ready, 1)
                        if c < len(ahead):
                            tap_products(g + 1, ahead[c:c + 1])

                def power_sum(g):
                    pe.wait_ge(added, tiles_before[g + 1])
                    if g:
                        pe.wait_ge(power_ready, g)
                    for d in range(2):
                        last = pe.matmul(sum_acc[:, :], ones[:, :], power[g % 2][:, d, :], start=d == 0, stop=d == 1)
                    last.then_inc(summed, 1)

                pe.wait_ge(loaded, 80)
                pe.wait_ge(const_set, 1)
                tap_products(0, range(nts[0]))
                for g in range(len(groups)):
                    for j in range(per_group * g, per_group * (g + 1)):
                        transform(j)
                        if j == per_group * g:
                            power_sum(g)

            @block.scalar
            def _(act):
                def decays(g, tiles):
                    s, _ = groups[min(g, len(groups) - 1)]
                    first = SEQS[s][0] // P
                    for tt in tiles:
                        m = tiles_before[g] + tt
                        if m >= 2:
                            act.wait_ge(decayed, m - 1)
                        act.activation(decay[m % 2][:, :], rate[:, :], ACT.Exp,
                                       scale=nt_sb[:, first + tt:first + tt + 1]).then_inc(decay_ready, 1)
                        act.wait_ge(decayed, m + 1)
                        if m:
                            act.wait_ge(added, m)
                        act.activation(squares[:, :, :], taps[m % 2][:, :, :], ACT.Square).then_inc(squared, 1)

                def copies(j):
                    g, _, _ = jobs[j]
                    s_n = sns[groups[g][0]]
                    if j >= 2:
                        act.wait_ge(k_stored[j % 2], 16 * (j // 2))
                    for c in range(CLASSES):
                        v = j * CLASSES + c
                        act.wait_ge(k_ready, v + 1)
                        act.activation(kout[j % 2][:, c, 0:s_n, :], kacc[v % 4][:, 0:s_n, :], ACT.Copy).then_inc(k_copied, 1)
                        decays(g + 1, taps_during(j)[c:c + 1])

                act.wait_ge(loaded, 80)
                decays(0, range(nts[0]))
                for g in range(len(groups)):
                    for j in range(per_group * g, per_group * (g + 1)):
                        copies(j)
                        if j == per_group * g:
                            act.wait_ge(summed, g + 1)
                            if g >= 2:
                                act.wait_ge(power_stored, 16 * (g - 1))
                            n = SEQS[groups[g][0]][1]
                            act.activation(pout[g % 2][:, :], sum_acc[:, :], ACT.Copy, scale=float(n) * n).then_inc(power_ready, 1)

            @block.gpsimd
            def _(pool):
                pool.memset(ones[:, :], 1.0).then_inc(const_set, 1)
                for g, (s, o) in enumerate(groups):
                    for tt in range(nts[s]):
                        m = tiles_before[g] + tt
                        pool.wait_ge(decayed, m + 1)
                        if g >= 2 and tt == 0:
                            pool.wait_ge(staged, per_group * (g - 1))
                        pool.tensor_tensor(both[0][g % 2][:, tt, :], taps[m % 2][:, 0, :], taps[m % 2][:, 1, :], ALU.add)
                        pool.tensor_tensor(both[1][g % 2][:, tt, :], taps[m % 2][:, 0, :], taps[m % 2][:, 1, :],
                                           ALU.subtract).then_inc(combined, 1)
                        pool.wait_ge(squared, m + 1)
                        if tt == 0:
                            if g >= 2:
                                pool.wait_ge(summed, g - 1)
                            pool.tensor_copy(power[g % 2][:, :, :], squares[:, :, :]).then_inc(added, 1)
                        else:
                            pool.wait_ge(added, m)
                            pool.tensor_tensor(power[g % 2][:, :, :], power[g % 2][:, :, :], squares[:, :, :],
                                               ALU.add).then_inc(added, 1)

            @block.vector
            def _(dve):
                ch = Chain(dve, step)

                def decayed_taps(g, tiles):
                    s, o = groups[min(g, len(groups) - 1)]
                    for tt in tiles:
                        m = tiles_before[g] + tt
                        dve.wait_ge(taps_ready, m + 1)
                        dve.wait_ge(decay_ready, m + 1)
                        if m >= 2:
                            dve.wait_ge(squared, m - 1)
                            dve.wait_ge(combined, m - 1)
                        dve.tensor_tensor(taps[m % 2][:, 0, :], tap_acc[:, 0, :], decay[m % 2][:, :], ALU.mult)
                        dve.scalar_tensor_tensor(taps[m % 2][:, 1, :], tap_acc[:, 1, :],
                                                 keep[:, :] if tt == 0 else 1.0, decay[m % 2][:, :],
                                                 ALU.mult, ALU.mult).then_inc(decayed, 1)

                def stage(j):
                    g, ri, half = jobs[j]
                    s_n = sns[groups[g][0]]
                    src, cols = both[ri][g % 2], slice(half * HC, (half + 1) * HC)
                    dve.wait_ge(combined, tiles_before[g + 1])
                    if j:
                        dve.wait_ge(staged, j)
                    if j >= 2:
                        dve.wait_ge(k_ready, (j - 1) * CLASSES)
                    radix_stage(dve, ch, lambda a: src[:, a * s_n:(a + 1) * s_n, cols],
                                lambda c: cr[j % 2][:, c, 0:s_n, :], lambda c: sn[j % 2][:, c, 0:s_n, :],
                                lambda i: tmp[:, i, 0:s_n * HC].rearrange("p (s c) -> p s c", s=s_n)).then_inc(staged, 1)

                dve.wait_ge(loaded, 80)
                decayed_taps(0, range(nts[0]))
                stage(0)
                for j in range(len(jobs) - 1):
                    decayed_taps(jobs[j][0] + 1, taps_during(j))
                    stage(j + 1)


def long_convolutions(nc, fwd_tab, inv_tab, k_d, power_d, hy_bias, mix_d, ident, y_d):
    jobs = [(s, o, half) for o in range(ORDER) for s in range(len(SEQS)) for half in range(2)]
    nts, sns = [n // P for _, n in SEQS], [n // 512 for _, n in SEQS]
    most, wide = max(nts), max(sns)
    lag = 2
    classes = [(j, c) for j in range(len(jobs)) for c in range(CLASSES)]
    before = [sum(sns[jobs[j][0]] for j, _ in classes[:g]) for g in range(len(classes) + 1)]
    last_jobs = [j for j, (_, o, _) in enumerate(jobs) if o == ORDER - 1]
    turned_before = {j: sum(nts[jobs[i][0]] for i in last_jobs if i < j) for j in last_jobs}
    n_spec = lag + 1
    with ExitStack() as ctx:
        p = Phase(nc, ctx, "conv")
        z = [p.sb(f"z{s}", [P, nts[s], HY]) for s in range(len(SEQS))]
        gate = p.sb("gate", [P, most, HC])
        power, bias = p.sb("power", [P, len(SEQS), ORDER, HY]), p.sb("bias", [P, ORDER, HY])
        cr, sn = ([p.sb(f"{x}{b}", [P, CLASSES, wide, HC]) for b in range(2)] for x in ("cr", "sn"))
        tmp = p.sb("tmp", [P, 9, wide * HC])
        ftab, itab = ([p.sb(f"{x}{s}", [P, CLASSES, 3, sns[s], sns[s], P]) for s in range(len(SEQS))] for x in ("ftab", "itab"))
        kf = [p.sb(f"kf{b}", [P, 2, wide, HC]) for b in range(2)]
        xe = [p.sb(f"xe{b}", [P, 2, HC]) for b in range(2)]
        prod = p.sb("prod", [P, 2, 2, HC])
        spec = [p.sb(f"spec{b}", [P, 2, wide, HC]) for b in range(n_spec)]
        y_t = p.sb("y_t", [P, HC // P, most, P])
        facc = [p.ps(f"facc{b}", [P, 2, HC]) for b in range(3)]
        iacc = [p.ps(f"iacc{b}", [P, 2, HC]) for b in range(3)]
        tbank = [p.ps(f"tbank{b}", [P, CH]) for b in range(2)]
        names = ("loaded norm_ready rooted step staged f_ready x_copied products spec_ready i_ready i_copied "
                 "gate_loaded ended transposed copied stored").split()
        sem = {x: p.sem(x) for x in names}
        z_loaded = [[p.sem(f"z_loaded{s}{half}") for half in range(2)] for s in range(len(SEQS))]
        ftab_loaded = [[p.sem(f"ftab_loaded{s}{c}") for c in range(CLASSES)] for s in range(len(SEQS))]
        itab_loaded = [p.sem(f"itab_loaded{s}") for s in range(len(SEQS))]
        k_loaded = [p.sem(f"k_loaded{b}") for b in range(2)]

        with nc.Block() as block:
            @block.sync
            def _(sp):
                def load_kf(g):
                    j, c = classes[g]
                    s, o, half = jobs[j]
                    sp.dma_start(kf[g % 2][:, :, 0:sns[s], :], k_d[s][o, half, :, :, c, :, :]).then_inc(k_loaded[g % 2], 16)

                for s, (t0, n) in enumerate(SEQS):
                    first = t0 // P
                    for half in range(2):
                        cols = slice(half * HC, (half + 1) * HC)
                        sp.dma_start(z[s][:, :, cols], mix_d[first:first + nts[s], :, 2 * HY + half * HC:2 * HY + (half + 1) * HC
                                                            ].rearrange("t p c -> p t c")).then_inc(z_loaded[s][half], 16)
                        for c in range(2 * half, 2 * half + 2):
                            sp.dma_start(ftab[s][:, c, :, :, :, :], fwd_tab[s][c]).then_inc(ftab_loaded[s][c], 16)
                    if s == 0:
                        load_kf(0)
                        load_kf(1)
                    if s == 0:
                        sp.dma_start(bias[:, :, :].rearrange("p o c -> p (o c)"),
                                     hy_bias.rearrange("o c -> (o c)").rearrange("(a n) -> a n", a=1).broadcast_to([P, ORDER * HY])
                                     ).then_inc(sem["loaded"], 16)
                        for q in range(len(SEQS)):
                            sp.dma_start(power[:, q, :, :], power_d[q].rearrange("o p c -> p o c")).then_inc(sem["loaded"], 16)
                    sp.dma_start(itab[s][:, :, :, :, :, :], inv_tab[s].rearrange("c p j s k q -> p c j s k q")
                                 ).then_inc(itab_loaded[s], 16)
                for j, (s, o, half) in enumerate(jobs):
                    first = SEQS[s][0] // P
                    for g in range(max(2, j * CLASSES), (j + 1) * CLASSES):
                        sp.wait_ge(sem["spec_ready"], before[g - 1])
                        load_kf(g)
                    if j:
                        sp.wait_ge(sem["ended"], j)
                    col = o * HY + half * HC
                    sp.dma_start(gate[:, 0:nts[s], :], mix_d[first:first + nts[s], :, col:col + HC].rearrange("t p c -> p t c")
                                 ).then_inc(sem["gate_loaded"], 16)

            @block.tensor
            def _(pe):
                def forward(g):
                    j, c = classes[g]
                    s = jobs[j][0]
                    if c == 0:
                        pe.wait_ge(sem["staged"], j + 1)
                    pe.wait_ge(ftab_loaded[s][c], 16)
                    for kb in range(sns[s]):
                        v = before[g] + kb
                        if v >= 3:
                            pe.wait_ge(sem["x_copied"], v - 2)
                        for ri, terms in enumerate((((0, cr), (2, sn)), ((1, cr), (0, sn)))):
                            for i, (which, src) in enumerate(terms):
                                for sb in range(sns[s]):
                                    last = pe.matmul(facc[v % 3][:, ri, :], ftab[s][:, c, which, sb, kb, :],
                                                     src[j % 2][:, c, sb, :],
                                                     start=i == 0 and sb == 0, stop=i == 1 and sb == sns[s] - 1)
                        last.then_inc(sem["f_ready"], 1)

                def inverse(g):
                    j, c = classes[g]
                    s = jobs[j][0]
                    if c == 0:
                        pe.wait_ge(itab_loaded[s], 16)
                    pe.wait_ge(sem["spec_ready"], before[g + 1])
                    for sb in range(sns[s]):
                        v = before[g] + sb
                        if v >= 3:
                            pe.wait_ge(sem["i_copied"], v - 2)
                        for ri, terms in enumerate((((0, 0), (1, 1)), ((0, 1), (2, 0)))):
                            for i, (which, part) in enumerate(terms):
                                for kb in range(sns[s]):
                                    last = pe.matmul(iacc[v % 3][:, ri, :], itab[s][:, c, which, kb, sb, :],
                                                     spec[g % n_spec][:, part, kb, :],
                                                     start=i == 0 and kb == 0, stop=i == 1 and kb == sns[s] - 1)
                        last.then_inc(sem["i_ready"], 1)

                def turn(j):
                    s, _, half = jobs[j]
                    pe.wait_ge(sem["ended"], j + 1)
                    for tt in range(nts[s]):
                        v = turned_before[j] + tt
                        if v >= 2:
                            pe.wait_ge(sem["copied"], v - 1)
                        for q in range(HC // P):
                            last = pe.transpose(tbank[v % 2][:, q * P:(q + 1) * P],
                                                z[s][:, tt, half * HC + q * P:half * HC + (q + 1) * P], ident[:, :])
                        last.then_inc(sem["transposed"], 1)

                for g in range(len(classes) + lag):
                    if g < len(classes):
                        forward(g)
                    if g >= lag:
                        inverse(g - lag)
                        j, c = classes[g - lag]
                        if c == CLASSES - 1 and j - 1 in last_jobs:
                            turn(j - 1)
                turn(len(jobs) - 1)

            @block.scalar
            def _(act):
                def copy_forward(g):
                    j, c = classes[g]
                    for kb in range(sns[jobs[j][0]]):
                        v = before[g] + kb
                        act.wait_ge(sem["f_ready"], v + 1)
                        if v >= 2:
                            act.wait_ge(sem["spec_ready"], v - 1)
                        act.activation(xe[v % 2][:, :, :], facc[v % 3][:, :, :], ACT.Copy).then_inc(sem["x_copied"], 1)

                def copy_inverse(g):
                    j, c = classes[g]
                    for sb in range(sns[jobs[j][0]]):
                        v = before[g] + sb
                        act.wait_ge(sem["i_ready"], v + 1)
                        act.activation(cr[j % 2][:, c, sb, :], iacc[v % 3][:, 0, :], ACT.Copy)
                        act.activation(sn[j % 2][:, c, sb, :], iacc[v % 3][:, 1, :], ACT.Copy).then_inc(sem["i_copied"], 1)

                def copy_turned(j):
                    s = jobs[j][0]
                    if j > last_jobs[0]:
                        act.wait_ge(sem["stored"], 16 * (HC // P) * (j - last_jobs[0]))
                    for tt in range(nts[s]):
                        v = turned_before[j] + tt
                        act.wait_ge(sem["transposed"], v + 1)
                        act.activation(y_t[:, :, tt, :], tbank[v % 2][:, 0:HC].rearrange("p (c q) -> p c q", q=P),
                                       ACT.Copy).then_inc(sem["copied"], 1)

                def store_turned(j):
                    s, _, half = jobs[j]
                    t0, n = SEQS[s]
                    act.wait_ge(sem["copied"], turned_before[j] + nts[s])
                    for q in range(HC // P):
                        act.dma_start(y_d[half * (HC // P) + q, :, t0:t0 + n], y_t[:, q, 0:nts[s], :].rearrange(
                            "p t q -> p (t q)")).then_inc(sem["stored"], 16)

                for g in range(len(classes) + lag):
                    if g < len(classes):
                        copy_forward(g)
                    if g == 0:
                        act.wait_ge(sem["loaded"], 48)
                        act.activation(power[:, :, :, :], power[:, :, :, :], ACT.Sqrt).then_inc(sem["rooted"], 1)
                    if g >= lag:
                        copy_inverse(g - lag)
                        j, c = classes[g - lag]
                        if c == CLASSES - 1 and j - 1 in last_jobs:
                            copy_turned(j - 1)
                            store_turned(j - 1)
                copy_turned(len(jobs) - 1)
                store_turned(len(jobs) - 1)
                act.wait_ge(sem["stored"], 16 * (HC // P) * len(last_jobs))

            @block.gpsimd
            def _(pool):
                for g, (j, c) in enumerate(classes):
                    pool.wait_ge(k_loaded[g % 2], 16 * (g // 2 + 1))
                    if g >= n_spec:
                        pool.wait_ge(sem["i_ready"], before[g - n_spec + 1])
                    for kb in range(sns[jobs[j][0]]):
                        v = before[g] + kb
                        pool.wait_ge(sem["x_copied"], v + 1)
                        if v:
                            pool.wait_ge(sem["spec_ready"], v)
                        k = kf[g % 2][:, :, kb, :]
                        pool.tensor_tensor(prod[:, 0, :, :], xe[v % 2][:, :, :], k, ALU.mult)
                        pool.tensor_tensor(prod[:, 1, :, :], xe[v % 2][:, :, :], k[:, ::-1, :],
                                           ALU.mult).then_inc(sem["products"], 1)
                        pool.wait_ge(sem["products"], v + 1)
                        out = spec[g % n_spec]
                        pool.tensor_tensor(out[:, 0, kb, :], prod[:, 0, 0, :], prod[:, 0, 1, :], ALU.subtract)
                        pool.tensor_tensor(out[:, 1, kb, :], prod[:, 1, 0, :], prod[:, 1, 1, :],
                                           ALU.add).then_inc(sem["spec_ready"], 1)

            @block.vector
            def _(dve):
                ch = Chain(dve, sem["step"])

                def stage(j):
                    s, o, half = jobs[j]
                    s_n, cols = sns[s], slice(half * HC, (half + 1) * HC)
                    if o == 0:
                        dve.wait_ge(z_loaded[s][half], 16)
                    if j:
                        dve.wait_ge(sem["staged"], j)
                    radix_stage(dve, ch, lambda a: z[s][:, a * s_n:(a + 1) * s_n, cols],
                                lambda c: cr[j % 2][:, c, 0:s_n, :], lambda c: sn[j % 2][:, c, 0:s_n, :],
                                lambda i: tmp[:, i, 0:s_n * HC].rearrange("p (s c) -> p s c", s=s_n)
                                ).then_inc(sem["staged"], 1)

                def end(j):
                    s, o, half = jobs[j]
                    s_n, nt, cols = sns[s], nts[s], slice(half * HC, (half + 1) * HC)
                    dve.wait_ge(sem["i_copied"], before[(j + 1) * CLASSES])
                    dve.wait_ge(sem["staged"], min(j + 2, len(jobs)))
                    dr, dn = (lambda c: cr[j % 2][:, c, 0:s_n, :]), (lambda c: sn[j % 2][:, c, 0:s_n, :])

                    def t(i):
                        return tmp[:, i, 0:s_n * HC].rearrange("p (s c) -> p s c", s=s_n)
                    for i, (src, c, e, op) in enumerate((
                            (dr, 0, 3, ALU.add), (dr, 0, 3, ALU.subtract), (dr, 1, 2, ALU.add), (dr, 1, 2, ALU.subtract),
                            (dn, 0, 3, ALU.add), (dn, 0, 3, ALU.subtract), (dn, 1, 2, ALU.add), (dn, 1, 2, ALU.subtract))):
                        ch(dve.tensor_tensor(t(i), src(c), src(e), op))
                    ch.need(ch.count)
                    y = dr
                    ch(dve.tensor_tensor(y(0), t(0), t(2), ALU.add))
                    ch(dve.tensor_tensor(y(2), t(0), t(2), ALU.subtract))
                    ch(dve.tensor_tensor(t(8), t(5), t(7), ALU.add))
                    ch(dve.tensor_scalar(y(1), t(1), C1, None, ALU.mult))
                    ch(dve.tensor_scalar(y(3), t(1), S1, None, ALU.mult))
                    ch.need(ch.count)
                    ch(dve.tensor_tensor(y(2), y(2), t(8), ALU.add))
                    for i, w1_, w3_ in ((3, S1, -C1), (4, S1, C1), (6, C1, -S1)):
                        ch(dve.scalar_tensor_tensor(y(1), t(i), w1_, y(1), ALU.mult, ALU.add))
                        ch(dve.scalar_tensor_tensor(y(3), t(i), w3_, y(3), ALU.mult, ALU.add))
                        ch.need(ch.count)
                    ch.need(ch(dve.tensor_scalar(y(2), y(2), RH, None, ALU.mult)))
                    ys = cr[j % 2][:, :, 0:s_n, :]
                    zs = z[s][:, :, cols].rearrange("p (a s) c -> p a s c", a=CLASSES)

                    def everywhere(row):
                        return row.unsqueeze(1).unsqueeze(1).broadcast_to([P, CLASSES, s_n, HC])
                    ch(dve.tensor_tensor(ys, ys, everywhere(power[:, s, o, cols]), ALU.mult))
                    ch(dve.tensor_tensor(zs, zs, everywhere(bias[:, o, cols]), ALU.mult))
                    ch.need(ch.count)
                    ch.need(ch(dve.tensor_tensor(zs, zs, ys, ALU.add)))
                    dve.wait_ge(sem["gate_loaded"], 16 * (j + 1))
                    last = dve.tensor_tensor(zs, zs, gate[:, 0:nt, :].rearrange("p (a s) c -> p a s c", a=CLASSES), ALU.mult)
                    last.then_inc(sem["ended"], 1)
                    dve.wait_ge(sem["ended"], j + 1)

                stage(0)
                stage(1)
                dve.wait_ge(sem["rooted"], 1)
                dve.reciprocal(power[:, :, :, :], power[:, :, :, :]).then_inc(sem["norm_ready"], 1)
                dve.wait_ge(sem["norm_ready"], 1)
                for j in range(len(jobs)):
                    end(j)
                    if j + 2 < len(jobs):
                        stage(j + 2)


DIRS = 2
GATE_P = 64


def mlstm_gates(nc, gates_d, neg_max_d, a_cols, floor_cols, ident):
    with ExitStack() as ctx:
        p = Phase(nc, ctx, "gates")
        gi, gf, ab, ls, one, f_sum, a, top, m, fl = (p.sb(s, [GATE_P, T]) for s in (
            "gi", "gf", "ab", "ls", "one", "f_sum", "a", "top", "m", "floor"))
        tbank = [p.ps(f"tbank{b}", [P, TT, GATE_P]) for b in range(2)]
        loaded, step, soft, floored = p.sem("loaded"), p.sem("step"), p.sem("soft"), p.sem("floored")
        act_step, transposed, copied, stored = p.sem("act_step"), p.sem("transposed"), p.sem("copied"), p.sem("stored")
        m_ready, a_ready, top_ready = p.sem("m_ready"), p.sem("a_ready"), p.sem("top_ready")

        def scans():
            for d in range(DIRS):
                for t0, n in SEQS:
                    yield slice(32 * d, 32 * d + 32), slice(t0, t0 + n), d == 1

        with nc.Block() as block:
            @block.sync
            def _(sp):
                sp.dma_start(gi[:, :], gates_d[0, 0:GATE_P, :]).then_inc(loaded, 16)
                sp.dma_start(gf[:, :], gates_d[0, GATE_P:P, :]).then_inc(loaded, 16)
                sp.wait_ge(top_ready, 1)
                sp.dma_start(neg_max_d, top[:, :]).then_inc(stored, 16)
                sp.wait_ge(stored, 16)

            @block.scalar
            def _(act):
                act.wait_ge(loaded, 32)
                act.activation(ab[:, :], gf[:, :], ACT.Abs).then_inc(act_step, 1)
                act.wait_ge(act_step, 1)
                act.activation(ab[:, :], ab[:, :], ACT.Exp, scale=-1.0).then_inc(act_step, 1)
                act.wait_ge(act_step, 2)
                act.activation(ab[:, :], ab[:, :], ACT.Ln, bias=1.0).then_inc(soft, 1)
                act.wait_ge(m_ready, 1)
                act.activation(fl[:, :], m[:, :], ACT.Exp, scale=-1.0).then_inc(floored, 1)

            @block.vector
            def _(dve):
                ch = Chain(dve, step)
                ch(dve.memset(one[:, :], 1.0))
                dve.wait_ge(soft, 1)
                ch.need(ch(dve.scalar_tensor_tensor(ls[:, :], gf[:, :], 0.0, ab[:, :], ALU.min, ALU.subtract)))
                for rows, cols, back in scans():
                    o, x = f_sum[rows, cols], ls[rows, cols]
                    ch(dve.tensor_tensor_scan(out=o[:, ::-1] if back else o, data0=one[rows, cols],
                                              data1=x[:, ::-1] if back else x, initial=0.0, op0=ALU.mult, op1=ALU.add))
                ch.need(ch.count)
                ch.need(ch(dve.tensor_tensor(a[:, :], gi[:, :], f_sum[:, :], ALU.subtract)))
                for rows, cols, back in scans():
                    o, x = top[rows, cols], a[rows, cols]
                    ch(dve.tensor_tensor_scan(out=o[:, ::-1] if back else o, data0=x[:, ::-1] if back else x,
                                              data1=x[:, ::-1] if back else x, initial=0.0, op0=ALU.max, op1=ALU.max))
                ch.need(ch.count)
                dve.tensor_tensor(m[:, :], f_sum[:, :], top[:, :], ALU.add).then_inc(m_ready, 1)
                dve.wait_ge(m_ready, 1)
                dve.tensor_scalar(a[:, :], a[:, :], math.log(HD ** -0.5), None, ALU.add).then_inc(a_ready, 1)
                dve.tensor_scalar(top[:, :], top[:, :], -1.0, None, ALU.mult).then_inc(top_ready, 1)
                for j, cols in enumerate((a_cols, floor_cols)):
                    dve.wait_ge(transposed, j + 1)
                    dve.tensor_copy(cols[:, :, :], tbank[j][:, :, :]).then_inc(copied, 1)

            @block.tensor
            def _(pe):
                for j, src in enumerate((a, fl)):
                    pe.wait_ge((a_ready, floored)[j], 1)
                    for tt in range(TT):
                        last = pe.transpose(tbank[j][:, tt, :], src[:, tt * P:(tt + 1) * P], ident[0:GATE_P, 0:GATE_P])
                    last.then_inc(transposed, 1)


def mlstm_heads(nc, qk_d, tok_d, o_d, neg_max_d, masks, ml_gain, a_cols, floor_cols, ident, y_d):
    jobs = [(h, s) for h in range(HEADS) for s in range(len(SEQS))]
    nts = [n // P for _, n in SEQS]
    most = max(nts)
    W = HD + 1
    with ExitStack() as ctx:
        p = Phase(nc, ctx, "heads")
        q, k = ([p.sb(f"{s}{b}", [P, T]) for b in range(2)] for s in ("q", "k"))
        v = [p.sb(f"v{b}", [P, TT, W]) for b in range(2)]
        neg_m = [p.sb(f"neg_m{d}", [P, T]) for d in range(DIRS)]
        diag = [p.sb(f"diag{d}", [P, TT, P]) for d in range(DIRS)]
        mask = p.sb("mask", [P, DIRS, P])
        e = [[p.sb(f"e{d}_{b}", [P, most * P]) for b in range(2)] for d in range(DIRS)]
        pt = [[p.sb(f"pt{d}_{b}", [P, most * (most + 1) // 2, P]) for b in range(2)] for d in range(DIRS)]
        hs = p.sb("hs", [P, most, DIRS, W])
        den, rden = p.sb("den", [P, most, DIRS]), p.sb("rden", [P, most, DIRS])
        x1, x2 = p.sb("x1", [P, most, HD]), p.sb("x2", [P, most, HD])
        hn = p.sb("hn", [P, most, HD])
        ss, rs = p.sb("ss", [P, most]), p.sb("rs", [P, most])
        eps = p.sb("eps", [P, 1])
        gm = p.sb("gain", [P, HEADS])
        og, y = p.sb("og", [P, T]), p.sb("y", [P, T])
        sacc = [p.ps(f"sacc{b}", [P, most * P]) for b in range(2)]
        hacc = [p.ps(f"hacc{b}", [P, CH]) for b in range(2)]
        tbank = [p.ps(f"tbank{b}", [P, CH]) for b in range(2)]
        names = ("const_loaded const_set v_set ones_set m_loaded diag_ready scored exp_ready weighted attended "
                 "h_copied abs_ready squared step normed transposed scaled y_stored og_loaded rooted").split()
        sem = {s: p.sem(s) for s in names}
        qk_loaded = [p.sem(f"qk_loaded{b}") for b in range(2)]
        v_loaded = [p.sem(f"v_loaded{b}") for b in range(2)]

        tiles_before = [sum(nts[s] for _, s in jobs[:j]) for j in range(len(jobs) + 1)]

        def place(d, nt, s_tile, t_tile):
            if d == 0:
                return s_tile * nt - s_tile * (s_tile - 1) // 2 + t_tile - s_tile
            return s_tile * (s_tile + 1) // 2 + t_tile

        def by_turns(j, of_job, of_job_before):
            here = nts[jobs[j][1]] if j < len(jobs) else 0
            there = nts[jobs[j - 1][1]] if 1 <= j <= len(jobs) else 0
            for i in range(max(here, there)):
                if i < here:
                    of_job(j, i)
                if i < there:
                    of_job_before(j - 1, i)

        with nc.Block() as block:
            @block.sync
            def _(sp):
                sp.dma_start(mask[:, :, :], masks).then_inc(sem["const_loaded"], 16)
                sp.dma_start(gm[:, :], ml_gain).then_inc(sem["const_loaded"], 16)
                for h in range(HEADS):
                    b = h % 2
                    if h >= 2:
                        sp.wait_ge(sem["attended"], tiles_before[2 * (h - 1)])
                    sp.dma_start(q[b][:, :], qk_d[h]).then_inc(qk_loaded[b], 16)
                    sp.dma_start(k[b][:, :], qk_d[HEADS + h]).then_inc(qk_loaded[b], 16)
                    if h == 0:
                        sp.wait_ge(sem["ones_set"], 2)
                    sp.dma_start(v[b][:, :, 0:HD], tok_d[:, :, 3 * HY + h * HD:3 * HY + (h + 1) * HD].rearrange(
                        "t p c -> p t c")).then_inc(v_loaded[b], 16)
                    if h:
                        sp.wait_ge(sem["exp_ready"], tiles_before[2 * h])
                    for d in range(DIRS):
                        row = neg_max_d[32 * d + h:32 * d + h + 1, :]
                        sp.dma_start(neg_m[d][:, :], row.broadcast_to([P, T])).then_inc(sem["m_loaded"], 16)
                    if h:
                        sp.wait_ge(sem["scaled"], tiles_before[2 * h])
                        sp.dma_start(y_d[HY // P + h - 1], y[:, :]).then_inc(sem["y_stored"], 16)
                    sp.dma_start(og[:, :], o_d[h]).then_inc(sem["og_loaded"], 16)
                sp.wait_ge(sem["scaled"], tiles_before[-1])
                sp.dma_start(y_d[HY // P + HEADS - 1], y[:, :]).then_inc(sem["y_stored"], 16)
                sp.wait_ge(sem["y_stored"], 16 * HEADS)

            @block.gpsimd
            def _(pool):
                for b in range(2):
                    pool.memset(v[b][:, :, HD:W], 1.0).then_inc(sem["ones_set"], 1)
                pool.memset(eps[:, :], EPS).then_inc(sem["const_set"], 1)
                pool.wait_ge(sem["const_loaded"], 32)
                for h in range(HEADS):
                    pool.wait_ge(sem["m_loaded"], 32 * (h + 1))
                    if h:
                        pool.wait_ge(sem["exp_ready"], tiles_before[2 * h])
                    for d in range(DIRS):
                        pool.tensor_tensor(diag[d][:, :, :], neg_m[d][:, :].rearrange("p (t q) -> p t q", q=P),
                                           mask[:, d:d + 1, :].broadcast_to([P, TT, P]),
                                           ALU.add).then_inc(sem["diag_ready"], 1)

            @block.tensor
            def _(pe):
                pe.wait_ge(sem["ones_set"], 2)

                def score(j, st):
                    h, s = jobs[j]
                    t0, n = SEQS[s]
                    if s == 0 and st == 0:
                        pe.wait_ge(qk_loaded[h % 2], 32 * (h // 2 + 1))
                    i = tiles_before[j] + st
                    if i >= 2:
                        pe.wait_ge(sem["weighted"], i - 1)
                    for c in range(0, n, CH):
                        last = pe.matmul(sacc[i % 2][:, c:c + CH], k[h % 2][:, t0 + st * P:t0 + (st + 1) * P],
                                         q[h % 2][:, t0 + c:t0 + c + CH], start=True, stop=True)
                    last.then_inc(sem["scored"], 1)

                def attend(j, tt):
                    h, s = jobs[j]
                    nt, first = nts[s], SEQS[s][0] // P
                    if tt == 0:
                        if s == 0:
                            pe.wait_ge(v_loaded[h % 2], 16 * (h // 2 + 1))
                        pe.wait_ge(sem["weighted"], tiles_before[j + 1])
                    i = tiles_before[j] + tt
                    if i >= 2:
                        pe.wait_ge(sem["h_copied"], i - 1)
                    for d in range(DIRS):
                        keys = range(0, tt + 1) if d == 0 else range(tt, nt)
                        for st in keys:
                            last = pe.matmul(hacc[i % 2][:, d * W:(d + 1) * W], pt[d][j % 2][:, place(d, nt, st, tt), :],
                                             v[h % 2][:, first + st, :], start=st == keys[0], stop=st == keys[-1])
                    last.then_inc(sem["attended"], 1)

                def turn_tiles(j):
                    nt = nts[jobs[j][1]]
                    pe.wait_ge(sem["normed"], j + 1)
                    for tt in range(nt):
                        i = tiles_before[j] + tt
                        if i >= 2:
                            pe.wait_ge(sem["scaled"], i - 1)
                        pe.transpose(tbank[i % 2][:, 0:P], hn[:, tt, :], ident[:, :]).then_inc(sem["transposed"], 1)

                for j in range(len(jobs) + 2):
                    by_turns(j, score, attend)
                    if j >= 2:
                        turn_tiles(j - 2)

            @block.scalar
            def _(act):
                act.wait_ge(sem["const_set"], 1)

                def weights(j, st):
                    h, s = jobs[j]
                    nt, first = nts[s], SEQS[s][0] // P
                    if st == 0:
                        act.wait_ge(sem["diag_ready"], 2 * (h + 1))
                    i = tiles_before[j] + st
                    if i >= 2:
                        act.wait_ge(sem["weighted"], i - 1)
                    for d in range(DIRS):
                        bias = a_cols[:, first + st, 32 * d + h:32 * d + h + 1]
                        dst, tile = e[d][i % 2], first + st
                        lo, hi = ((st + 1, nt) if d == 0 else (0, st))
                        last = act.activation(dst[:, st * P:(st + 1) * P], diag[d][:, tile, :], ACT.Exp, bias=bias)
                        if hi > lo:
                            last = act.activation(dst[:, lo * P:hi * P], neg_m[d][:, (first + lo) * P:(first + hi) * P],
                                                  ACT.Exp, bias=bias)
                    last.then_inc(sem["exp_ready"], 1)

                def copy_head(j, tt):
                    if tt == 0 and j:
                        act.wait_ge(sem["squared"], j)
                    i = tiles_before[j] + tt
                    act.wait_ge(sem["attended"], i + 1)
                    act.activation(hs[:, tt, :, :].rearrange("p d w -> p (d w)"), hacc[i % 2][:, 0:DIRS * W],
                                   ACT.Copy).then_inc(sem["h_copied"], 1)

                def magnitude(j):
                    nt = nts[jobs[j][1]]
                    act.wait_ge(sem["h_copied"], tiles_before[j + 1])
                    act.activation(den[:, 0:nt, :], hs[:, 0:nt, :, HD], ACT.Abs).then_inc(sem["abs_ready"], 1)

                def root(j):
                    nt = nts[jobs[j][1]]
                    act.wait_ge(sem["squared"], j + 1)
                    act.activation(rs[:, 0:nt], ss[:, 0:nt], ACT.Sqrt, bias=eps[:, :], scale=1.0 / HD
                                   ).then_inc(sem["rooted"], 1)

                for j in range(len(jobs) + 1):
                    by_turns(j, weights, copy_head)
                    if j:
                        magnitude(j - 1)
                        root(j - 1)

            @block.vector
            def _(dve):
                ch = Chain(dve, sem["step"])
                dve.wait_ge(sem["const_loaded"], 32)

                def weigh(j):
                    s = jobs[j][1]
                    nt = nts[s]
                    if j >= 2:
                        dve.wait_ge(sem["attended"], tiles_before[j - 1])
                    for st in range(nt):
                        i = tiles_before[j] + st
                        dve.wait_ge(sem["scored"], i + 1)
                        dve.wait_ge(sem["exp_ready"], i + 1)
                        for d in range(DIRS):
                            lo, hi = (st, nt) if d == 0 else (0, st + 1)
                            at = place(d, nt, st, lo)
                            last = dve.tensor_tensor(pt[d][j % 2][:, at:at + hi - lo, :].rearrange("p t q -> p (t q)"),
                                                     sacc[i % 2][:, lo * P:hi * P], e[d][i % 2][:, lo * P:hi * P], ALU.mult)
                        last.then_inc(sem["weighted"], 1)

                def normalise(j):
                    h, s = jobs[j]
                    nt, first = nts[s], SEQS[s][0] // P
                    dve.wait_ge(sem["abs_ready"], j + 1)
                    floor = floor_cols[:, first:first + nt, :].rearrange("p t (d r) -> p t d r", d=DIRS)[:, :, :, h]
                    ch.need(ch(dve.tensor_tensor(den[:, 0:nt, :], den[:, 0:nt, :], floor, ALU.max)))
                    ch.need(ch(dve.reciprocal(rden[:, 0:nt, :], den[:, 0:nt, :])))
                    for d, x in ((0, x1), (1, x2)):
                        ch(dve.tensor_tensor(x[:, 0:nt, :], hs[:, 0:nt, d, 0:HD],
                                             rden[:, 0:nt, d:d + 1].broadcast_to([P, nt, HD]), ALU.mult))
                    ch.need(ch.count)
                    ch.need(ch(dve.tensor_tensor(x1[:, 0:nt, :], x1[:, 0:nt, :], x2[:, 0:nt, :], ALU.add)))
                    ch.need(ch(dve.tensor_tensor(x2[:, 0:nt, :], x1[:, 0:nt, :], x1[:, 0:nt, :], ALU.mult)))
                    dve.reduce_sum(ss[:, 0:nt], x2[:, 0:nt, :], axis=mybir.AxisListType.X).then_inc(sem["squared"], 1)
                    dve.wait_ge(sem["rooted"], j + 1)
                    ch.need(ch(dve.reciprocal(rs[:, 0:nt], rs[:, 0:nt])))
                    if j:
                        dve.wait_ge(sem["transposed"], tiles_before[j])
                    dve.tensor_tensor(hn[:, 0:nt, :], x1[:, 0:nt, :],
                                      rs[:, 0:nt].unsqueeze(2).broadcast_to([P, nt, HD]), ALU.mult).then_inc(sem["normed"], 1)

                def scale(j):
                    h, s = jobs[j]
                    t0, nt = SEQS[s][0], nts[s]
                    dve.wait_ge(sem["og_loaded"], 16 * (h + 1))
                    if h:
                        dve.wait_ge(sem["y_stored"], 16 * h)
                    for tt in range(nt):
                        i = tiles_before[j] + tt
                        dve.wait_ge(sem["transposed"], i + 1)
                        cols = slice(t0 + tt * P, t0 + (tt + 1) * P)
                        dve.scalar_tensor_tensor(y[:, cols], tbank[i % 2][:, 0:P], gm[:, h:h + 1], og[:, cols],
                                                 ALU.mult, ALU.mult).then_inc(sem["scaled"], 1)

                for j in range(len(jobs) + 2):
                    if j < len(jobs):
                        weigh(j)
                    if j >= 2:
                        scale(j - 2)
                    if 1 <= j <= len(jobs):
                        normalise(j - 1)


WEIGHTS = ["w_in_t", "w_out_t", "w_up_t", "w_down_t"]


def encoder(nc, a, out_prompt, out_sample):
    def scratch(name, shape):
        return nc.dram_tensor(name, shape, F32).ap()
    h2_d = scratch("h2_scratch", (HID, T))
    k_d = [scratch(f"k_scratch{s}", (ORDER, 2, P, 2, CLASSES, n // 512, HC)) for s, (_, n) in enumerate(SEQS)]
    power_d = scratch("power_scratch", (len(SEQS), ORDER, P, HY))
    qk_d = scratch("qk_scratch", (N_QK, P, T))
    tok_d = scratch("tok_scratch", (TT, P, 4 * HY))
    o_d = scratch("o_scratch", (N_O, P, T))
    gates_d = scratch("gates_scratch", (1, P, T))
    neg_max_d = scratch("neg_max_scratch", (GATE_P, T))
    y_d = scratch("y_scratch", (KD, P, T))
    g_d = scratch("g_scratch", (KF, P, T))

    with ExitStack() as whole:
        Phase.lasting = whole
        w = Phase(nc, whole, "all")
        ident = w.sb("ident", [P, P])
        ident_loaded = w.sem("ident_loaded")
        with nc.Block() as block:
            @block.sync
            def _(sp):
                sp.dma_start(ident[:, :], a["identity"]).then_inc(ident_loaded, 16)
                sp.wait_ge(ident_loaded, 16)

        hyena_hidden(nc, a, a["filt_w1"], a["positions"], h2_d)
        fwd, inv = ([a[f"{x}{s}"] for s in range(len(SEQS))] for x in ("fwd", "inv"))
        hyena_filters(nc, fwd, a["neg_t"], a["rates"], a, h2_d, k_d, power_d)
        with ExitStack() as ctx:
            p = Phase(nc, ctx, "h1")
            ht_hi, ht_lo = p.sb("hi", [P, KD, T], F32R), p.sb("lo", [P, KD, T], F32R)
            norm_transpose(nc, "n1", a["norm1_g"], ident, ht_hi, ht_lo, x_dram=a["x"])
            input_projection(nc, a["w_in_t"], a["conv_par"], a["gate_bias"], ident, ht_hi, ht_lo, qk_d, tok_d, o_d, gates_d)
        long_convolutions(nc, fwd, inv, k_d, power_d, a["hy_bias"], tok_d, ident, y_d)
        with ExitStack() as ctx:
            p = Phase(nc, ctx, "cols")
            a_cols, floor_cols = p.sb("a", [P, TT, GATE_P]), p.sb("floor", [P, TT, GATE_P])
            mlstm_gates(nc, gates_d, neg_max_d, a_cols, floor_cols, ident)
            mlstm_heads(nc, qk_d, tok_d, o_d, neg_max_d, a["masks"], a["ml_gain"], a_cols, floor_cols, ident, y_d)
        x_sb = w.sb("x", [P, TT, D])
        token_major_projection(nc, "out", KD, a["w_out_t"], y_d, x_sb, x_dram=a["x"])
        with ExitStack() as ctx:
            p = Phase(nc, ctx, "h2")
            ht_hi, ht_lo = p.sb("hi", [P, KD, T], F32R), p.sb("lo", [P, KD, T], F32R)
            norm_transpose(nc, "n2", a["norm2_g"], ident, ht_hi, ht_lo, x_sb=x_sb)
            gated_up_projection(nc, a["w_up_t"], a["ffn_par"], ht_hi, ht_lo, g_d)
        token_major_projection(nc, "down", KF, a["w_down_t"], g_d, x_sb, final=(a["final_g"], (out_prompt, out_sample)))


def laid_out(inputs):
    get = {n: np.asarray(v) for n, v in inputs.items()}
    a = {}
    a["x"] = np.concatenate([get["x_prompt"].reshape(-1, D), get["x_sample"].reshape(-1, D)]).reshape(TT, P, D)
    w_in = get["w_in"][0]
    hy, ml = 3 * HY, HEADS * HD
    gate_cols = np.zeros((D, P), np.float32)
    for g, row in enumerate(GATE_ROWS):
        gate_cols[:, row:row + HEADS] = w_in[:, hy + 4 * ml + g * HEADS:hy + 4 * ml + (g + 1) * HEADS]
    w = np.concatenate([w_in[:, hy:hy + 2 * ml], w_in[:, :hy], w_in[:, hy + 2 * ml:hy + 4 * ml], gate_cols], axis=1)

    def column_tiles(m):
        return m.reshape(KD, P, -1, P).transpose(2, 1, 0, 3)

    a["w_in_t"] = column_tiles(w)
    par = np.concatenate([get["conv_w"][0], get["conv_b"]], axis=0)
    par = np.concatenate([par[:, hy:], par[:, :hy]], axis=1)
    a["conv_par"] = par.reshape(4, N_CONV, P).transpose(2, 1, 0)
    bias = np.zeros((P, 1), np.float32)
    for g, row in enumerate(GATE_ROWS):
        bias[row:row + HEADS, 0] = get["gate_b"][0, g * HEADS:(g + 1) * HEADS]
    a["gate_bias"] = bias

    def halves(m):
        return m.reshape(-1, 2, P, 2, D // 2).transpose(3, 0, 2, 1, 4)

    def pairs(m):
        return m.reshape(m.shape[0], 2, KF, P).transpose(0, 2, 1, 3).reshape(m.shape[0], -1)

    a["w_out_t"] = halves(get["w_out"][0])
    a["w_up_t"] = column_tiles(pairs(get["w_up"][0]))
    a["w_down_t"] = halves(get["w_down"][0])
    a["ffn_par"] = pairs(np.concatenate([get["ffn_conv_w"][0], get["ffn_conv_b"]], axis=0)).reshape(4, 2 * KF, P).transpose(2, 1, 0)
    a["ml_gain"] = get["ml_norm_g"].reshape(HEADS, HD).T
    a["filt_w1"], a["filt_w2"], a["filt_w3"] = get["filt_w1"][0], get["filt_w2"][0], get["filt_w3"][0]
    a["filt_bf"] = np.stack([get["filt_b1"][0], get["filt_freq1"][0], get["filt_b2"][0], get["filt_freq2"][0]], axis=1)
    a["hy_bias"] = get["hy_bias"][0]
    a["norm1_g"], a["norm2_g"], a["final_g"] = get["norm1_g"][0], get["norm2_g"][0], get["final_g"]
    a["positions"], a["neg_t"], a["rates"] = filter_tables()
    for s, (_, n) in enumerate(SEQS):
        a[f"fwd{s}"], a[f"inv{s}"] = transform_tables(n)
    a["identity"] = np.eye(P, dtype=np.float32)
    a["keep"] = np.ones((P, 1), np.float32)
    a["keep"][0, 0] = 0.0
    key, query = np.arange(P)[:, None], np.arange(P)[None, :]
    a["masks"] = np.stack([np.where(key > query, -1e30, 0.0), np.where(key < query, -1e30, 0.0)], axis=1).astype(np.float32)
    return {n: np.ascontiguousarray(v) for n, v in a.items()}


def kernel(**inputs):
    import concourse.bacc as bacc
    from concourse.bass_utils import run_bass_kernel_spmd

    nc = bacc.Bacc("TRN2", target_bir_lowering=False, num_devices=1)
    arrays = {f"arg_{n}": v for n, v in laid_out(inputs).items()}
    a = {n[4:]: nc.dram_tensor(n, v.shape, mybir.dt.from_np(v.dtype), kind="ExternalInput").ap()
         for n, v in arrays.items()}
    outs = [nc.dram_tensor(f"out_{s}", (1, n, D), F32, kind="ExternalOutput").ap() for s, (_, n) in enumerate(SEQS)]
    encoder(nc, a, *outs)
    r = run_bass_kernel_spmd(nc, [arrays], core_ids=[0])
    return tuple(r.results[0][f"out_{s}"] for s in range(len(SEQS)))
```

```python
import math
from contextlib import ExitStack

import numpy as np

import concourse.bass as bass
from concourse import mybir
from concourse.alu_op_type import AluOpType as ALU

F32, F32R = mybir.dt.float32, mybir.dt.float32r
ACT = mybir.ActivationFunctionType

P = 128
D = 1024
KD = D // P
SEQS = [(0, 1024), (1024, 512)]
T = sum(n for _, n in SEQS)
TT = T // P
CH = 512
NCH = T // CH
HY = 512
HEADS, HD = 4, 128
ORDER = 2
EMB, HID = 33, 64
FF = 2816
KF = FF // P
EPS = 1e-6
CLASSES = 4

N_QK, N_MIX, N_V, N_O = 2 * HEADS, 3 * HY // P, HEADS, HEADS
IN_KINDS = ["qk"] * N_QK + ["mix"] * N_MIX + ["v"] * N_V + ["o"] * N_O + ["gate"]
FIRST_MIX = N_QK
FIRST_V = FIRST_MIX + N_MIX
FIRST_O = FIRST_V + N_V
N_CONV = N_QK + N_MIX
GATE_ROWS = [0, 64, 32, 96]


def pipelined(eng, kinds, stages, first=0, tail=True):
    count, deepest = len(kinds), max(lag for lag, _ in stages) if tail else 0

    def kind_of(k):
        return kinds[k] if 0 <= k < count else None

    def signature(n):
        return [(kind_of(n - lag), kind_of(n - lag - 2)) for lag, _ in stages]

    def step(n0, n, i):
        for lag, body in stages:
            kind = kind_of(n - lag)
            if kind is not None:
                k0 = n - lag
                body(i * 2 + k0 if i is not None else k0, k0 % 2,
                     i + k0 // 2 if i is not None else k0 // 2, kind, kind_of(k0 - 2))

    n = first
    while n < count + deepest:
        run = 1
        while n + run < count + deepest and signature(n + run) == signature(n):
            run += 1
        if run >= 4:
            with eng.Fori(0, run // 2) as i:
                step(n, n, i)
                step(n, n + 1, i)
            n += run // 2 * 2
        else:
            step(n, n, None)
            n += 1


class Phase:

    lasting = None

    def __init__(self, nc, ctx, name, part_of=None):
        self.nc, self.ctx, self.name, self.sems = nc, ctx, name, part_of.sems if part_of else []
        if not part_of:
            ctx.callback(self.clear)

    def sb(self, name, shape, dt=F32):
        return self.ctx.enter_context(self.nc.sbuf_tensor(f"{self.name}_{name}", shape, dt))

    def ps(self, name, shape, dt=F32):
        return self.ctx.enter_context(self.nc.psum_tensor(f"{self.name}_{name}", shape, dt))

    def sem(self, name):
        self.sems.append(self.ctx.enter_context(self.nc.semaphore(f"{self.name}_{name}")))
        return self.sems[-1]

    def pool_dma_sem(self, name):
        return Phase.lasting.enter_context(self.nc.semaphore(f"{self.name}_{name}"))

    def part(self, name):
        return Phase(self.nc, self.ctx, name, part_of=self)

    def clear(self):
        if self.sems:
            nums = sorted(s.num for s in self.sems)
            starts = [n for n in nums if n - 1 not in nums]
            ends = [n + 1 for n in nums if n + 1 not in nums]
            with self.nc.Block() as block:
                @block.sync
                def _(sp):
                    for start, end in zip(starts, ends):
                        sp.sem_clear(range(start, end))


def three_pass(pe, out, w_hi, w_lo, x_hi, x_lo, first, last):
    pe.matmul(out, w_hi, x_hi, start=first, stop=False)
    pe.matmul(out, w_hi, x_lo, start=False, stop=False)
    return pe.matmul(out, w_lo, x_hi, start=False, stop=last)


def norm_transpose(block, p, g, ident, ht_hi, ht_lo, bank, junk, x_dram=None, x_sb=None):
    x_in = [p.sb(f"x_in{b}", [P, D]) for b in range(2)] if x_sb is None else None
    gain = p.sb("gain", [P, D])
    sumsq, root, rstd = (p.sb(n, [P, TT]) for n in ("sumsq", "root", "rstd"))
    eps, eps_set = p.sb("eps", [P, 1]), p.sem("eps_set")
    xn = [p.sb(f"xn{b}", [P, D]) for b in range(2)]
    x_loaded = [p.sem(f"x_loaded{b}") for b in range(2)]
    gain_loaded = p.sem("gain_loaded")
    squared, root_ready, rstd_ready = p.sem("squared"), p.sem("root_ready"), p.sem("rstd_ready")
    xn_ready, transposed = p.sem("xn_ready"), p.sem("transposed")
    hi_ready, lo_ready = p.sem("hi_ready"), p.sem("lo_ready")
    kinds = ["tile"] * TT

    def x_of(k, b):
        return x_in[b][:, :] if x_sb is None else x_sb[:, bass.ds(k, 1), :].rearrange("p a d -> p (a d)")

    @block.sync
    def _(sp):
        sp.dma_start(gain[:, :], g.rearrange("(a d) -> a d", a=1).broadcast_to([P, D])).then_inc(gain_loaded, 16)

        def load(k, b, turn, kind, before):
            if before:
                sp.wait_ge(xn_ready, k - 1)
            sp.dma_start(x_in[b][:, :], x_dram[bass.ds(k, 1), :, :].rearrange("a p d -> (a p) d")
                         ).then_inc(x_loaded[b], 16)
        if x_sb is None:
            pipelined(sp, kinds, [(0, load)])

    @block.scalar
    def _(act):
        act.wait_ge(eps_set, 1)

        def square(k, b, turn, kind, before):
            if x_sb is None:
                act.wait_ge(x_loaded[b], (turn + 1) * 16)
            act.activation(junk, x_of(k, b), ACT.Square,
                           accum_out=sumsq[:, bass.ds(k, 1)]).then_inc(squared, 1)
            act.wait_ge(squared, k + 1)
            act.activation(root[:, bass.ds(k, 1)], sumsq[:, bass.ds(k, 1)], ACT.Sqrt, bias=eps[:, :],
                           scale=1.0 / D).then_inc(root_ready, 1)

        def high(k, b, turn, kind, before):
            for h in range(2):
                act.wait_ge(transposed, k * 2 + h + 1)
                act.activation(ht_hi[:, 4 * h:4 * h + 4, bass.ds(k * P, P)], bank[2 * b + h][:, :, :],
                               ACT.Copy).then_inc(hi_ready, 1)
        pipelined(act, kinds, [(0, square), (1, high)])

    @block.vector
    def _(dve):
        dve.memset(eps[:, :], EPS).then_inc(eps_set, 1)
        dve.wait_ge(gain_loaded, 16)

        def scale(k, b, turn, kind, before):
            dve.wait_ge(root_ready, k + 1)
            dve.reciprocal(rstd[:, bass.ds(k, 1)], root[:, bass.ds(k, 1)]).then_inc(rstd_ready, 1)
            if before:
                dve.wait_ge(transposed, k * 2 - 2)
            dve.wait_ge(rstd_ready, k + 1)
            dve.scalar_tensor_tensor(xn[b][:, :], x_of(k, b), rstd[:, bass.ds(k, 1)], gain[:, :],
                                     ALU.mult, ALU.mult).then_inc(xn_ready, 1)

        def low(k, b, turn, kind, before):
            for h in range(2):
                dve.wait_ge(hi_ready, k * 2 + h + 1)
                dve.tensor_tensor(ht_lo[:, 4 * h:4 * h + 4, bass.ds(k * P, P)], bank[2 * b + h][:, :, :],
                                  ht_hi[:, 4 * h:4 * h + 4, bass.ds(k * P, P)].bitcast(F32),
                                  ALU.subtract).then_inc(lo_ready, 1)
        pipelined(dve, kinds, [(0, scale), (1, low)])

    @block.tensor
    def _(pe):
        def turn_tiles(k, b, turn, kind, before):
            pe.wait_ge(xn_ready, k + 1)
            for h in range(2):
                if before:
                    pe.wait_ge(lo_ready, k * 2 + h - 3)
                for q in range(4):
                    c = 4 * h + q
                    last = pe.transpose(bank[2 * b + h][:, q, :], xn[b][:, c * P:(c + 1) * P], ident[:, :])
                last.then_inc(transposed, 1)
        pipelined(pe, kinds, [(0, turn_tiles)])
    return lo_ready, 2 * TT



def split_weights(p, w_tiles, kinds, width=D):
    raw = [p.sb(f"w_raw{b}", [P, KD, P]) for b in range(2)]
    hi = [p.sb(f"w_hi{b}", [P, KD, P], F32R) for b in range(2)]
    lo = [p.sb(f"w_lo{b}", [P, KD, P], F32R) for b in range(2)]
    return raw, hi, lo


def channel_major_product(pe, out, w_hi, w_lo, ht_hi, ht_lo):
    for kt in range(KD):
        for c in range(NCH):
            last = three_pass(pe, out[:, c * CH:(c + 1) * CH], w_hi[:, kt, :], w_lo[:, kt, :],
                              ht_hi[:, kt, c * CH:(c + 1) * CH], ht_lo[:, kt, c * CH:(c + 1) * CH],
                              kt == 0, kt == KD - 1)
    return last


def add_neighbours(dve, u, acc, w_prev, w_next, half_step, done, k):
    for t0, n in SEQS:
        dve.scalar_tensor_tensor(u[:, t0 + 1:t0 + n], acc[:, t0:t0 + n - 1], w_prev, u[:, t0 + 1:t0 + n],
                                 ALU.mult, ALU.add).then_inc(half_step, 1)
    for s, (t0, n) in enumerate(SEQS):
        dve.wait_ge(half_step, k * 2 + s + 1)
        last = dve.scalar_tensor_tensor(u[:, t0:t0 + n - 1], acc[:, t0 + 1:t0 + n], w_next, u[:, t0:t0 + n - 1],
                                        ALU.mult, ALU.add)
    last.then_inc(done, 1)


def input_projection(nc, x_dram, g, w_tiles, conv_par, gate_bias, ident, qk_d, tok_d, o_d, gates_d):
    with ExitStack() as ctx:
        p = Phase(nc, ctx, "in")
        ht_hi, ht_lo = p.sb("h_hi", [P, KD, T], F32R), p.sb("h_lo", [P, KD, T], F32R)
        raw, w_hi, w_lo = split_weights(p, w_tiles, IN_KINDS)
        cp = p.sb("conv_par", [P, N_CONV, 4])
        gb = p.sb("gate_bias", [P, 1])
        u = [p.sb(f"u{b}", [P, T]) for b in range(2)]
        out = [p.sb(f"out{b}", [P, TT, P]) for b in range(2)]
        acc = [p.ps(f"acc{b}", [P, T]) for b in range(2)]
        tbank = [p.ps(f"tbank{b}", [P, 4, P]) for b in range(2)]
        par_loaded = p.sem("par_loaded")
        raw_loaded = [p.sem(f"raw_loaded{b}") for b in range(2)]
        stored = [p.pool_dma_sem(f"stored{b}") for b in range(2)]
        hi_ready, lo_ready, multiplied = p.sem("hi_ready"), p.sem("lo_ready"), p.sem("multiplied")
        centred, half_step, u_ready = p.sem("centred"), p.sem("half_step"), p.sem("u_ready")
        transposed, t_copied, activated = p.sem("transposed"), p.sem("t_copied"), p.sem("activated")

        def u_free(eng, k, before):
            if before in ("mix", "v"):
                eng.wait_ge(transposed, (k - 2 - FIRST_MIX) * 3 + 3)
            elif before == "qk":
                eng.wait_ge(activated, k - 1)
            elif before:
                eng.wait_ge(activated, k - 1 - (FIRST_O - N_QK))

        banks = [bank.rearrange("p (a b) -> p a b", b=P) for bank in
                 (acc[1][:, 0:CH], acc[1][:, CH:2 * CH], acc[1][:, 2 * CH:], acc[0][:, 2 * CH:])]
        junk = p.sb("junk", [P, D])[:, :]
        with nc.Block() as block:
            normed, all_normed = norm_transpose(block, p.part("in_norm"), g, ident, ht_hi, ht_lo,
                                                banks, junk, x_dram=x_dram)

            @block.sync
            def _(sp):
                sp.dma_start(cp[:, :, :], conv_par).then_inc(par_loaded, 16)
                sp.dma_start(gb[:, :], gate_bias).then_inc(par_loaded, 16)

                def load(k, b, turn, kind, before):
                    if before:
                        sp.wait_ge(lo_ready, k - 1)
                    sp.dma_start(raw[b][:, :, :], w_tiles[bass.ds(k, 1), :, :, :].rearrange("a p k c -> (a p) k c")
                                 ).then_inc(raw_loaded[b], 16)
                pipelined(sp, ["w"] * len(IN_KINDS), [(0, load)])

            @block.scalar
            def _(act):
                act.wait_ge(par_loaded, 32)

                def high(k, b, turn, kind, before):
                    act.wait_ge(raw_loaded[b], (turn + 1) * 16)
                    if before:
                        act.wait_ge(multiplied, k - 1)
                    act.activation(w_hi[b][:, :, :], raw[b][:, :, :], ACT.Copy).then_inc(hi_ready, 1)

                def finish(k, b, turn, kind, before):
                    if before:
                        act.wait_ge(stored[b], turn * 16)
                    if kind in ("mix", "v"):
                        for g in range(3):
                            act.wait_ge(transposed, (k - FIRST_MIX) * 3 + g + 1)
                            act.activation(out[b][:, 4 * g:4 * g + 4, :], tbank[(b + g) % 2][:, :, :],
                                           ACT.Copy).then_inc(t_copied, 1)
                    else:
                        act.wait_ge(u_ready, k + 1)
                        func = {"qk": ACT.Silu, "o": ACT.Sigmoid, "gate": ACT.Copy}[kind]
                        act.activation(out[b][:, :, :].rearrange("p a b -> p (a b)"), u[b][:, :],
                                       func).then_inc(activated, 1)

                def centre(k, b, turn, kind, before):
                    if kind in ("qk", "mix"):
                        act.wait_ge(multiplied, k + 1)
                        u_free(act, k, before)
                        act.activation(u[b][:, :], acc[b][:, :], ACT.Identity,
                                       bias=cp[:, bass.ds(k, 1), 3:4].rearrange("p a b -> p (a b)"),
                                       scale=cp[:, bass.ds(k, 1), 1:2].rearrange("p a b -> p (a b)")
                                       ).then_inc(centred, 1)
                pipelined(act, IN_KINDS, [(0, high), (2, finish), (1, centre)])

            @block.vector
            def _(dve):
                dve.wait_ge(par_loaded, 32)

                def low(k, b, turn, kind, before):
                    dve.wait_ge(hi_ready, k + 1)
                    dve.tensor_tensor(w_lo[b][:, :, :], raw[b][:, :, :], w_hi[b][:, :, :].bitcast(F32),
                                      ALU.subtract).then_inc(lo_ready, 1)

                def gather(k, b, turn, kind, before):
                    if kind in ("qk", "mix"):
                        dve.wait_ge(centred, k + 1)
                        add_neighbours(dve, u[b], acc[b],
                                       cp[:, bass.ds(k, 1), 0:1].rearrange("p a b -> p (a b)"),
                                       cp[:, bass.ds(k, 1), 2:3].rearrange("p a b -> p (a b)"),
                                       half_step, u_ready, k)
                    else:
                        dve.wait_ge(multiplied, k + 1)
                        u_free(dve, k, before)
                        if kind == "gate":
                            dve.tensor_scalar(u[b][:, :], acc[b][:, :], gb[:, :], None, ALU.add).then_inc(u_ready, 1)
                        else:
                            dve.tensor_copy(u[b][:, :], acc[b][:, :]).then_inc(u_ready, 1)
                pipelined(dve, IN_KINDS, [(0, low), (1, gather)])

            @block.tensor
            def _(pe):
                pe.wait_ge(normed, all_normed)

                def product(k, b, turn, kind, before):
                    pe.wait_ge(lo_ready, k + 1)
                    if before:
                        pe.wait_ge(u_ready, k - 1)
                    channel_major_product(pe, acc[b], w_hi[b], w_lo[b], ht_hi, ht_lo).then_inc(multiplied, 1)

                def turn_tiles(k, b, turn, kind, before):
                    if kind not in ("mix", "v"):
                        return
                    pe.wait_ge(u_ready, k + 1)
                    for g in range(3):
                        n = (k - FIRST_MIX) * 3 + g
                        if not isinstance(n, int) or n >= 2:
                            pe.wait_ge(t_copied, n - 1)
                        for q in range(4):
                            t = 4 * g + q
                            last = pe.transpose(tbank[(b + g) % 2][:, q, :], u[b][:, t * P:(t + 1) * P], ident[:, :])
                        last.then_inc(transposed, 1)
                pipelined(pe, IN_KINDS, [(0, product), (1, turn_tiles)])

            @block.gpsimd
            def _(pool):
                def store(k, b, turn, kind, before):
                    if kind in ("mix", "v"):
                        pool.wait_ge(t_copied, (k - FIRST_MIX) * 3 + 3)
                        pool.dma_start(tok_d[:, :, bass.ds((k - FIRST_MIX) * P, P)].rearrange("t p c -> p t c"),
                                       out[b][:, :, :]).then_inc(stored[b], 16)
                        return
                    first, dst = {"qk": (0, qk_d), "o": (FIRST_O, o_d), "gate": (FIRST_O + N_O, gates_d)}[kind]
                    pool.wait_ge(activated, k + 1 - (0 if kind == "qk" else FIRST_O - N_QK))
                    pool.dma_start(dst[bass.ds(k - first, 1), :, :].rearrange("a p t -> (a p) t"),
                                   out[b][:, :, :].rearrange("p a b -> p (a b)")).then_inc(stored[b], 16)
                pipelined(pool, IN_KINDS, [(0, store)])
                n = len(IN_KINDS)
                pool.wait_ge(stored[0], 16 * ((n + 1) // 2))
                pool.wait_ge(stored[1], 16 * (n // 2))


def gated_up_projection(nc, x_sb, g, w_tiles, conv_par, ident, g_d):
    kinds = ["ff"] * (2 * KF)
    with ExitStack() as ctx:
        p = Phase(nc, ctx, "up")
        ht_hi, ht_lo = p.sb("h_hi", [P, KD, T], F32R), p.sb("h_lo", [P, KD, T], F32R)
        raw, w_hi, w_lo = split_weights(p, w_tiles, kinds)
        cp = p.sb("conv_par", [P, 2 * KF, 4])
        u = [p.sb(f"u{b}", [P, T]) for b in range(2)]
        sg = p.sb("silu_gate", [P, T])
        prod = p.sb("prod", [P, T])
        acc = [p.ps(f"acc{b}", [P, T]) for b in range(2)]
        par_loaded, stored = p.sem("par_loaded"), p.pool_dma_sem("stored")
        raw_loaded = [p.sem(f"raw_loaded{b}") for b in range(2)]
        hi_ready, lo_ready, multiplied = p.sem("hi_ready"), p.sem("lo_ready"), p.sem("multiplied")
        centred, half_step, u_ready = p.sem("centred"), p.sem("half_step"), p.sem("u_ready")
        gate_ready, gated = p.sem("gate_ready"), p.sem("gated")

        banks = [bank.rearrange("p (a b) -> p a b", b=P) for bank in
                 (acc[1][:, 0:CH], acc[1][:, CH:2 * CH], acc[1][:, 2 * CH:], acc[0][:, 2 * CH:])]
        with nc.Block() as block:
            normed, all_normed = norm_transpose(block, p.part("up_norm"), g, ident, ht_hi, ht_lo,
                                                banks, sg[:, 0:D], x_sb=x_sb)

            @block.sync
            def _(sp):
                sp.dma_start(cp[:, :, :], conv_par).then_inc(par_loaded, 16)

                def load(k, b, turn, kind, before):
                    if before:
                        sp.wait_ge(lo_ready, k - 1)
                    sp.dma_start(raw[b][:, :, :], w_tiles[bass.ds(k, 1), :, :, :].rearrange("a p k c -> (a p) k c")
                                 ).then_inc(raw_loaded[b], 16)
                pipelined(sp, kinds, [(0, load)])

            @block.scalar
            def _(act):
                act.wait_ge(par_loaded, 16)

                def high(k, b, turn, kind, before):
                    act.wait_ge(raw_loaded[b], (turn + 1) * 16)
                    if before:
                        act.wait_ge(multiplied, k - 1)
                    act.activation(w_hi[b][:, :, :], raw[b][:, :, :], ACT.Copy).then_inc(hi_ready, 1)

                def silu(k, b, turn, kind, before):
                    if b == 1:
                        act.wait_ge(u_ready, k + 1)
                        if before:
                            act.wait_ge(gated, turn)
                        act.activation(sg[:, :], u[1][:, :], ACT.Silu).then_inc(gate_ready, 1)

                def centre(k, b, turn, kind, before):
                    act.wait_ge(multiplied, k + 1)
                    if before:
                        act.wait_ge(gated, turn)
                    act.activation(u[b][:, :], acc[b][:, :], ACT.Identity,
                                   bias=cp[:, bass.ds(k, 1), 3:4].rearrange("p a b -> p (a b)"),
                                   scale=cp[:, bass.ds(k, 1), 1:2].rearrange("p a b -> p (a b)")
                                   ).then_inc(centred, 1)
                pipelined(act, kinds, [(0, high), (2, silu), (1, centre)])

            @block.vector
            def _(dve):
                dve.wait_ge(par_loaded, 16)

                def low(k, b, turn, kind, before):
                    dve.wait_ge(hi_ready, k + 1)
                    dve.tensor_tensor(w_lo[b][:, :, :], raw[b][:, :, :], w_hi[b][:, :, :].bitcast(F32),
                                      ALU.subtract).then_inc(lo_ready, 1)

                def gate(k, b, turn, kind, before):
                    if b == 1:
                        dve.wait_ge(gate_ready, turn + 1)
                        if before:
                            dve.wait_ge(stored, turn * 16)
                        dve.tensor_tensor(prod[:, :], sg[:, :], u[0][:, :], ALU.mult).then_inc(gated, 1)

                def gather(k, b, turn, kind, before):
                    dve.wait_ge(centred, k + 1)
                    add_neighbours(dve, u[b], acc[b],
                                   cp[:, bass.ds(k, 1), 0:1].rearrange("p a b -> p (a b)"),
                                   cp[:, bass.ds(k, 1), 2:3].rearrange("p a b -> p (a b)"),
                                   half_step, u_ready, k)
                pipelined(dve, kinds, [(0, low), (2, gate), (1, gather)])

            @block.tensor
            def _(pe):
                pe.wait_ge(normed, all_normed)

                def product(k, b, turn, kind, before):
                    pe.wait_ge(lo_ready, k + 1)
                    if before:
                        pe.wait_ge(u_ready, k - 1)
                    channel_major_product(pe, acc[b], w_hi[b], w_lo[b], ht_hi, ht_lo).then_inc(multiplied, 1)
                pipelined(pe, kinds, [(0, product)])

            @block.gpsimd
            def _(pool):
                with pool.Fori(0, KF) as i:
                    pool.wait_ge(gated, i + 1)
                    pool.dma_start(g_d[bass.ds(i, 1), :, :].rearrange("a p t -> (a p) t"), prod[:, :]).then_inc(stored, 16)
                pool.wait_ge(stored, 16 * KF)


def token_major_projection(nc, name, kt_count, w_halves, src_d, x_sb, x_dram=None, final=None):
    half = D // 2
    with ExitStack() as ctx:
        p = Phase(nc, ctx, name)
        w_raw = [p.sb(f"w_raw{b}", [P, 2, half]) for b in range(2)]
        w_hi, w_lo = (p.sb(n, [P, kt_count, half], F32R) for n in ("w_hi", "w_lo"))
        s_raw = p.sb("s_raw", [P, kt_count, P])
        s_hi, s_lo = ([p.sb(f"{n}{b}", [P, kt_count, P], F32R) for b in range(2)] for n in ("s_hi", "s_lo"))
        acc = [p.ps(f"acc{b}", [P, half]) for b in range(2)]
        s_loaded = p.sem("s_loaded")
        x_loaded = [p.sem(f"x_loaded{h}") for h in range(2)]
        w_loaded = [p.sem(f"w_loaded{b}") for b in range(2)]
        w_hi_ready, w_lo_ready, w_used = p.sem("w_hi_ready"), p.sem("w_lo_ready"), p.sem("w_used")
        s_hi_ready, s_lo_ready = p.sem("s_hi_ready"), p.sem("s_lo_ready")
        multiplied, added = p.sem("multiplied"), p.sem("added")
        if final:
            gain, y = p.sb("gain", [P, D]), p.sb("y", [P, D])
            sumsq, root, rstd = (p.sb(n, [P, TT]) for n in ("sumsq", "root", "rstd"))
            eps = p.sb("eps", [P, 1])
            eps_set, gain_loaded, squared, root_ready = (p.sem(n) for n in ("eps_set", "gain_loaded", "squared", "root_ready"))
            rstd_ready, y_ready, stored = p.sem("rstd_ready"), p.sem("y_ready"), p.pool_dma_sem("stored")
        pairs = kt_count // 2
        w_kinds = ["w"] * (pairs - 1) + ["last"]
        uses = [(pairs + 1) // 2, pairs // 2]
        second_after, skew = (2, pairs // 2), 2
        n_prompt = SEQS[0][1] // P
        t_kinds = ["first"] + ["prompt"] * (n_prompt - 1) + ["sample"] * (TT - n_prompt - 1) + ["last"]

        def row(k):
            return x_sb[:, bass.ds(k, 1), :].rearrange("p a d -> p (a d)")

        with nc.Block() as block:
            @block.sync
            def _(sp):
                def load_s(h, k, b, turn, kind, before):
                    if h or kind != "first":
                        sp.wait_ge(s_lo_ready, k + h * TT)
                    sp.dma_start(s_raw[:, :, :], src_d[:, :, bass.ds(k * P, P)].rearrange("k p t -> p k t")
                                 ).then_inc(s_loaded, 16)

                if final:
                    sp.dma_start(gain[:, :], final[0].rearrange("(a d) -> a d", a=1).broadcast_to([P, D])).then_inc(gain_loaded, 16)
                for h in range(2):
                    def load_w(k, b, turn, kind, before):
                        if before:
                            sp.wait_ge(w_lo_ready, k - 1 + h * pairs)
                        elif h:
                            sp.wait_ge(w_lo_ready, pairs)
                        sp.dma_start(w_raw[b][:, :, :], w_halves[h, bass.ds(k, 1), :, :, :].rearrange("a p q c -> (a p) q c")
                                     ).then_inc(w_loaded[b], 16)
                    load_s(h, 0, 0, 0, "first", None)
                    pipelined(sp, w_kinds[:second_after[h]], [(0, load_w)])
                    load_s(h, 1, 1, 0, "prompt", None)
                    pipelined(sp, w_kinds, [(0, load_w)], first=second_after[h])
                    if x_dram is not None:
                        sp.dma_start(x_sb[:, :, h * half:(h + 1) * half], x_dram[:, :, h * half:(h + 1) * half].rearrange(
                            "t p d -> p t d")).then_inc(x_loaded[h], 16)
                    pipelined(sp, t_kinds, [(0, lambda *at: load_s(h, *at))], first=2)

            @block.scalar
            def _(act):
                def high_s(h, k, b, turn, kind, before):
                    act.wait_ge(s_loaded, (k + 1 + h * TT) * 16)
                    if h or before:
                        act.wait_ge(multiplied, k - 1 + h * TT)
                    act.activation(s_hi[b][:, :, :], s_raw[:, :, :], ACT.Copy).then_inc(s_hi_ready, 1)

                def square(k, b, turn, kind, before):
                    act.wait_ge(added, TT + k + 1)
                    if kind != "first":
                        act.wait_ge(stored, k * 16)
                    act.activation(y[:, :], row(k), ACT.Square, accum_out=sumsq[:, bass.ds(k, 1)]).then_inc(squared, 1)
                    act.wait_ge(squared, k + 1)
                    act.activation(root[:, bass.ds(k, 1)], sumsq[:, bass.ds(k, 1)], ACT.Sqrt, bias=eps[:, :],
                                   scale=1.0 / D).then_inc(root_ready, 1)

                if final:
                    act.wait_ge(eps_set, 1)
                for h in range(2):
                    def high_w(k, b, turn, kind, before):
                        act.wait_ge(w_loaded[b], (turn + 1) * 16 + h * uses[b] * 16)
                        if h and kind == "last":
                            act.wait_ge(multiplied, TT)
                        elif h:
                            act.wait_ge(w_used, k * 2 + 2)
                        act.activation(w_hi[:, bass.ds(k * 2, 2), :], w_raw[b][:, :, :],
                                       ACT.Copy).then_inc(w_hi_ready, 1)
                    high_s(h, 0, 0, 0, "first", None)
                    pipelined(act, w_kinds[:second_after[h]], [(0, high_w)])
                    high_s(h, 1, 1, 0, "prompt", None)
                    pipelined(act, w_kinds, [(0, high_w)], first=second_after[h])
                    stages = [(0, lambda *at: high_s(h, *at))]
                    if final and h:
                        stages.append((2, square))
                    pipelined(act, t_kinds, stages, first=2)

            @block.vector
            def _(dve):
                def low_s(h, k, b, turn, kind, before):
                    dve.wait_ge(s_hi_ready, k + 1 + h * TT)
                    dve.tensor_tensor(s_lo[b][:, :, :], s_raw[:, :, :], s_hi[b][:, :, :].bitcast(F32),
                                      ALU.subtract).then_inc(s_lo_ready, 1)

                def accumulate(h, k, b, turn, kind, before):
                    dve.wait_ge(multiplied, k + 1 + h * TT)
                    if x_dram is not None and kind == "first":
                        dve.wait_ge(x_loaded[h], 16)
                    x = x_sb[:, bass.ds(k, 1), h * half:(h + 1) * half].rearrange("p a c -> p (a c)")
                    dve.tensor_tensor(x, acc[b][:, :], x, ALU.add).then_inc(added, 1)

                def scale(k, b, turn, kind, before):
                    dve.wait_ge(root_ready, k + 1)
                    dve.reciprocal(rstd[:, bass.ds(k, 1)], root[:, bass.ds(k, 1)]).then_inc(rstd_ready, 1)
                    dve.wait_ge(rstd_ready, k + 1)
                    dve.scalar_tensor_tensor(y[:, :], row(k), rstd[:, bass.ds(k, 1)], gain[:, :],
                                             ALU.mult, ALU.mult).then_inc(y_ready, 1)

                if final:
                    dve.memset(eps[:, :], EPS).then_inc(eps_set, 1)
                    dve.wait_ge(gain_loaded, 16)
                for h in range(2):
                    def low_w(k, b, turn, kind, before):
                        dve.wait_ge(w_hi_ready, k + 1 + h * pairs)
                        dve.tensor_tensor(w_lo[:, bass.ds(k * 2, 2), :], w_raw[b][:, :, :],
                                          w_hi[:, bass.ds(k * 2, 2), :].bitcast(F32), ALU.subtract).then_inc(w_lo_ready, 1)
                    low_s(h, 0, 0, 0, "first", None)
                    pipelined(dve, w_kinds[:second_after[h]], [(0, low_w)])
                    if h:
                        accumulate(0, TT - 1, (TT - 1) % 2, None, "last", None)
                    low_s(h, 1, 1, 0, "prompt", None)
                    pipelined(dve, w_kinds, [(0, low_w)], first=second_after[h])
                    accumulate(h, 0, 0, 0, "first", None)
                    stages = [(0, lambda *at: low_s(h, *at)), (1, lambda *at: accumulate(h, *at))]
                    if final and h:
                        stages.append((2, scale))
                    pipelined(dve, t_kinds, stages, first=2, tail=h == 1)

            @block.tensor
            def _(pe):
                for h in range(2):
                    def begin(k, b, before):
                        pe.wait_ge(s_lo_ready, k + 1 + h * TT)
                        if h or before:
                            pe.wait_ge(added, k - 1 + h * TT)

                    def row_tile(b, kt):
                        return three_pass(pe, acc[b][:, :], s_hi[b][:, kt, :], s_lo[b][:, kt, :],
                                          w_hi[:, kt, :], w_lo[:, kt, :], kt == 0, kt == kt_count - 1)

                    def product(k, b, turn, kind, before):
                        begin(k, b, before)
                        for kt in range(kt_count):
                            last = row_tile(b, kt)
                            if kind == "last" and h == 0 and kt < kt_count - 1:
                                last.then_inc(w_used, 1)
                        last.then_inc(multiplied, 1)

                    begin(0, 0, None)
                    for pair in range(pairs + skew):
                        if pair < pairs:
                            pe.wait_ge(w_lo_ready, h * pairs + pair + 1)
                            for kt in (2 * pair, 2 * pair + 1):
                                last = row_tile(0, kt)
                            if pair == pairs - 1:
                                last.then_inc(multiplied, 1)
                        if pair == skew:
                            begin(1, 1, None)
                        if pair >= skew:
                            for kt in (2 * (pair - skew), 2 * (pair - skew) + 1):
                                last = row_tile(1, kt)
                    last.then_inc(multiplied, 1)
                    pipelined(pe, t_kinds, [(0, product)], first=2)

            if final:
                @block.gpsimd
                def _(pool):
                    def store(k, b, turn, kind, before):
                        pool.wait_ge(y_ready, k + 1)
                        prompt = kind in ("first", "prompt")
                        dst = final[1][0 if prompt else 1]
                        pool.dma_start(dst[0, bass.ds(k * P - (0 if prompt else SEQS[1][0]), P), :], y[:, :]
                                       ).then_inc(stored, 16)
                    pipelined(pool, t_kinds, [(0, store)])
                    pool.wait_ge(stored, 16 * TT)


C1, S1, RH = math.cos(math.pi / 8), math.sin(math.pi / 8), math.sqrt(0.5)


def transform_tables(n):
    b = n // 4
    m = np.arange(b)[:, None]
    fwd = np.zeros((CLASSES, P, 3, b // P, b // P, P), np.float32)
    inv = np.zeros((CLASSES, P, 3, b // P, b // P, P), np.float32)
    for c in range(CLASSES):
        k = c + 8 * np.arange(b)[None, :]
        phase = 2 * np.pi * ((m * (2 * k + 1)) % (4 * n)) / (4 * n)
        for j, a in enumerate((np.cos(phase), np.sin(phase), -np.sin(phase))):
            fwd[c, :, j] = a.reshape(b // P, P, b // P, P).transpose(1, 0, 2, 3)
            inv[c, :, j] = a.T.reshape(b // P, P, b // P, P).transpose(1, 0, 2, 3)
    return fwd, inv


def filter_tables():
    zs, ts = [], []
    for _, n in SEQS:
        t = np.linspace(0.0, 1.0, n, dtype=np.float32)[:, None]
        bands = (EMB - 1) // 2
        freqs = np.linspace(1e-4, bands - 1, bands, dtype=np.float32)
        ang = np.float32(2.0 * math.pi / n) * np.arange(n, dtype=np.float32)[:, None] * freqs[None, :]
        zs.append(np.concatenate([t, np.cos(ang), -np.sin(ang)], axis=-1).astype(np.float32))
        ts.append(-t[:, 0])
    lo, hi = math.log(1e-2) / 1.5, math.log(1e-2) / 0.3
    rates = np.abs(np.linspace(lo, hi, HY, dtype=np.float32))
    return (np.ascontiguousarray(np.concatenate(zs).T), np.ascontiguousarray(np.concatenate(ts).reshape(TT, P).T),
            np.ascontiguousarray(np.broadcast_to(rates, (P, HY))))


class Chain:

    def __init__(self, eng, sem):
        self.eng, self.sem, self.count = eng, sem, 0

    def __call__(self, ins):
        ins.then_inc(self.sem, 1)
        self.count += 1
        return self.count

    def need(self, count):
        self.eng.wait_ge(self.sem, count)


def radix_stage(dve, ch, x, cr, sn, tmp):
    r, t1, t2, u, v, pp, qq, ps_, qs = (tmp(j) for j in range(9))
    n_r = ch(dve.tensor_scalar(r, x(2), RH, None, ALU.mult))
    n_1 = ch(dve.tensor_scalar(t1, x(1), C1, None, ALU.mult))
    n_2 = ch(dve.tensor_scalar(t2, x(1), S1, None, ALU.mult))
    ch.need(n_r)
    ch(dve.tensor_tensor(u, x(0), r, ALU.add))
    ch(dve.tensor_tensor(v, x(0), r, ALU.subtract))
    ch.need(n_1)
    ch(dve.scalar_tensor_tensor(pp, x(3), S1, t1, ALU.mult, ALU.add))
    ch(dve.scalar_tensor_tensor(qs, x(3), -S1, t1, ALU.mult, ALU.add))
    ch.need(n_2)
    ch(dve.scalar_tensor_tensor(qq, x(3), -C1, t2, ALU.mult, ALU.add))
    n_p = ch(dve.scalar_tensor_tensor(ps_, x(3), C1, t2, ALU.mult, ALU.add))
    ch.need(n_p)
    for c, a, b, sign in ((0, u, pp, ALU.add), (3, u, pp, ALU.subtract), (1, v, qq, ALU.add), (2, v, qq, ALU.subtract)):
        ch(dve.tensor_tensor(cr(c), a, b, sign))
    for c, a, sign in ((0, ps_, ALU.add), (3, ps_, ALU.subtract), (1, qs, ALU.add), (2, qs, ALU.subtract)):
        last = dve.tensor_tensor(sn(c), a, r, sign)
    return last


def hyena_hidden(block, p, par, w1, z_t, h2_d, between):
    magic, two_pi_hi, two_pi_lo = 1.5 * 2.0 ** 23, 6.28125, 2 * math.pi - 6.28125
    limit = 3.1415925
    z = p.sb("z", [EMB, T])
    w1_sb = p.sb("w1", [EMB, HID])
    w2_sb = p.sb("w2", [HID, HID])
    bf = p.sb("bf", [HID, 4])
    x, n, h = p.sb("x", [HID, T]), p.sb("n", [HID, T]), p.sb("h", [HID, T])
    acc = p.ps("acc", [HID, T])
    loaded, multiplied, step, sined, stored = (p.sem(s) for s in ("loaded", "multiplied", "step", "sined", "stored"))

    @block.sync
    def _(sp):
        sp.dma_start(z[:, :], z_t).then_inc(loaded, 16)
        sp.dma_start(w1_sb[:, :], w1).then_inc(loaded, 16)
        sp.dma_start(w2_sb[:, :], par["filt_w2"]).then_inc(loaded, 16)
        sp.dma_start(bf[:, :], par["filt_bf"]).then_inc(loaded, 16)

    @block.tensor
    def _(pe):
        pe.wait_ge(loaded, 64)
        for layer, (w, src) in enumerate(((w1_sb, z), (w2_sb, h))):
            if layer:
                pe.wait_ge(sined, 1)
            for c in range(NCH):
                last = pe.matmul(acc[:, c * CH:(c + 1) * CH], w[:, :], src[:, c * CH:(c + 1) * CH],
                                 start=True, stop=True)
            last.then_inc(multiplied, 1)

    def reduced_argument(dve, layer):
        ch = Chain(dve, step)
        ch.count = 6 * layer
        dve.wait_ge(multiplied, layer + 1)
        if layer:
            dve.wait_ge(sined, 1)
        ch.need(ch(dve.tensor_scalar(x[:, :], acc[:, :], bf[:, 2 * layer:2 * layer + 1],
                                     bf[:, 2 * layer + 1:2 * layer + 2], ALU.add, ALU.mult)))
        ch.need(ch(dve.tensor_scalar(n[:, :], x[:, :], 1 / (2 * math.pi), magic, ALU.mult, ALU.add)))
        ch.need(ch(dve.tensor_scalar(n[:, :], n[:, :], -magic, None, ALU.add)))
        ch.need(ch(dve.scalar_tensor_tensor(x[:, :], n[:, :], -two_pi_hi, x[:, :], ALU.mult, ALU.add)))
        ch.need(ch(dve.scalar_tensor_tensor(x[:, :], n[:, :], -two_pi_lo, x[:, :], ALU.mult, ALU.add)))
        ch.need(ch(dve.tensor_scalar(x[:, :], x[:, :], limit, -limit, ALU.min, ALU.max)))

    def sine(act, layer):
        act.wait_ge(step, 6 * (layer + 1))
        if layer:
            act.wait_ge(multiplied, 2)
        act.activation(h[:, :], x[:, :], ACT.Sin).then_inc(sined, 1)

    @block.vector
    def _(dve):
        dve.wait_ge(loaded, 64)
        reduced_argument(dve, 0)

    between(lambda act: sine(act, 0))

    @block.vector
    def _(dve):
        reduced_argument(dve, 1)

    @block.scalar
    def _(act):
        sine(act, 1)

    @block.sync
    def _(sp):
        sp.wait_ge(sined, 2)
        sp.dma_start(h2_d, h[:, :]).then_inc(stored, 16)
        sp.wait_ge(stored, 16)


HC = HY // 2


def hyena_filters(nc, tables, neg_t, rates, par, h2_d, k_d, power_d):
    groups = [(s, o) for s in range(len(SEQS)) for o in range(ORDER)]
    nts = [n // P for _, n in SEQS]
    sns = [n // 512 for _, n in SEQS]
    tiles_before = [sum(nts[s] for s, _ in groups[:g]) for g in range(len(groups) + 1)]
    jobs = [(g, ri, half) for g in range(len(groups)) for ri in range(2) for half in range(2)]
    per_group = 4
    with ExitStack() as ctx:
        p = Phase(nc, ctx, "filt")
        h2_parts = p.sb("h2_parts", [P, T], F32R)
        w3_hi, w3_lo = p.sb("w3_hi", [P, 2, ORDER, HY], F32R), p.sb("w3_lo", [HID, 2, ORDER, HY], F32R)
        nt_sb, rate = p.sb("neg_t", [P, TT]), p.sb("rates", [P, HY])
        keep, ones = p.sb("keep", [P, 1]), p.sb("ones", [P, P])
        decay = [p.sb(f"decay{b}", [P, HY]) for b in range(2)]
        taps = [p.sb(f"taps{b}", [P, 2, HY]) for b in range(2)]
        squares = p.sb("squares", [P, 2, HY])
        power = p.sb("power", [P, 2, HY])
        both = [[p.sb(f"both{ri}_{b}", [P, max(nts), HY]) for b in range(2)] for ri in range(2)]
        cr, sn = ([p.sb(f"{x}{b}", [P, CLASSES, max(sns), HC]) for b in range(2)] for x in ("cr", "sn"))
        tmp = p.sb("tmp", [P, 9, max(sns) * HC])
        flat = tmp[:, :, :].rearrange("p i c -> p (i c)")
        h2_raw = flat[:, 0:T]
        w3_raw = flat[:, T:T + 2 * ORDER * HY].rearrange("p (d o c) -> p d o c", d=2, o=ORDER)
        tabs = [p.sb(f"tab{s}", [P, CLASSES, 3, sns[s], sns[s], P]) for s in range(len(SEQS))]
        kout = [p.sb(f"kout{b}", [P, CLASSES, max(sns), HC]) for b in range(2)]
        pout = p.sb("pout", [P, HY])
        tap_acc = p.ps("tap_acc", [P, 2, HY])
        sum_acc = p.ps("sum_acc", [P, HY])
        kbank = p.ps("kbank", [P, 4, max(sns), HC])
        kacc = [kbank[:, b, :, :] for b in range(4)]
        spare_acc = kbank[:, 0:2, :, :].rearrange("p b s c -> p b (s c)")
        loaded, const_set, hi_split, lo_split = (p.sem(n) for n in ("loaded", "const_set", "hi_split", "lo_split"))
        tab_loaded = [p.sem(f"tab_loaded{s}") for s in range(len(SEQS))]
        taps_ready, decay_ready, decayed = p.sem("taps_ready"), p.sem("decay_ready"), p.sem("decayed")
        squared, combined, added, summed = p.sem("squared"), p.sem("combined"), p.sem("added"), p.sem("summed")
        step, staged, k_ready, k_copied = p.sem("step"), p.sem("staged"), p.sem("k_ready"), p.sem("k_copied")
        power_ready, power_stored = p.sem("power_ready"), p.sem("power_stored")
        k_stored = [p.sem(f"k_stored{b}") for b in range(2)]

        def taps_psum(g, m):
            return spare_acc if g == 0 and m % 2 else tap_acc

        def taps_during(j):
            g, i, turns = jobs[j][0] + 1, j % per_group, per_group - 1
            nt = nts[groups[g][0]] if g < len(groups) and i < turns else 0
            return range(nt * i // turns, nt * (i + 1) // turns)

        def taps_after(j, c):
            ahead = taps_during(j)
            i = c - (CLASSES - len(ahead))
            return ahead[i:i + 1] if i >= 0 else ahead[0:0]

        with nc.Block() as block:
            @block.sync
            def _(sp):
                for part in (slice(0, HID), slice(HID, P)):
                    sp.dma_start(h2_raw[part, :], h2_d).then_inc(loaded, 16)
                    sp.dma_start(w3_raw[part, :, :, :], par["filt_w3"].rearrange("h (d o c) -> h d o c", d=2, o=ORDER)
                                 ).then_inc(loaded, 16)
                sp.dma_start(nt_sb[:, :], neg_t).then_inc(loaded, 16)
                sp.dma_start(rate[:, :], rates).then_inc(loaded, 16)
                sp.dma_start(keep[:, :], par["keep"]).then_inc(loaded, 16)
                for s in range(len(SEQS)):
                    sp.dma_start(tabs[s][:, :, :, :, :, :], tables[s].rearrange("c p j s k q -> p c j s k q")
                                 ).then_inc(tab_loaded[s], 16)
                for j, (g, ri, half) in enumerate(jobs):
                    s, o = groups[g]
                    sp.wait_ge(k_copied, (j + 1) * CLASSES)
                    sp.dma_start(k_d[s][o, half, :, ri, :, :, :], kout[j % 2][:, :, 0:sns[s], :]).then_inc(k_stored[j % 2], 16)
                    if j % per_group == 0:
                        sp.wait_ge(power_ready, g + 1)
                        sp.dma_start(power_d[s, o], pout[:, :]).then_inc(power_stored, 16)
                sp.wait_ge(power_stored, 16 * len(groups))
                for b in range(2):
                    sp.wait_ge(k_stored[b], 16 * (len(jobs) // 2))

            @block.tensor
            def _(pe):
                def tap_products(g, tiles):
                    for tt in tiles:
                        s, o = groups[g]
                        t0 = SEQS[s][0]
                        m = tiles_before[g] + tt
                        if g:
                            pe.wait_ge(decayed, m)
                        elif m >= 2:
                            pe.wait_ge(decayed, m - 1)
                        rows = slice(t0 + tt * P, t0 + (tt + 1) * P)
                        for d in range(2):
                            out = taps_psum(g, m)[:, d, :]
                            pe.matmul(out, h2_parts[:, rows], w3_hi[:, d, o, :], start=True, stop=False)
                            last = pe.matmul(out, h2_parts[0:HID, rows], w3_lo[:, d, o, :], start=False, stop=True)
                        last.then_inc(taps_ready, 1)

                def transform(j):
                    g, ri, half = jobs[j]
                    s = groups[g][0]
                    s_n = sns[s]
                    pe.wait_ge(staged, j + 1)
                    pe.wait_ge(tab_loaded[s], 16)
                    terms = [(0, cr), (2, sn)] if ri == 0 else [(1, cr), (0, sn)]
                    if j == 0:
                        pe.wait_ge(decayed, tiles_before[1])
                    for c in range(CLASSES):
                        v = j * CLASSES + c
                        if v >= 4:
                            pe.wait_ge(k_copied, v - 3)
                        for kb in range(s_n):
                            for i, (which, src) in enumerate(terms):
                                for sb in range(s_n):
                                    last = pe.matmul(kacc[v % 4][:, kb, :], tabs[s][:, c, which, sb, kb, :],
                                                     src[j % 2][:, c, sb, :],
                                                     start=i == 0 and sb == 0, stop=i == 1 and sb == s_n - 1)
                        last.then_inc(k_ready, 1)
                        tap_products(g + 1, taps_after(j, c))

                def power_sum(g):
                    pe.wait_ge(added, tiles_before[g + 1])
                    if g:
                        pe.wait_ge(power_ready, g)
                    for d in range(2):
                        last = pe.matmul(sum_acc[:, :], ones[:, :], power[:, d, :], start=d == 0, stop=d == 1)
                    last.then_inc(summed, 1)

                pe.wait_ge(lo_split, 2)
                pe.wait_ge(const_set, 1)
                tap_products(0, range(nts[0]))
                for g in range(len(groups)):
                    power_sum(g)
                    for j in range(per_group * g, per_group * (g + 1)):
                        transform(j)

            @block.scalar
            def _(act):
                all_tiles = [(g, tt) for g in range(len(groups)) for tt in range(nts[groups[g][0]])]

                def decay_of(m):
                    g, tt = all_tiles[m]
                    tile = SEQS[groups[g][0]][0] // P + tt
                    if m >= 2:
                        act.wait_ge(decayed, m - 1)
                    act.activation(decay[m % 2][:, :], rate[:, :], ACT.Exp,
                                   scale=nt_sb[:, tile:tile + 1]).then_inc(decay_ready, 1)

                def decays(g, tiles):
                    for tt in tiles:
                        m = tiles_before[g] + tt
                        if m + 1 < len(all_tiles):
                            decay_of(m + 1)
                        act.wait_ge(decayed, m + 1)
                        if m:
                            act.wait_ge(added, m)
                        act.activation(squares[:, :, :], taps[m % 2][:, :, :], ACT.Square).then_inc(squared, 1)

                def copies(j):
                    g, _, _ = jobs[j]
                    s_n = sns[groups[g][0]]
                    if j >= 2:
                        act.wait_ge(k_stored[j % 2], 16 * (j // 2))
                    for c in range(CLASSES):
                        v = j * CLASSES + c
                        act.wait_ge(k_ready, v + 1)
                        act.activation(kout[j % 2][:, c, 0:s_n, :], kacc[v % 4][:, 0:s_n, :], ACT.Copy).then_inc(k_copied, 1)
                        decays(g + 1, taps_after(j, c))

                act.wait_ge(loaded, 112)
                act.activation(h2_parts[:, :], h2_raw, ACT.Copy).then_inc(hi_split, 1)
                act.activation(w3_hi[:, :, :, :], w3_raw, ACT.Copy).then_inc(hi_split, 1)
                decay_of(0)
                decays(0, range(nts[0]))
                for g in range(len(groups)):
                    for j in range(per_group * g, per_group * (g + 1)):
                        copies(j)
                        if j == per_group * g:
                            act.wait_ge(summed, g + 1)
                            if g:
                                act.wait_ge(power_stored, 16 * g)
                            n = SEQS[groups[g][0]][1]
                            act.activation(pout[:, :], sum_acc[:, :], ACT.Copy, scale=float(n) * n).then_inc(power_ready, 1)

            @block.gpsimd
            def _(pool):
                pool.memset(ones[:, :], 1.0).then_inc(const_set, 1)
                for g, (s, o) in enumerate(groups):
                    for tt in range(nts[s]):
                        m = tiles_before[g] + tt
                        pool.wait_ge(decayed, m + 1)
                        if g >= 2 and tt == 0:
                            pool.wait_ge(staged, per_group * (g - 1))
                        pool.tensor_tensor(both[0][g % 2][:, tt, :], taps[m % 2][:, 0, :], taps[m % 2][:, 1, :], ALU.add)
                        pool.tensor_tensor(both[1][g % 2][:, tt, :], taps[m % 2][:, 0, :], taps[m % 2][:, 1, :],
                                           ALU.subtract).then_inc(combined, 1)
                        if g == 0:
                            continue
                        pool.wait_ge(squared, m + 1)
                        pool.wait_ge(added, m)
                        if tt == 0:
                            pool.wait_ge(summed, g)
                            pool.tensor_copy(power[:, :, :], squares[:, :, :]).then_inc(added, 1)
                        else:
                            pool.tensor_tensor(power[:, :, :], power[:, :, :], squares[:, :, :],
                                               ALU.add).then_inc(added, 1)

            @block.vector
            def _(dve):
                ch = Chain(dve, step)

                def add_squares(m):
                    dve.wait_ge(squared, m + 1)
                    if m:
                        dve.wait_ge(added, m)
                        dve.tensor_tensor(power[:, :, :], power[:, :, :], squares[:, :, :], ALU.add).then_inc(added, 1)
                    else:
                        dve.tensor_copy(power[:, :, :], squares[:, :, :]).then_inc(added, 1)

                def decayed_taps(g, tiles):
                    s, o = groups[min(g, len(groups) - 1)]
                    for tt in tiles:
                        m = tiles_before[g] + tt
                        dve.wait_ge(taps_ready, m + 1)
                        dve.wait_ge(decay_ready, m + 1)
                        if m >= 2:
                            dve.wait_ge(squared, m - 1)
                            dve.wait_ge(combined, m - 1)
                        acc = taps_psum(g, m)
                        dve.tensor_tensor(taps[m % 2][:, 0, :], acc[:, 0, :], decay[m % 2][:, :], ALU.mult)
                        dve.scalar_tensor_tensor(taps[m % 2][:, 1, :], acc[:, 1, :],
                                                 keep[:, :] if tt == 0 else 1.0, decay[m % 2][:, :],
                                                 ALU.mult, ALU.mult).then_inc(decayed, 1)
                        if g == 0 and m:
                            add_squares(m - 1)
                        if g == 0 and tt == nts[s] - 1:
                            add_squares(m)

                def stage(j):
                    g, ri, half = jobs[j]
                    s_n = sns[groups[g][0]]
                    src, cols = both[ri][g % 2], slice(half * HC, (half + 1) * HC)
                    dve.wait_ge(combined, tiles_before[g + 1])
                    if j:
                        dve.wait_ge(staged, j)
                    if j >= 2:
                        dve.wait_ge(k_ready, (j - 1) * CLASSES)
                    radix_stage(dve, ch, lambda a: src[:, a * s_n:(a + 1) * s_n, cols],
                                lambda c: cr[j % 2][:, c, 0:s_n, :], lambda c: sn[j % 2][:, c, 0:s_n, :],
                                lambda i: tmp[:, i, 0:s_n * HC].rearrange("p (s c) -> p s c", s=s_n)).then_inc(staged, 1)

                dve.wait_ge(hi_split, 1)
                dve.tensor_tensor(h2_parts[HID:P, :], h2_raw[HID:P, :], h2_parts[HID:P, :].bitcast(F32),
                                  ALU.subtract).then_inc(lo_split, 1)
                dve.wait_ge(hi_split, 2)
                dve.tensor_tensor(w3_lo[:, :, :, :], w3_raw[0:HID, :, :, :], w3_hi[0:HID, :, :, :].bitcast(F32),
                                  ALU.subtract).then_inc(lo_split, 1)
                dve.wait_ge(loaded, 112)
                decayed_taps(0, range(nts[0]))
                stage(0)
                for j in range(len(jobs) - 1):
                    stage(j + 1)
                    decayed_taps(jobs[j][0] + 1, taps_during(j))


def long_convolutions(nc, fwd_tab, inv_tab, k_d, power_d, hy_bias, mix_d, ident, y_d):
    jobs = [(s, o, half) for o in range(ORDER) for half in range(2) for s in range(len(SEQS))]
    nts, sns = [n // P for _, n in SEQS], [n // 512 for _, n in SEQS]
    most, wide = max(nts), max(sns)
    lag = 2
    classes = [(j, c) for j in range(len(jobs)) for c in range(CLASSES)]
    before = [sum(sns[jobs[j][0]] for j, _ in classes[:g]) for g in range(len(classes) + 1)]
    last_jobs = [j for j, (_, o, _) in enumerate(jobs) if o == ORDER - 1]
    turned_before = {j: sum(nts[jobs[i][0]] for i in last_jobs if i < j) for j in last_jobs}
    n_spec = lag + 1
    ring = 3
    with ExitStack() as ctx:
        p = Phase(nc, ctx, "conv")
        z = [p.sb(f"z{s}", [P, nts[s], HY]) for s in range(len(SEQS))]
        gate = p.sb("gate", [P, most, HC])
        power, bias = p.sb("power", [P, len(SEQS), ORDER, HY]), p.sb("bias", [P, ORDER, HY])
        cr, sn = ([p.sb(f"{x}{b}", [P, CLASSES, wide, HC]) for b in range(ring)] for x in ("cr", "sn"))
        tmp = p.sb("tmp", [P, 9, wide * HC])
        ftab, itab = ([p.sb(f"{x}{s}", [P, CLASSES, 3, sns[s], sns[s], P]) for s in range(len(SEQS))] for x in ("ftab", "itab"))
        kf = [p.sb(f"kf{b}", [P, 2, wide, HC]) for b in range(2)]
        xe = [p.sb(f"xe{b}", [P, 2, HC]) for b in range(2)]
        prod = p.sb("prod", [P, 2, 2, HC])
        spec = [p.sb(f"spec{b}", [P, 2, wide, HC]) for b in range(n_spec)]
        y_t = p.sb("y_t", [P, HC // P, most, P])
        facc = [p.ps(f"facc{b}", [P, 2, HC]) for b in range(3)]
        iacc = [p.ps(f"iacc{b}", [P, 2, HC]) for b in range(3)]
        tbank = [p.ps(f"tbank{b}", [P, CH]) for b in range(2)]
        names = ("loaded norm_ready rooted step staged f_ready x_copied products spec_ready i_ready i_copied "
                 "gate_loaded ended transposed copied stored").split()
        sem = {x: p.sem(x) for x in names}
        z_loaded = [[p.sem(f"z_loaded{s}{half}") for half in range(2)] for s in range(len(SEQS))]
        ftab_loaded = [[p.sem(f"ftab_loaded{s}{c}") for c in range(CLASSES)] for s in range(len(SEQS))]
        itab_loaded = [[p.sem(f"itab_loaded{s}{c}") for c in range(CLASSES)] for s in range(len(SEQS))]
        k_loaded = [p.sem(f"k_loaded{b}") for b in range(2)]

        with nc.Block() as block:
            @block.sync
            def _(sp):
                def load_kf(g):
                    j, c = classes[g]
                    s, o, half = jobs[j]
                    sp.dma_start(kf[g % 2][:, :, 0:sns[s], :], k_d[s][o, half, :, :, c, :, :]).then_inc(k_loaded[g % 2], 16)

                def load_z(s, half):
                    first, col = SEQS[s][0] // P, 2 * HY + half * HC
                    sp.dma_start(z[s][:, :, half * HC:(half + 1) * HC], mix_d[first:first + nts[s], :, col:col + HC].rearrange(
                        "t p c -> p t c")).then_inc(z_loaded[s][half], 16)

                def load_forward(s, c):
                    sp.dma_start(ftab[s][:, c, :, :, :, :], fwd_tab[s][c]).then_inc(ftab_loaded[s][c], 16)

                def load_inverse(s, c):
                    sp.dma_start(itab[s][:, c, :, :, :, :], inv_tab[s][c]).then_inc(itab_loaded[s][c], 16)

                load_z(0, 0)
                load_forward(0, 0)
                load_kf(0)
                load_forward(0, 1)
                load_kf(1)
                for c in range(2, CLASSES):
                    load_forward(0, c)
                    load_inverse(0, c - 2)
                load_z(1, 0)
                for c in range(CLASSES):
                    load_forward(1, c)
                for c in range(2, CLASSES):
                    load_inverse(0, c)
                load_z(0, 1)
                for c in range(CLASSES):
                    load_inverse(1, c)
                load_z(1, 1)
                sp.dma_start(bias[:, :, :].rearrange("p o c -> p (o c)"),
                             hy_bias.rearrange("o c -> (o c)").rearrange("(a n) -> a n", a=1).broadcast_to([P, ORDER * HY])
                             ).then_inc(sem["loaded"], 16)
                for q in range(len(SEQS)):
                    sp.dma_start(power[:, q, :, :], power_d[q].rearrange("o p c -> p o c")).then_inc(sem["loaded"], 16)

                def load_gate(j):
                    s, o, half = jobs[j]
                    first, col = SEQS[s][0] // P, o * HY + half * HC
                    if j:
                        sp.wait_ge(sem["ended"], j)
                    sp.dma_start(gate[:, 0:nts[s], :], mix_d[first:first + nts[s], :, col:col + HC].rearrange("t p c -> p t c")
                                 ).then_inc(sem["gate_loaded"], 16)

                for g in range(2, len(classes)):
                    sp.wait_ge(sem["spec_ready"], before[g - 1])
                    load_kf(g)
                    j, c = classes[g]
                    if c == 2 and j:
                        load_gate(j - 1)
                load_gate(len(jobs) - 1)

            @block.tensor
            def _(pe):
                def forward(g):
                    j, c = classes[g]
                    s = jobs[j][0]
                    if c == 0:
                        pe.wait_ge(sem["staged"], j + 1)
                    pe.wait_ge(ftab_loaded[s][c], 16)
                    for kb in range(sns[s]):
                        v = before[g] + kb
                        if v >= 3:
                            pe.wait_ge(sem["x_copied"], v - 2)
                        for ri, terms in enumerate((((0, cr), (2, sn)), ((1, cr), (0, sn)))):
                            for i, (which, src) in enumerate(terms):
                                for sb in range(sns[s]):
                                    last = pe.matmul(facc[v % 3][:, ri, :], ftab[s][:, c, which, sb, kb, :],
                                                     src[j % ring][:, c, sb, :],
                                                     start=i == 0 and sb == 0, stop=i == 1 and sb == sns[s] - 1)
                        last.then_inc(sem["f_ready"], 1)

                def inverse(g):
                    j, c = classes[g]
                    s = jobs[j][0]
                    pe.wait_ge(itab_loaded[s][c], 16)
                    pe.wait_ge(sem["spec_ready"], before[g + 1])
                    for sb in range(sns[s]):
                        v = before[g] + sb
                        if v >= 3:
                            pe.wait_ge(sem["i_copied"], v - 2)
                        for ri, terms in enumerate((((0, 0), (1, 1)), ((0, 1), (2, 0)))):
                            for i, (which, part) in enumerate(terms):
                                for kb in range(sns[s]):
                                    last = pe.matmul(iacc[v % 3][:, ri, :], itab[s][:, c, which, kb, sb, :],
                                                     spec[g % n_spec][:, part, kb, :],
                                                     start=i == 0 and kb == 0, stop=i == 1 and kb == sns[s] - 1)
                        last.then_inc(sem["i_ready"], 1)

                def turn(j):
                    s, _, half = jobs[j]
                    pe.wait_ge(sem["ended"], j + 1)
                    for tt in range(nts[s]):
                        v = turned_before[j] + tt
                        if v >= 2:
                            pe.wait_ge(sem["copied"], v - 1)
                        for q in range(HC // P):
                            last = pe.transpose(tbank[v % 2][:, q * P:(q + 1) * P],
                                                z[s][:, tt, half * HC + q * P:half * HC + (q + 1) * P], ident[:, :])
                        last.then_inc(sem["transposed"], 1)

                for g in range(len(classes) + lag):
                    if g < len(classes):
                        forward(g)
                    if g >= lag:
                        inverse(g - lag)
                        j, c = classes[g - lag]
                        if c == 1 and j - 2 in last_jobs:
                            turn(j - 2)
                turn(len(jobs) - 2)
                turn(len(jobs) - 1)

            @block.scalar
            def _(act):
                def copy_forward(g):
                    j, c = classes[g]
                    for kb in range(sns[jobs[j][0]]):
                        v = before[g] + kb
                        act.wait_ge(sem["f_ready"], v + 1)
                        if v >= 2:
                            act.wait_ge(sem["spec_ready"], v - 1)
                        act.activation(xe[v % 2][:, :, :], facc[v % 3][:, :, :], ACT.Copy).then_inc(sem["x_copied"], 1)

                def copy_inverse(g):
                    j, c = classes[g]
                    for sb in range(sns[jobs[j][0]]):
                        v = before[g] + sb
                        act.wait_ge(sem["i_ready"], v + 1)
                        act.activation(cr[j % ring][:, c, sb, :], iacc[v % 3][:, 0, :], ACT.Copy)
                        act.activation(sn[j % ring][:, c, sb, :], iacc[v % 3][:, 1, :], ACT.Copy).then_inc(sem["i_copied"], 1)

                def copy_turned(j):
                    s = jobs[j][0]
                    if j > last_jobs[0]:
                        act.wait_ge(sem["stored"], 16 * (HC // P) * (j - last_jobs[0]))
                    for tt in range(nts[s]):
                        v = turned_before[j] + tt
                        act.wait_ge(sem["transposed"], v + 1)
                        act.activation(y_t[:, :, tt, :], tbank[v % 2][:, 0:HC].rearrange("p (c q) -> p c q", q=P),
                                       ACT.Copy).then_inc(sem["copied"], 1)

                def store_turned(j):
                    s, _, half = jobs[j]
                    t0, n = SEQS[s]
                    act.wait_ge(sem["copied"], turned_before[j] + nts[s])
                    for q in range(HC // P):
                        act.dma_start(y_d[half * (HC // P) + q, :, t0:t0 + n], y_t[:, q, 0:nts[s], :].rearrange(
                            "p t q -> p (t q)")).then_inc(sem["stored"], 16)

                for g in range(len(classes) + lag):
                    if g < len(classes):
                        copy_forward(g)
                    if g == CLASSES:
                        act.wait_ge(sem["loaded"], 48)
                        act.activation(power[:, :, :, :], power[:, :, :, :], ACT.Sqrt).then_inc(sem["rooted"], 1)
                    if g >= lag:
                        copy_inverse(g - lag)
                        j, c = classes[g - lag]
                        if c == 1 and j - 2 in last_jobs:
                            copy_turned(j - 2)
                            store_turned(j - 2)
                for j in last_jobs[-2:]:
                    copy_turned(j)
                    store_turned(j)
                act.wait_ge(sem["stored"], 16 * (HC // P) * len(last_jobs))

            @block.gpsimd
            def _(pool):
                for g, (j, c) in enumerate(classes):
                    pool.wait_ge(k_loaded[g % 2], 16 * (g // 2 + 1))
                    if g >= n_spec:
                        pool.wait_ge(sem["i_ready"], before[g - n_spec + 1])
                    for kb in range(sns[jobs[j][0]]):
                        v = before[g] + kb
                        pool.wait_ge(sem["x_copied"], v + 1)
                        if v:
                            pool.wait_ge(sem["spec_ready"], v)
                        k = kf[g % 2][:, :, kb, :]
                        pool.tensor_tensor(prod[:, 0, :, :], xe[v % 2][:, :, :], k, ALU.mult)
                        pool.tensor_tensor(prod[:, 1, :, :], xe[v % 2][:, :, :], k[:, ::-1, :],
                                           ALU.mult).then_inc(sem["products"], 1)
                        pool.wait_ge(sem["products"], v + 1)
                        out = spec[g % n_spec]
                        pool.tensor_tensor(out[:, 0, kb, :], prod[:, 0, 0, :], prod[:, 0, 1, :], ALU.subtract)
                        pool.tensor_tensor(out[:, 1, kb, :], prod[:, 1, 0, :], prod[:, 1, 1, :],
                                           ALU.add).then_inc(sem["spec_ready"], 1)

            @block.vector
            def _(dve):
                ch = Chain(dve, sem["step"])

                def stage(j):
                    s, o, half = jobs[j]
                    s_n, cols = sns[s], slice(half * HC, (half + 1) * HC)
                    if o == 0:
                        dve.wait_ge(z_loaded[s][half], 16)
                    if j:
                        dve.wait_ge(sem["staged"], j)
                    radix_stage(dve, ch, lambda a: z[s][:, a * s_n:(a + 1) * s_n, cols],
                                lambda c: cr[j % ring][:, c, 0:s_n, :], lambda c: sn[j % ring][:, c, 0:s_n, :],
                                lambda i: tmp[:, i, 0:s_n * HC].rearrange("p (s c) -> p s c", s=s_n)
                                ).then_inc(sem["staged"], 1)

                def end(j):
                    s, o, half = jobs[j]
                    s_n, nt, cols = sns[s], nts[s], slice(half * HC, (half + 1) * HC)
                    dve.wait_ge(sem["i_copied"], before[(j + 1) * CLASSES])
                    dve.wait_ge(sem["staged"], min(j + ring, len(jobs)))
                    dr, dn = (lambda c: cr[j % ring][:, c, 0:s_n, :]), (lambda c: sn[j % ring][:, c, 0:s_n, :])

                    def t(i):
                        return tmp[:, i, 0:s_n * HC].rearrange("p (s c) -> p s c", s=s_n)
                    for i, (src, c, e, op) in enumerate((
                            (dr, 0, 3, ALU.add), (dr, 0, 3, ALU.subtract), (dr, 1, 2, ALU.add), (dr, 1, 2, ALU.subtract),
                            (dn, 0, 3, ALU.add), (dn, 0, 3, ALU.subtract), (dn, 1, 2, ALU.add), (dn, 1, 2, ALU.subtract))):
                        ch(dve.tensor_tensor(t(i), src(c), src(e), op))
                    ch.need(ch.count)
                    y = dr
                    ch(dve.tensor_tensor(y(0), t(0), t(2), ALU.add))
                    ch(dve.tensor_tensor(y(2), t(0), t(2), ALU.subtract))
                    ch(dve.tensor_tensor(t(8), t(5), t(7), ALU.add))
                    ch(dve.tensor_scalar(y(1), t(1), C1, None, ALU.mult))
                    ch(dve.tensor_scalar(y(3), t(1), S1, None, ALU.mult))
                    ch.need(ch.count)
                    ch(dve.tensor_tensor(y(2), y(2), t(8), ALU.add))
                    for i, w1_, w3_ in ((3, S1, -C1), (4, S1, C1), (6, C1, -S1)):
                        ch(dve.scalar_tensor_tensor(y(1), t(i), w1_, y(1), ALU.mult, ALU.add))
                        ch(dve.scalar_tensor_tensor(y(3), t(i), w3_, y(3), ALU.mult, ALU.add))
                        ch.need(ch.count)
                    ch.need(ch(dve.tensor_scalar(y(2), y(2), RH, None, ALU.mult)))
                    ys = cr[j % ring][:, :, 0:s_n, :]
                    zs = z[s][:, :, cols].rearrange("p (a s) c -> p a s c", a=CLASSES)

                    def everywhere(row):
                        return row.unsqueeze(1).unsqueeze(1).broadcast_to([P, CLASSES, s_n, HC])
                    ch(dve.tensor_tensor(ys, ys, everywhere(power[:, s, o, cols]), ALU.mult))
                    ch(dve.tensor_tensor(zs, zs, everywhere(bias[:, o, cols]), ALU.mult))
                    ch.need(ch.count)
                    ch.need(ch(dve.tensor_tensor(zs, zs, ys, ALU.add)))
                    dve.wait_ge(sem["gate_loaded"], 16 * (j + 1))
                    last = dve.tensor_tensor(zs, zs, gate[:, 0:nt, :].rearrange("p (a s) c -> p a s c", a=CLASSES), ALU.mult)
                    last.then_inc(sem["ended"], 1)
                    dve.wait_ge(sem["ended"], j + 1)

                for j in range(ring):
                    stage(j)
                dve.wait_ge(sem["rooted"], 1)
                dve.reciprocal(power[:, :, :, :], power[:, :, :, :]).then_inc(sem["norm_ready"], 1)
                dve.wait_ge(sem["norm_ready"], 1)
                for j in range(len(jobs)):
                    end(j)
                    if j + ring < len(jobs):
                        stage(j + ring)


DIRS = 2
GATE_P = 64


def mlstm_gates(block, p, gates_d, neg_max_d, cols_d, ident, other_act):
    gi, gf, ab, ls, one, f_sum, a, top, m, fl = (p.sb(s, [GATE_P, T]) for s in (
        "gi", "gf", "ab", "ls", "one", "f_sum", "a", "top", "m", "floor"))
    columns = [p.sb(s, [P, TT, GATE_P]) for s in ("a_cols", "floor_cols")]
    tbank = [p.ps(f"tbank{b}", [P, TT, GATE_P]) for b in range(2)]
    loaded, step, soft, floored = p.sem("loaded"), p.sem("step"), p.sem("soft"), p.sem("floored")
    act_step, transposed, copied, stored = p.sem("act_step"), p.sem("transposed"), p.sem("copied"), p.sem("stored")
    m_ready, a_ready, top_ready = p.sem("m_ready"), p.sem("a_ready"), p.sem("top_ready")

    def scans():
        for d in range(DIRS):
            for t0, n in SEQS:
                yield slice(32 * d, 32 * d + 32), slice(t0, t0 + n), d == 1

    @block.sync
    def _(sp):
        sp.dma_start(gi[:, :], gates_d[0, 0:GATE_P, :]).then_inc(loaded, 16)
        sp.dma_start(gf[:, :], gates_d[0, GATE_P:P, :]).then_inc(loaded, 16)
        sp.wait_ge(top_ready, 1)
        sp.dma_start(neg_max_d, top[:, :]).then_inc(stored, 16)
        for j in range(2):
            sp.wait_ge(copied, j + 1)
            sp.dma_start(cols_d[j], columns[j][:, :, :]).then_inc(stored, 16)
        sp.wait_ge(stored, 48)

    @block.scalar
    def _(act):
        act.wait_ge(loaded, 32)
        act.activation(ab[:, :], gf[:, :], ACT.Abs).then_inc(act_step, 1)
        act.wait_ge(act_step, 1)
        act.activation(ab[:, :], ab[:, :], ACT.Exp, scale=-1.0).then_inc(act_step, 1)
        act.wait_ge(act_step, 2)
        act.activation(ab[:, :], ab[:, :], ACT.Ln, bias=1.0).then_inc(soft, 1)
        other_act(act)
        act.wait_ge(m_ready, 1)
        act.activation(fl[:, :], m[:, :], ACT.Exp, scale=-1.0).then_inc(floored, 1)
        for j, cols in enumerate(columns):
            act.wait_ge(transposed, j + 1)
            act.activation(cols[:, :, :], tbank[j][:, :, :], ACT.Copy).then_inc(copied, 1)

    @block.vector
    def _(dve):
        ch = Chain(dve, step)
        ch(dve.memset(one[:, :], 1.0))
        dve.wait_ge(soft, 1)
        ch.need(ch(dve.scalar_tensor_tensor(ls[:, :], gf[:, :], 0.0, ab[:, :], ALU.min, ALU.subtract)))
        for rows, cols, back in scans():
            o, x = f_sum[rows, cols], ls[rows, cols]
            ch(dve.tensor_tensor_scan(out=o[:, ::-1] if back else o, data0=one[rows, cols],
                                      data1=x[:, ::-1] if back else x, initial=0.0, op0=ALU.mult, op1=ALU.add))
        ch.need(ch.count)
        ch.need(ch(dve.tensor_tensor(a[:, :], gi[:, :], f_sum[:, :], ALU.subtract)))
        for rows, cols, back in scans():
            o, x = top[rows, cols], a[rows, cols]
            ch(dve.tensor_tensor_scan(out=o[:, ::-1] if back else o, data0=x[:, ::-1] if back else x,
                                      data1=x[:, ::-1] if back else x, initial=0.0, op0=ALU.max, op1=ALU.max))
        ch.need(ch.count)
        dve.tensor_tensor(m[:, :], f_sum[:, :], top[:, :], ALU.add).then_inc(m_ready, 1)
        dve.wait_ge(m_ready, 1)
        dve.tensor_scalar(a[:, :], a[:, :], math.log(HD ** -0.5), None, ALU.add).then_inc(a_ready, 1)
        dve.tensor_scalar(top[:, :], top[:, :], -1.0, None, ALU.mult).then_inc(top_ready, 1)

    @block.tensor
    def _(pe):
        for j, src in enumerate((a, fl)):
            pe.wait_ge((a_ready, floored)[j], 1)
            for tt in range(TT):
                last = pe.transpose(tbank[j][:, tt, :], src[:, tt * P:(tt + 1) * P], ident[0:GATE_P, 0:GATE_P])
            last.then_inc(transposed, 1)


def gates_and_hidden(nc, gates_d, neg_max_d, cols_d, ident, par, h2_d):
    with ExitStack() as ctx:
        p = Phase(nc, ctx, "gates")
        with nc.Block() as block:
            hyena_hidden(block, p.part("hidden"), par, par["filt_w1"], par["positions"], h2_d,
                         lambda sine: mlstm_gates(block, p, gates_d, neg_max_d, cols_d, ident, sine))


def mlstm_heads(nc, qk_d, tok_d, o_d, neg_max_d, cols_d, masks, ml_gain, ident, y_d):
    jobs = [(h, s) for h in range(HEADS) for s in range(len(SEQS))]
    nts = [n // P for _, n in SEQS]
    most = max(nts)
    W = HD + 1
    with ExitStack() as ctx:
        p = Phase(nc, ctx, "heads")
        q, k = ([p.sb(f"{s}{b}", [P, T]) for b in range(2)] for s in ("q", "k"))
        v = [p.sb(f"v{b}", [P, TT, W]) for b in range(2)]
        neg_m = [[p.sb(f"neg_m{d}_{b}", [P, T]) for b in range(2)] for d in range(DIRS)]
        diag = [[p.sb(f"diag{d}_{b}", [P, TT, P]) for b in range(2)] for d in range(DIRS)]
        mask = p.sb("mask", [P, DIRS, P])
        e = [[p.sb(f"e{d}_{b}", [P, most * P]) for b in range(2)] for d in range(DIRS)]
        pt = [[p.sb(f"pt{d}_{s}", [P, nt * (nt + 1) // 2, P]) for s, nt in enumerate(nts)] for d in range(DIRS)]
        hs = p.sb("hs", [P, most, DIRS, W])
        den, rden = p.sb("den", [P, most, DIRS]), p.sb("rden", [P, most, DIRS])
        x1, x2 = p.sb("x1", [P, most, HD]), p.sb("x2", [P, most, HD])
        hn = p.sb("hn", [P, most, HD])
        ss, rs = p.sb("ss", [P, most]), p.sb("rs", [P, most])
        eps = p.sb("eps", [P, 1])
        gm = p.sb("gain", [P, HEADS])
        a_cols, floor_cols = p.sb("a_cols", [P, TT, GATE_P]), p.sb("floor_cols", [P, TT, GATE_P])
        og, y = ([p.sb(f"{s}{b}", [P, T]) for b in range(2)] for s in ("og", "y"))
        sacc = [p.ps(f"sacc{b}", [P, most * P]) for b in range(2)]
        hacc = [p.ps(f"hacc{b}", [P, CH]) for b in range(2)]
        tbank = [p.ps(f"tbank{b}", [P, CH]) for b in range(2)]
        names = ("const_loaded const_set ones_set diag_ready scored exp_ready weighted attended "
                 "h_copied abs_ready squared step normed transposed scaled rooted").split()
        sem = {s: p.sem(s) for s in names}
        qk_loaded = [p.sem(f"qk_loaded{b}") for b in range(2)]
        v_loaded, m_loaded, og_loaded, y_stored = (
            [p.sem(f"{s}{b}") for b in range(2)] for s in ("v_loaded", "m_loaded", "og_loaded", "y_stored"))

        tiles_before = [sum(nts[s] for _, s in jobs[:j]) for j in range(len(jobs) + 1)]

        def place(d, nt, s_tile, t_tile):
            if d == 0:
                return s_tile * nt - s_tile * (s_tile - 1) // 2 + t_tile - s_tile
            return s_tile * (s_tile + 1) // 2 + t_tile

        def by_turns(j, of_job, of_job_before):
            here = nts[jobs[j][1]] if j < len(jobs) else 0
            there = nts[jobs[j - 1][1]] if 1 <= j <= len(jobs) else 0
            for i in range(max(here, there)):
                if i < here:
                    of_job(j, i)
                if i < there:
                    of_job_before(j - 1, i)

        with nc.Block() as block:
            @block.sync
            def _(sp):
                sp.dma_start(mask[:, :, :], masks).then_inc(sem["const_loaded"], 16)
                sp.dma_start(gm[:, :], ml_gain).then_inc(sem["const_loaded"], 16)
                for j, cols in enumerate((a_cols, floor_cols)):
                    sp.dma_start(cols[:, :, :], cols_d[j]).then_inc(sem["const_loaded"], 16)

                def store_head(h):
                    sp.wait_ge(sem["scaled"], tiles_before[2 * (h + 1)])
                    sp.dma_start(y_d[HY // P + h], y[h % 2][:, :]).then_inc(y_stored[h % 2], 16)

                for h in range(HEADS):
                    b = h % 2
                    if h >= 2:
                        sp.wait_ge(sem["exp_ready"], tiles_before[2 * (h - 1)])
                        sp.wait_ge(sem["diag_ready"], DIRS * (h - 1))
                    for d in range(DIRS):
                        row = neg_max_d[32 * d + h:32 * d + h + 1, :]
                        sp.dma_start(neg_m[d][b][:, :], row.broadcast_to([P, T])).then_inc(m_loaded[b], 16)
                    if h >= 2:
                        sp.wait_ge(sem["attended"], tiles_before[2 * (h - 1)])
                    sp.dma_start(q[b][:, :], qk_d[h]).then_inc(qk_loaded[b], 16)
                    sp.dma_start(k[b][:, :], qk_d[HEADS + h]).then_inc(qk_loaded[b], 16)
                    if h == 0:
                        sp.wait_ge(sem["ones_set"], 2)
                    sp.dma_start(v[b][:, :, 0:HD], tok_d[:, :, 3 * HY + h * HD:3 * HY + (h + 1) * HD].rearrange(
                        "t p c -> p t c")).then_inc(v_loaded[b], 16)
                    if h >= 2:
                        store_head(h - 2)
                    sp.dma_start(og[b][:, :], o_d[h]).then_inc(og_loaded[b], 16)
                for h in (HEADS - 2, HEADS - 1):
                    store_head(h)
                for b in range(2):
                    sp.wait_ge(y_stored[b], 16 * (HEADS // 2))

            @block.gpsimd
            def _(pool):
                for b in range(2):
                    pool.memset(v[b][:, :, HD:W], 1.0).then_inc(sem["ones_set"], 1)
                pool.memset(eps[:, :], EPS).then_inc(sem["const_set"], 1)
                pool.wait_ge(sem["const_loaded"], 64)
                for h in range(HEADS):
                    b = h % 2
                    pool.wait_ge(m_loaded[b], 32 * (h // 2 + 1))
                    if h >= 2:
                        pool.wait_ge(sem["exp_ready"], tiles_before[2 * (h - 1)])
                    for d in range(DIRS):
                        pool.tensor_tensor(diag[d][b][:, :, :], neg_m[d][b][:, :].rearrange("p (t q) -> p t q", q=P),
                                           mask[:, d:d + 1, :].broadcast_to([P, TT, P]),
                                           ALU.add).then_inc(sem["diag_ready"], 1)

            @block.tensor
            def _(pe):
                pe.wait_ge(sem["ones_set"], 2)

                def score(j, st):
                    h, s = jobs[j]
                    t0, n = SEQS[s]
                    if s == 0 and st == 0:
                        pe.wait_ge(qk_loaded[h % 2], 32 * (h // 2 + 1))
                    i = tiles_before[j] + st
                    if i >= 2:
                        pe.wait_ge(sem["weighted"], i - 1)
                    for c in range(0, n, CH):
                        last = pe.matmul(sacc[i % 2][:, c:c + CH], k[h % 2][:, t0 + st * P:t0 + (st + 1) * P],
                                         q[h % 2][:, t0 + c:t0 + c + CH], start=True, stop=True)
                    last.then_inc(sem["scored"], 1)

                def attend(j, tt):
                    h, s = jobs[j]
                    nt, first = nts[s], SEQS[s][0] // P
                    if tt == 0:
                        if s == 0:
                            pe.wait_ge(v_loaded[h % 2], 16 * (h // 2 + 1))
                        pe.wait_ge(sem["weighted"], tiles_before[j + 1])
                    i = tiles_before[j] + tt
                    if i >= 2:
                        pe.wait_ge(sem["h_copied"], i - 1)
                    for d in range(DIRS):
                        keys = range(0, tt + 1) if d == 0 else range(tt, nt)
                        for st in keys:
                            last = pe.matmul(hacc[i % 2][:, d * W:(d + 1) * W], pt[d][j % 2][:, place(d, nt, st, tt), :],
                                             v[h % 2][:, first + st, :], start=st == keys[0], stop=st == keys[-1])
                    last.then_inc(sem["attended"], 1)

                def turn_tiles(j):
                    nt = nts[jobs[j][1]]
                    pe.wait_ge(sem["normed"], j + 1)
                    for tt in range(nt):
                        i = tiles_before[j] + tt
                        if i >= 2:
                            pe.wait_ge(sem["scaled"], i - 1)
                        pe.transpose(tbank[i % 2][:, 0:P], hn[:, tt, :], ident[:, :]).then_inc(sem["transposed"], 1)

                for j in range(len(jobs) + 2):
                    by_turns(j, score, attend)
                    if j >= 2:
                        turn_tiles(j - 2)

            @block.scalar
            def _(act):
                act.wait_ge(sem["const_set"], 1)
                act.wait_ge(sem["const_loaded"], 64)

                def weights(j, st):
                    h, s = jobs[j]
                    nt, first = nts[s], SEQS[s][0] // P
                    if st == 0:
                        act.wait_ge(sem["diag_ready"], 2 * (h + 1))
                    i = tiles_before[j] + st
                    if i >= 2:
                        act.wait_ge(sem["weighted"], i - 1)
                    for d in range(DIRS):
                        bias = a_cols[:, first + st, 32 * d + h:32 * d + h + 1]
                        dst, tile = e[d][i % 2], first + st
                        lo, hi = ((st + 1, nt) if d == 0 else (0, st))
                        last = act.activation(dst[:, st * P:(st + 1) * P], diag[d][h % 2][:, tile, :], ACT.Exp, bias=bias)
                        if hi > lo:
                            last = act.activation(dst[:, lo * P:hi * P], neg_m[d][h % 2][:, (first + lo) * P:(first + hi) * P],
                                                  ACT.Exp, bias=bias)
                    last.then_inc(sem["exp_ready"], 1)

                def copy_head(j, tt):
                    if tt == 0 and j:
                        act.wait_ge(sem["squared"], j)
                    i = tiles_before[j] + tt
                    act.wait_ge(sem["attended"], i + 1)
                    act.activation(hs[:, tt, :, :].rearrange("p d w -> p (d w)"), hacc[i % 2][:, 0:DIRS * W],
                                   ACT.Copy).then_inc(sem["h_copied"], 1)

                def magnitude(j):
                    nt = nts[jobs[j][1]]
                    act.wait_ge(sem["h_copied"], tiles_before[j + 1])
                    act.activation(den[:, 0:nt, :], hs[:, 0:nt, :, HD], ACT.Abs).then_inc(sem["abs_ready"], 1)

                def root(j):
                    nt = nts[jobs[j][1]]
                    act.wait_ge(sem["squared"], j + 1)
                    act.activation(rs[:, 0:nt], ss[:, 0:nt], ACT.Sqrt, bias=eps[:, :], scale=1.0 / HD
                                   ).then_inc(sem["rooted"], 1)

                for j in range(len(jobs) + 1):
                    by_turns(j, weights, copy_head)
                    if j:
                        magnitude(j - 1)
                        root(j - 1)

            @block.vector
            def _(dve):
                ch = Chain(dve, sem["step"])
                dve.wait_ge(sem["const_loaded"], 64)

                def weigh(j):
                    s = jobs[j][1]
                    nt = nts[s]
                    if j >= 2:
                        dve.wait_ge(sem["attended"], tiles_before[j - 1])
                    for st in range(nt):
                        i = tiles_before[j] + st
                        dve.wait_ge(sem["scored"], i + 1)
                        dve.wait_ge(sem["exp_ready"], i + 1)
                        for d in range(DIRS):
                            lo, hi = (st, nt) if d == 0 else (0, st + 1)
                            at = place(d, nt, st, lo)
                            last = dve.tensor_tensor(pt[d][j % 2][:, at:at + hi - lo, :].rearrange("p t q -> p (t q)"),
                                                     sacc[i % 2][:, lo * P:hi * P], e[d][i % 2][:, lo * P:hi * P], ALU.mult)
                        last.then_inc(sem["weighted"], 1)

                def normalise(j):
                    h, s = jobs[j]
                    nt, first = nts[s], SEQS[s][0] // P
                    dve.wait_ge(sem["abs_ready"], j + 1)
                    floor = floor_cols[:, first:first + nt, :].rearrange("p t (d r) -> p t d r", d=DIRS)[:, :, :, h]
                    ch.need(ch(dve.tensor_tensor(den[:, 0:nt, :], den[:, 0:nt, :], floor, ALU.max)))
                    ch.need(ch(dve.reciprocal(rden[:, 0:nt, :], den[:, 0:nt, :])))
                    for d, x in ((0, x1), (1, x2)):
                        ch(dve.tensor_tensor(x[:, 0:nt, :], hs[:, 0:nt, d, 0:HD],
                                             rden[:, 0:nt, d:d + 1].broadcast_to([P, nt, HD]), ALU.mult))
                    ch.need(ch.count)
                    ch.need(ch(dve.tensor_tensor(x1[:, 0:nt, :], x1[:, 0:nt, :], x2[:, 0:nt, :], ALU.add)))
                    ch.need(ch(dve.tensor_tensor(x2[:, 0:nt, :], x1[:, 0:nt, :], x1[:, 0:nt, :], ALU.mult)))
                    dve.reduce_sum(ss[:, 0:nt], x2[:, 0:nt, :], axis=mybir.AxisListType.X).then_inc(sem["squared"], 1)
                    dve.wait_ge(sem["rooted"], j + 1)
                    ch.need(ch(dve.reciprocal(rs[:, 0:nt], rs[:, 0:nt])))
                    if j:
                        dve.wait_ge(sem["transposed"], tiles_before[j])
                    dve.tensor_tensor(hn[:, 0:nt, :], x1[:, 0:nt, :],
                                      rs[:, 0:nt].unsqueeze(2).broadcast_to([P, nt, HD]), ALU.mult).then_inc(sem["normed"], 1)

                def scale(j):
                    h, s = jobs[j]
                    t0, nt = SEQS[s][0], nts[s]
                    dve.wait_ge(og_loaded[h % 2], 16 * (h // 2 + 1))
                    if h >= 2:
                        dve.wait_ge(y_stored[h % 2], 16 * (h // 2))
                    for tt in range(nt):
                        i = tiles_before[j] + tt
                        dve.wait_ge(sem["transposed"], i + 1)
                        cols = slice(t0 + tt * P, t0 + (tt + 1) * P)
                        dve.scalar_tensor_tensor(y[h % 2][:, cols], tbank[i % 2][:, 0:P], gm[:, h:h + 1], og[h % 2][:, cols],
                                                 ALU.mult, ALU.mult).then_inc(sem["scaled"], 1)

                for j in range(len(jobs) + 2):
                    if j < len(jobs):
                        weigh(j)
                    if j >= 2:
                        scale(j - 2)
                    if 1 <= j <= len(jobs):
                        normalise(j - 1)


WEIGHTS = ["w_in_t", "w_out_t", "w_up_t", "w_down_t"]


def encoder(nc, a, out_prompt, out_sample):
    def scratch(name, shape):
        return nc.dram_tensor(name, shape, F32).ap()
    h2_d = scratch("h2_scratch", (HID, T))
    k_d = [scratch(f"k_scratch{s}", (ORDER, 2, P, 2, CLASSES, n // 512, HC)) for s, (_, n) in enumerate(SEQS)]
    power_d = scratch("power_scratch", (len(SEQS), ORDER, P, HY))
    qk_d = scratch("qk_scratch", (N_QK, P, T))
    tok_d = scratch("tok_scratch", (TT, P, 4 * HY))
    o_d = scratch("o_scratch", (N_O, P, T))
    gates_d = scratch("gates_scratch", (1, P, T))
    cols_d = scratch("cols_scratch", (2, P, TT, GATE_P))
    neg_max_d = scratch("neg_max_scratch", (GATE_P, T))
    y_d = scratch("y_scratch", (KD, P, T))
    g_d = scratch("g_scratch", (KF, P, T))

    with ExitStack() as whole:
        Phase.lasting = whole
        w = Phase(nc, whole, "all")
        ident = w.sb("ident", [P, P])
        ident_loaded = w.sem("ident_loaded")
        with nc.Block() as block:
            @block.sync
            def _(sp):
                sp.dma_start(ident[:, :], a["identity"]).then_inc(ident_loaded, 16)
                sp.wait_ge(ident_loaded, 16)

        fwd, inv = ([a[f"{x}{s}"] for s in range(len(SEQS))] for x in ("fwd", "inv"))
        input_projection(nc, a["x"], a["norm1_g"], a["w_in_t"], a["conv_par"], a["gate_bias"], ident, qk_d, tok_d, o_d, gates_d)
        gates_and_hidden(nc, gates_d, neg_max_d, cols_d, ident, a, h2_d)
        hyena_filters(nc, fwd, a["neg_t"], a["rates"], a, h2_d, k_d, power_d)
        long_convolutions(nc, fwd, inv, k_d, power_d, a["hy_bias"], tok_d, ident, y_d)
        mlstm_heads(nc, qk_d, tok_d, o_d, neg_max_d, cols_d, a["masks"], a["ml_gain"], ident, y_d)
        x_sb = w.sb("x", [P, TT, D])
        token_major_projection(nc, "out", KD, a["w_out_t"], y_d, x_sb, x_dram=a["x"])
        gated_up_projection(nc, x_sb, a["norm2_g"], a["w_up_t"], a["ffn_par"], ident, g_d)
        token_major_projection(nc, "down", KF, a["w_down_t"], g_d, x_sb, final=(a["final_g"], (out_prompt, out_sample)))


def laid_out(inputs):
    get = {n: np.asarray(v) for n, v in inputs.items()}
    a = {}
    a["x"] = np.concatenate([get["x_prompt"].reshape(-1, D), get["x_sample"].reshape(-1, D)]).reshape(TT, P, D)
    w_in = get["w_in"][0]
    hy, ml = 3 * HY, HEADS * HD
    gate_cols = np.zeros((D, P), np.float32)
    for g, row in enumerate(GATE_ROWS):
        gate_cols[:, row:row + HEADS] = w_in[:, hy + 4 * ml + g * HEADS:hy + 4 * ml + (g + 1) * HEADS]
    w = np.concatenate([w_in[:, hy:hy + 2 * ml], w_in[:, :hy], w_in[:, hy + 2 * ml:hy + 4 * ml], gate_cols], axis=1)

    def column_tiles(m):
        return m.reshape(KD, P, -1, P).transpose(2, 1, 0, 3)

    a["w_in_t"] = column_tiles(w)
    par = np.concatenate([get["conv_w"][0], get["conv_b"]], axis=0)
    par = np.concatenate([par[:, hy:], par[:, :hy]], axis=1)
    a["conv_par"] = par.reshape(4, N_CONV, P).transpose(2, 1, 0)
    bias = np.zeros((P, 1), np.float32)
    for g, row in enumerate(GATE_ROWS):
        bias[row:row + HEADS, 0] = get["gate_b"][0, g * HEADS:(g + 1) * HEADS]
    a["gate_bias"] = bias

    def halves(m):
        return m.reshape(-1, 2, P, 2, D // 2).transpose(3, 0, 2, 1, 4)

    def pairs(m):
        return m.reshape(m.shape[0], 2, KF, P).transpose(0, 2, 1, 3).reshape(m.shape[0], -1)

    a["w_out_t"] = halves(get["w_out"][0])
    a["w_up_t"] = column_tiles(pairs(get["w_up"][0]))
    a["w_down_t"] = halves(get["w_down"][0])
    a["ffn_par"] = pairs(np.concatenate([get["ffn_conv_w"][0], get["ffn_conv_b"]], axis=0)).reshape(4, 2 * KF, P).transpose(2, 1, 0)
    a["ml_gain"] = get["ml_norm_g"].reshape(HEADS, HD).T
    a["filt_w1"], a["filt_w2"], a["filt_w3"] = get["filt_w1"][0], get["filt_w2"][0], get["filt_w3"][0]
    a["filt_bf"] = np.stack([get["filt_b1"][0], get["filt_freq1"][0], get["filt_b2"][0], get["filt_freq2"][0]], axis=1)
    a["hy_bias"] = get["hy_bias"][0]
    a["norm1_g"], a["norm2_g"], a["final_g"] = get["norm1_g"][0], get["norm2_g"][0], get["final_g"]
    a["positions"], a["neg_t"], a["rates"] = filter_tables()
    for s, (_, n) in enumerate(SEQS):
        a[f"fwd{s}"], a[f"inv{s}"] = transform_tables(n)
    a["identity"] = np.eye(P, dtype=np.float32)
    a["keep"] = np.ones((P, 1), np.float32)
    a["keep"][0, 0] = 0.0
    key, query = np.arange(P)[:, None], np.arange(P)[None, :]
    a["masks"] = np.stack([np.where(key > query, -1e30, 0.0), np.where(key < query, -1e30, 0.0)], axis=1).astype(np.float32)
    return {n: np.ascontiguousarray(v) for n, v in a.items()}


def kernel(**inputs):
    import concourse.bacc as bacc
    from concourse.bass_utils import run_bass_kernel_spmd

    nc = bacc.Bacc("TRN2", target_bir_lowering=False, num_devices=1)
    arrays = {f"arg_{n}": v for n, v in laid_out(inputs).items()}
    a = {n[4:]: nc.dram_tensor(n, v.shape, mybir.dt.from_np(v.dtype), kind="ExternalInput").ap()
         for n, v in arrays.items()}
    outs = [nc.dram_tensor(f"out_{s}", (1, n, D), F32, kind="ExternalOutput").ap() for s, (_, n) in enumerate(SEQS)]
    encoder(nc, a, *outs)
    r = run_bass_kernel_spmd(nc, [arrays], core_ids=[0])
    return tuple(r.results[0][f"out_{s}"] for s in range(len(SEQS)))
```
